# Optimizing a Trainium2 kernel written in Bass

```python
import math
import jax
import jax.numpy as jnp
from jax import lax
import numpy as np

D_MODEL = 1024
BATCH = 1
SEQ = 512
DEPTH = 1
DEC_BATCH = 8
DEC_SEQ = 1
PAST_LEN = 256
PAGE_SIZE = 128

HEAD_DIM = 64
SB_HEADS = 8
NSA_HEADS = 8
NSA_KV_HEADS = 2
NSA_REP = NSA_HEADS // NSA_KV_HEADS
SB_WIDTH = SB_HEADS * HEAD_DIM
NSA_WIDTH = NSA_HEADS * HEAD_DIM
MIX_WIDTH = SB_WIDTH + NSA_WIDTH
KV_WIDTH = NSA_KV_HEADS * HEAD_DIM
N_BRANCH = 3
IN_COLS = 3 * SB_WIDTH + NSA_WIDTH + 6 * KV_WIDTH + N_BRANCH * NSA_HEADS
CMP_LEN = 32
CMP_STRIDE = 16
CMP_HIDDEN = 2 * HEAD_DIM
SEL_LEN = 64
SEL_TOPK = 16
FORCE_SCORE = 1.0e4
WINDOW = 512
ROPE_THETA = 10000.0
N_GROUPS = 4
EXPERTS_PER_GROUP = 4
N_EXPERTS = N_GROUPS * EXPERTS_PER_GROUP
TOP_K_EXPERTS = 2
D_FF_EXPERT = 512
Q_BLOCK = 128
NORM_EPS = 1e-6
NEG_BIG = -1.0e30

kernel_name = 'hymba_stickbreak_nsa_hiermoe_step'

def rms_norm(x, g):
    xf = x.astype(jnp.float32)
    y = xf * lax.rsqrt(jnp.mean(xf * xf, axis=-1, keepdims=True) + NORM_EPS)
    return (y * g.astype(jnp.float32)).astype(x.dtype)

def rotary(x, pos):
    half = HEAD_DIM // 2
    inv_freq = ROPE_THETA ** (-jnp.arange(half, dtype=jnp.float32) / half)
    ang = pos.astype(jnp.float32)[:, None] * inv_freq[None, :]
    bshape = (1, pos.shape[0]) + (1,) * (x.ndim - 3) + (half,)
    cos = jnp.cos(ang).reshape(bshape)
    sin = jnp.sin(ang).reshape(bshape)
    xf = x.astype(jnp.float32)
    x1, x2 = xf[..., :half], xf[..., half:]
    return jnp.concatenate([x1 * cos - x2 * sin, x2 * cos + x1 * sin], axis=-1).astype(x.dtype)

def project(h, w_in, pos):
    B, L = h.shape[:2]
    sizes = [SB_WIDTH] * 3 + [NSA_WIDTH] + [KV_WIDTH] * 6 + [N_BRANCH * NSA_HEADS]
    cuts = np.cumsum(sizes)[:-1].tolist()
    parts = jnp.split(jnp.einsum('bld,dc->blc', h, w_in), cuts, axis=-1)
    sb_q, sb_k, sb_v = [t.reshape(B, L, SB_HEADS, HEAD_DIM) for t in parts[:3]]
    q = rotary(parts[3].reshape(B, L, NSA_KV_HEADS, NSA_REP, HEAD_DIM), pos)
    ck, cv, sk, sv, wk, wv = [t.reshape(B, L, NSA_KV_HEADS, HEAD_DIM) for t in parts[4:10]]
    ck, sk, wk = rotary(ck, pos), rotary(sk, pos), rotary(wk, pos)
    gates = jax.nn.sigmoid(parts[10].astype(jnp.float32)).reshape(B, L, NSA_KV_HEADS, NSA_REP, N_BRANCH)
    return sb_q, sb_k, sb_v, q, ck, cv, sk, sv, wk, wv, gates

def sweep_query_blocks(fn, q, q_pos):
    B, T = q.shape[:2]
    nb = T // Q_BLOCK
    qb = jnp.moveaxis(q.reshape((B, nb, Q_BLOCK) + q.shape[2:]), 1, 0)
    pb = q_pos.reshape(nb, Q_BLOCK)
    out = lax.map(lambda args: fn(*args), (qb, pb))
    return jax.tree_util.tree_map(lambda o: jnp.moveaxis(o, 0, 1).reshape((B, T) + o.shape[3:]), out)

def stick_breaking_attend(q, k, v, q_pos, k_pos):
    z = jnp.einsum('bqhd,blhd->bhql', q, k).astype(jnp.float32) / math.sqrt(HEAD_DIM)
    mask = k_pos[None, :] < q_pos[:, None]
    log_keep = jnp.where(mask, jax.nn.log_sigmoid(-z), 0.0)
    log_rest = lax.cumsum(log_keep, axis=3, reverse=True) - log_keep
    a = jnp.where(mask, jnp.exp(jax.nn.log_sigmoid(z) + log_rest), 0.0)
    return jnp.einsum('bhql,blhd->bqhd', a.astype(v.dtype), v)

def compressed_block_ends(length):
    nc = (length - CMP_LEN) // CMP_STRIDE + 1
    return jnp.arange(nc, dtype=jnp.int32) * CMP_STRIDE + CMP_LEN - 1

def compress_blocks(k, pe, w1, w2):
    B, L = k.shape[:2]
    nc = (L - CMP_LEN) // CMP_STRIDE + 1
    ratio = CMP_LEN // CMP_STRIDE
    chunks = k[:, :(nc + ratio - 1) * CMP_STRIDE].reshape(B, nc + ratio - 1, CMP_STRIDE, NSA_KV_HEADS, HEAD_DIM)
    blocks = jnp.concatenate([chunks[:, r:r + nc] for r in range(ratio)], axis=2)
    blocks = blocks + pe[None, None, :, None, :].astype(k.dtype)
    flat = jnp.moveaxis(blocks, 3, 2).reshape(B, nc, NSA_KV_HEADS, CMP_LEN * HEAD_DIM)
    hid = jax.nn.gelu(jnp.einsum('bnge,eh->bngh', flat, w1))
    return jnp.einsum('bngh,hd->bngd', hid, w2)

def nsa_compressed_selected(q, q_pos, kc, vc, c_end, k_sel, v_sel):
    B, Q = q.shape[:2]
    L = k_sel.shape[1]
    scale = 1.0 / math.sqrt(HEAD_DIM)
    s = jnp.einsum('bqgrd,bngd->bgrqn', q, kc).astype(jnp.float32) * scale
    cmask = c_end[None, :] <= q_pos[:, None]
    s = jnp.where(cmask, s, NEG_BIG)
    m = jnp.max(s, axis=-1, keepdims=True)
    e = jnp.where(cmask, jnp.exp(s - m), 0.0)
    p = e / jnp.maximum(jnp.sum(e, axis=-1, keepdims=True), 1e-30)
    o_cmp = jnp.einsum('bgrqn,bngd->bqgrd', p.astype(vc.dtype), vc)
    n_sel = -(-L // SEL_LEN)
    j_start = jnp.arange(n_sel, dtype=jnp.int32) * SEL_LEN
    c_start = c_end - (CMP_LEN - 1)
    cover = (c_start[:, None] < j_start[None, :] + SEL_LEN) & (c_end[:, None] >= j_start[None, :])
    imp = jnp.einsum('bgrqn,nj->bgqj', p, cover.astype(jnp.float32))
    jj = jnp.arange(n_sel, dtype=jnp.int32)[None, :]
    q_blk = (q_pos // SEL_LEN)[:, None]
    forced = (jj == 0) | (jj == q_blk) | (jj == q_blk - 1)
    valid = j_start[None, :] <= q_pos[:, None]
    imp = jnp.where(forced, FORCE_SCORE, jnp.where(valid, imp, -1.0))
    _, idx = lax.top_k(imp, min(SEL_TOPK, n_sel))
    pos = (idx[..., None] * SEL_LEN + jnp.arange(SEL_LEN, dtype=jnp.int32)).reshape(B, NSA_KV_HEADS, Q, -1)
    pos_c = jnp.minimum(pos, L - 1)
    gather = jax.vmap(jax.vmap(lambda a, i: a[i]))
    kg = gather(jnp.moveaxis(k_sel, 2, 1), pos_c)
    vg = gather(jnp.moveaxis(v_sel, 2, 1), pos_c)
    s2 = jnp.einsum('bqgrd,bgqkd->bgrqk', q, kg).astype(jnp.float32) * scale
    smask = (pos <= q_pos[None, None, :, None])[:, :, None]
    p2 = jax.nn.softmax(jnp.where(smask, s2, NEG_BIG), axis=-1)
    o_sel = jnp.einsum('bgrqk,bgqkd->bqgrd', p2.astype(vg.dtype), vg)
    return o_cmp, o_sel

def window_attend(q, q_pos, k, v, k_pos):
    s = jnp.einsum('bqgrd,blgd->bgrql', q, k).astype(jnp.float32) / math.sqrt(HEAD_DIM)
    kp, qp = k_pos[None, :], q_pos[:, None]
    mask = (kp <= qp) & (kp >= qp - WINDOW) & (kp >= 0)
    p = jax.nn.softmax(jnp.where(mask, s, NEG_BIG), axis=-1)
    return jnp.einsum('bgrql,blgd->bqgrd', p.astype(v.dtype), v)

def merge_nsa_branches(o_cmp, o_sel, o_win, gates):
    B, L = o_cmp.shape[:2]
    o = gates[..., 0:1] * o_cmp + gates[..., 1:2] * o_sel + gates[..., 2:3] * o_win
    return o.astype(o_cmp.dtype).reshape(B, L, NSA_WIDTH)

def gather_pages(cache, page_table):
    g = cache[page_table]
    return g.reshape((g.shape[0], -1) + cache.shape[2:])

def mixer_prompt(h, w_in, cmp_pe_k, cmp_pe_v, cmp_k_w1, cmp_k_w2, cmp_v_w1, cmp_v_w2):
    B, T = h.shape[:2]
    pos = jnp.arange(T, dtype=jnp.int32)
    sb_q, sb_k, sb_v, q, ck, cv, sk, sv, wk, wv, gates = project(h, w_in, pos)
    o_sb = sweep_query_blocks(lambda qb, pb: stick_breaking_attend(qb, sb_k, sb_v, pb, pos), sb_q, pos)
    kc = compress_blocks(ck, cmp_pe_k, cmp_k_w1, cmp_k_w2)
    vc = compress_blocks(cv, cmp_pe_v, cmp_v_w1, cmp_v_w2)
    c_end = compressed_block_ends(T)
    o_cmp, o_sel = sweep_query_blocks(
        lambda qb, pb: nsa_compressed_selected(qb, pb, kc, vc, c_end, sk, sv), q, pos)
    wk_pad = jnp.pad(wk, ((0, 0), (WINDOW, 0), (0, 0), (0, 0)))
    wv_pad = jnp.pad(wv, ((0, 0), (WINDOW, 0), (0, 0), (0, 0)))

    def win_block(qb, pb):
        start = pb[0]
        kb = lax.dynamic_slice_in_dim(wk_pad, start, WINDOW + Q_BLOCK, axis=1)
        vb = lax.dynamic_slice_in_dim(wv_pad, start, WINDOW + Q_BLOCK, axis=1)
        kpos = start - WINDOW + jnp.arange(WINDOW + Q_BLOCK, dtype=jnp.int32)
        return window_attend(qb, pb, kb, vb, kpos)

    o_win = sweep_query_blocks(win_block, q, pos)
    o_nsa = merge_nsa_branches(o_cmp, o_sel, o_win, gates)
    keep = min(WINDOW, T)
    new_state = (sb_k, sb_v, ck, cv, sk, sv, wk[:, T - keep:], wv[:, T - keep:])
    return o_sb.reshape(B, T, SB_WIDTH), o_nsa, new_state

def mixer_sample(h, cache_sb_k, cache_sb_v, cache_cmp_k, cache_cmp_v, cache_sel_k, cache_sel_v,
                 state_win_k, state_win_v, page_table, w_in, cmp_pe_k, cmp_pe_v,
                 cmp_k_w1, cmp_k_w2, cmp_v_w1, cmp_v_w2):
    Bd, S = h.shape[:2]
    past = page_table.shape[1] * cache_sb_k.shape[1]
    q_pos = past + jnp.arange(S, dtype=jnp.int32)
    all_pos = jnp.arange(past + S, dtype=jnp.int32)
    sb_q, sb_k, sb_v, q, ck, cv, sk, sv, wk, wv, gates = project(h, w_in, q_pos)

    def with_past(cache, new):
        return jnp.concatenate([gather_pages(cache, page_table).astype(new.dtype), new], axis=1)

    o_sb = stick_breaking_attend(sb_q, with_past(cache_sb_k, sb_k), with_past(cache_sb_v, sb_v), q_pos, all_pos)
    kc = compress_blocks(with_past(cache_cmp_k, ck), cmp_pe_k, cmp_k_w1, cmp_k_w2)
    vc = compress_blocks(with_past(cache_cmp_v, cv), cmp_pe_v, cmp_v_w1, cmp_v_w2)
    c_end = compressed_block_ends(past + S)
    o_cmp, o_sel = nsa_compressed_selected(q, q_pos, kc, vc, c_end,
                                           with_past(cache_sel_k, sk), with_past(cache_sel_v, sv))
    keep = state_win_k.shape[1]
    wk_all = jnp.concatenate([state_win_k.astype(wk.dtype), wk], axis=1)
    wv_all = jnp.concatenate([state_win_v.astype(wv.dtype), wv], axis=1)
    wpos = past - keep + jnp.arange(keep + S, dtype=jnp.int32)
    o_win = window_attend(q, q_pos, wk_all, wv_all, wpos)
    o_nsa = merge_nsa_branches(o_cmp, o_sel, o_win, gates)
    new_state = (sb_k, sb_v, ck, cv, sk, sv, wk_all[:, S:], wv_all[:, S:])
    return o_sb.reshape(Bd, S, SB_WIDTH), o_nsa, new_state

def hierarchical_moe(h, router_group_w, router_group_b, router_expert_w, router_expert_b, w_gate, w_up, w_down):
    g_logits = jnp.einsum('nd,dg->ng', h, router_group_w).astype(jnp.float32) + router_group_b.astype(jnp.float32)
    g_prob = jax.nn.softmax(g_logits, axis=-1)
    g_idx = jnp.argmax(g_logits, axis=-1)
    g_w = jnp.take_along_axis(g_prob, g_idx[:, None], axis=-1)
    e_logits = jnp.einsum('nd,dge->nge', h, router_expert_w).astype(jnp.float32) + router_expert_b.astype(jnp.float32)
    e_logits = jnp.take_along_axis(e_logits, g_idx[:, None, None], axis=1)[:, 0]
    top_w, top_i = lax.top_k(jax.nn.softmax(e_logits, axis=-1), TOP_K_EXPERTS)
    top_w = top_w / jnp.sum(top_w, axis=-1, keepdims=True)
    expert_id = g_idx[:, None] * EXPERTS_PER_GROUP + top_i
    combine = jnp.sum(jax.nn.one_hot(expert_id, N_EXPERTS, dtype=jnp.float32) * (g_w * top_w)[..., None], axis=1)
    gate = jnp.einsum('nd,edf->nef', h, w_gate)
    up = jnp.einsum('nd,edf->nef', h, w_up)
    act = jax.nn.silu(gate) * up * combine[..., None].astype(h.dtype)
    return jnp.einsum('nef,efd->nd', act, w_down)

def finish_layer(x, o_sb, o_nsa, norm_sb_out, norm_nsa_out, w_out, norm_ffn, router_group_w, router_group_b,
                 router_expert_w, router_expert_b, w_gate, w_up, w_down):
    mix = jnp.concatenate([rms_norm(o_sb, norm_sb_out), rms_norm(o_nsa, norm_nsa_out)], axis=-1)
    x = x + jnp.einsum('blc,cd->bld', mix, w_out)
    B, L, D = x.shape
    h = rms_norm(x, norm_ffn).reshape(B * L, D)
    y = hierarchical_moe(h, router_group_w, router_group_b, router_expert_w, router_expert_b, w_gate, w_up, w_down)
    return x + y.reshape(B, L, D)

def setup_inputs(seed: int = 0) -> dict:
    key = jax.random.key(seed)
    ks = jax.random.split(key, 32)
    f32 = jnp.float32
    n_pages = PAST_LEN // PAGE_SIZE
    n_used = DEC_BATCH * n_pages
    n_pool = (n_used * 5) // 4
    win_keep = min(WINDOW, PAST_LEN)

    def normal(k, shape, scale=1.0):
        return scale * jax.random.normal(k, shape, f32)

    def gain(k, shape):
        return 1.0 + 0.02 * jax.random.normal(k, shape, f32)

    page_table = jax.random.permutation(ks[10], n_pool)[:n_used].reshape(DEC_BATCH, n_pages).astype(jnp.int32)
    return {
        'x_prompt': normal(ks[0], (BATCH, SEQ, D_MODEL)),
        'x_sample': normal(ks[1], (DEC_BATCH, DEC_SEQ, D_MODEL)),
        'cache_sb_k': normal(ks[2], (DEPTH, n_pool, PAGE_SIZE, SB_HEADS, HEAD_DIM)),
        'cache_sb_v': normal(ks[3], (DEPTH, n_pool, PAGE_SIZE, SB_HEADS, HEAD_DIM)),
        'cache_cmp_k': normal(ks[4], (DEPTH, n_pool, PAGE_SIZE, NSA_KV_HEADS, HEAD_DIM)),
        'cache_cmp_v': normal(ks[5], (DEPTH, n_pool, PAGE_SIZE, NSA_KV_HEADS, HEAD_DIM)),
        'cache_sel_k': normal(ks[6], (DEPTH, n_pool, PAGE_SIZE, NSA_KV_HEADS, HEAD_DIM)),
        'cache_sel_v': normal(ks[7], (DEPTH, n_pool, PAGE_SIZE, NSA_KV_HEADS, HEAD_DIM)),
        'state_win_k': normal(ks[8], (DEPTH, DEC_BATCH, win_keep, NSA_KV_HEADS, HEAD_DIM)),
        'state_win_v': normal(ks[9], (DEPTH, DEC_BATCH, win_keep, NSA_KV_HEADS, HEAD_DIM)),
        'page_table': page_table,
        'w_in': normal(ks[11], (DEPTH, D_MODEL, IN_COLS), D_MODEL ** -0.5),
        'cmp_pe_k': normal(ks[12], (DEPTH, CMP_LEN, HEAD_DIM), 0.1),
        'cmp_pe_v': normal(ks[13], (DEPTH, CMP_LEN, HEAD_DIM), 0.1),
        'cmp_k_w1': normal(ks[14], (DEPTH, CMP_LEN * HEAD_DIM, CMP_HIDDEN), (CMP_LEN * HEAD_DIM) ** -0.5),
        'cmp_k_w2': normal(ks[15], (DEPTH, CMP_HIDDEN, HEAD_DIM), CMP_HIDDEN ** -0.5),
        'cmp_v_w1': normal(ks[16], (DEPTH, CMP_LEN * HEAD_DIM, CMP_HIDDEN), (CMP_LEN * HEAD_DIM) ** -0.5),
        'cmp_v_w2': normal(ks[17], (DEPTH, CMP_HIDDEN, HEAD_DIM), CMP_HIDDEN ** -0.5),
        'norm_sb_out': gain(ks[18], (DEPTH, SB_WIDTH)),
        'norm_nsa_out': gain(ks[19], (DEPTH, NSA_WIDTH)),
        'w_out': normal(ks[20], (DEPTH, MIX_WIDTH, D_MODEL), MIX_WIDTH ** -0.5),
        'norm_attn': gain(ks[21], (DEPTH, D_MODEL)),
        'norm_ffn': gain(ks[22], (DEPTH, D_MODEL)),
        'router_group_w': normal(ks[23], (DEPTH, D_MODEL, N_GROUPS), D_MODEL ** -0.5),
        'router_group_b': normal(ks[24], (DEPTH, N_GROUPS), 0.01),
        'router_expert_w': normal(ks[25], (DEPTH, D_MODEL, N_GROUPS, EXPERTS_PER_GROUP), D_MODEL ** -0.5),
        'router_expert_b': normal(ks[26], (DEPTH, N_GROUPS, EXPERTS_PER_GROUP), 0.01),
        'w_gate': normal(ks[27], (DEPTH, N_EXPERTS, D_MODEL, D_FF_EXPERT), D_MODEL ** -0.5),
        'w_up': normal(ks[28], (DEPTH, N_EXPERTS, D_MODEL, D_FF_EXPERT), D_MODEL ** -0.5),
        'w_down': normal(ks[29], (DEPTH, N_EXPERTS, D_FF_EXPERT, D_MODEL), D_FF_EXPERT ** -0.5),
        'norm_final': gain(ks[30], (D_MODEL,)),
    }

def reference(x_prompt, x_sample, cache_sb_k, cache_sb_v, cache_cmp_k, cache_cmp_v, cache_sel_k, cache_sel_v,
              state_win_k, state_win_v, page_table, w_in, cmp_pe_k, cmp_pe_v, cmp_k_w1, cmp_k_w2,
              cmp_v_w1, cmp_v_w2, norm_sb_out, norm_nsa_out, w_out, norm_attn, norm_ffn,
              router_group_w, router_group_b, router_expert_w, router_expert_b, w_gate, w_up, w_down,
              norm_final):
    xp, xs = x_prompt, x_sample
    layer_states = []
    for l in range(DEPTH):
        hp = rms_norm(xp, norm_attn[l])
        o_sb_p, o_nsa_p, st_p = mixer_prompt(hp, w_in[l], cmp_pe_k[l], cmp_pe_v[l],
                                             cmp_k_w1[l], cmp_k_w2[l], cmp_v_w1[l], cmp_v_w2[l])
        xp = finish_layer(xp, o_sb_p, o_nsa_p, norm_sb_out[l], norm_nsa_out[l], w_out[l], norm_ffn[l],
                          router_group_w[l], router_group_b[l], router_expert_w[l], router_expert_b[l],
                          w_gate[l], w_up[l], w_down[l])
        hs = rms_norm(xs, norm_attn[l])
        o_sb_s, o_nsa_s, st_s = mixer_sample(hs, cache_sb_k[l], cache_sb_v[l], cache_cmp_k[l], cache_cmp_v[l],
                                             cache_sel_k[l], cache_sel_v[l], state_win_k[l], state_win_v[l],
                                             page_table, w_in[l], cmp_pe_k[l], cmp_pe_v[l],
                                             cmp_k_w1[l], cmp_k_w2[l], cmp_v_w1[l], cmp_v_w2[l])
        xs = finish_layer(xs, o_sb_s, o_nsa_s, norm_sb_out[l], norm_nsa_out[l], w_out[l], norm_ffn[l],
                          router_group_w[l], router_group_b[l], router_expert_w[l], router_expert_b[l],
                          w_gate[l], w_up[l], w_down[l])
        layer_states.append(st_p + st_s)
    (sb_k_p, sb_v_p, cmp_k_p, cmp_v_p, sel_k_p, sel_v_p, win_k_p, win_v_p,
     sb_k_s, sb_v_s, cmp_k_s, cmp_v_s, sel_k_s, sel_v_s, win_k_s, win_v_s) = [jnp.stack(t) for t in zip(*layer_states)]
    y_prompt = rms_norm(xp, norm_final)
    y_sample = rms_norm(xs, norm_final)
    return (y_prompt, y_sample, sb_k_p, sb_v_p, cmp_k_p, cmp_v_p, sel_k_p, sel_v_p, win_k_p, win_v_p,
            sb_k_s, sb_v_s, cmp_k_s, cmp_v_s, sel_k_s, sel_v_s, win_k_s, win_v_s)


_drawn_inputs = setup_inputs


def setup_inputs(seed=0):
    import zlib

    import numpy as np

    out = dict(_drawn_inputs(seed))
    spreads = {}
    factors = {'cmp_pe_k': 5.014,
     'norm_sb_out': 4.444,
     'norm_nsa_out': 3.982,
     'norm_ffn': 2.728,
     'router_group_b': 8.0,
     'router_expert_b': 41.736,
     'norm_final': 7.786}
    for name, (base, spread) in spreads.items():
        noise = np.random.default_rng([zlib.crc32(name.encode()), seed]).standard_normal(out[name].shape)
        drawn = base * np.exp(spread * noise) if base else spread * noise
        out[name] = jnp.asarray(drawn.astype(out[name].dtype))
    for name, factor in factors.items():
        out[name] = (out[name] * factor).astype(out[name].dtype)
    return out
```

```python
import numpy as np
from contextlib import ExitStack

import concourse.bass as bass
import concourse.mybir as mybir

ALU = mybir.AluOpType
ACT = mybir.ActivationFunctionType
AX = mybir.AxisListType
F32 = mybir.dt.float32
BF16 = mybir.dt.bfloat16
I32 = mybir.dt.int32
U32 = mybir.dt.uint32

P = 128
D = 1024
SEQ = 512
NB = 8
PAST = 256
PAGE = 128
NPG = PAST // PAGE
HD = 64
HEADS = 8
GROUPS = 2
REP = HEADS // GROUPS
KD = D // P
QT = SEQ // P
TILES = QT + 1
ROWS = [P] * QT + [NB]
TOK = SEQ + NB
COLS = 2840
CHUNK = 512
NCH = 6
SBQ, SBK, SBV, NQ, KV4, KV2 = range(NCH)
CMP_PAIRS = 16
CT = QT // 2 + NB
NCHUNK = CT * 16
NEG = -1.0e30
EPS = 1e-6
NE = 16
FF = 512
CAP = 5 * P
EXTRA = 8


def host_constants():
    pos = np.concatenate([np.arange(SEQ), np.full(NB, PAST), np.zeros(P - NB)]).astype(np.float32)
    half = HD // 2
    inv = (np.float32(10000.0) ** (-np.arange(half, dtype=np.float32) / np.float32(half))).astype(np.float32)
    ang = pos[:, None] * inv[None, :]
    cos, sin = np.cos(ang), np.sin(ang)
    rope = np.concatenate([cos, cos, -sin, sin], 1).reshape(TILES, P, 2 * HD).transpose(1, 0, 2)
    p = np.arange(P)
    qpos = np.arange(SEQ).reshape(QT, P).T
    ends = 16 * np.arange(32) + 31
    ends[31] = 10 ** 6
    seen = ends[None, None, :] <= qpos[:, :, None]
    own = (p[:, None] // 8 == p[None, :] // 16) & (p[None, :] % 16 < 15)
    parts = {
        "ident": np.eye(P),
        "rope": rope.reshape(P, -1),
        "cneg": np.where(seen, 0.0, NEG).reshape(P, -1),
        "cone": seen.reshape(P, -1),
        "iota16": np.tile(np.arange(16), (P, 1)),
        "base16": np.tile(np.arange(16) * CAP, (P, 1)),
        "maskb": p[:, None] // 8 == np.arange(8)[None],
        "maskh": p[:, None] % 8 == np.arange(8)[None],
        "sneg": np.where(own, 0.0, NEG),
        "spread": p[:, None] == np.arange(64)[None] // 8,
        "eps": np.full((P, 1), EPS),
        "one": np.ones((P, 1)),
    }
    q, k = p[:, None], p[None, :]
    bparts = {
        "identb": np.eye(P),
        "before": np.where(k >= q, NEG, 0.0),
        "upto": np.where(k > q, NEG, 0.0),
        "earlier": q < k,
        "onesb": np.ones((P, P)),
    }
    return parts, bparts


def columns(parts):
    at, n = {}, 0
    for name, a in parts.items():
        at[name] = (n, n + a.shape[1])
        n += a.shape[1]
    return at, n



class Signals:

    def __init__(self, nc, ctx):
        self.nc, self.ctx, self.sem, self.total, self.marks = nc, ctx, {}, {}, {}

    def mark(self, name, key, by=1):
        if name not in self.sem:
            self.sem[name] = self.ctx.enter_context(self.nc.semaphore(name))
            self.total[name] = 0
        self.total[name] += by
        self.marks[name, key] = self.total[name]

    def wait(self, eng, name, key):
        eng.wait_ge(self.sem[name], self.marks[name, key])

    def __getitem__(self, name):
        return self.sem[name]


def build(nc, a, out):
    cf_at, cf_n = columns(host_constants()[0])
    cb_at, cb_n = columns(host_constants()[1])
    with ExitStack() as ctx:
        body(nc, ctx, a, out, cf_at, cf_n, cb_at, cb_n)


def body(nc, ctx, a, out, cf_at, cf_n, cb_at, cb_n):
    def sb(name, shape, dt=F32):
        return ctx.enter_context(nc.sbuf_tensor(name, shape, dt))

    bank = [ctx.enter_context(nc.psum_tensor(f"bank{n}", [P, 512], F32)) for n in range(8)]
    cf = sb("cf", [P, cf_n])
    cb = sb("cb", [P, cb_n], BF16)
    c = {k: cf[:, v[0]:v[1]] for k, v in cf_at.items()}
    c.update({k: cb[:, v[0]:v[1]] for k, v in cb_at.items()})
    ident = c["ident"]
    rope = c["rope"].rearrange("p (i n) -> p i n", i=TILES)
    gain = sb("gain", [P, D])
    gain_out = sb("gain_out", [P, D])
    x = sb("x", [P, TILES, D])
    qsbT = sb("qsbT", [P, 4, TOK])
    ksbT = sb("ksbT", [P, 4, TOK])
    qnsaT = sb("qnsaT", [P, REP, TOK])
    kselT = sb("kselT", [P, TOK])
    kwinT = sb("kwinT", [P, TOK])
    vsb = sb("vsb", [P, TILES, 512])
    vsel = sb("vsel", [P, TILES, P])
    vwin = sb("vwin", [P, TILES, P])
    gates = sb("gates", [P, TILES, 24])
    kcT = sb("kcT", [P, NCHUNK])
    vc = sb("vc", [P, 2, P])
    reg0 = sb("reg0", [P, 12288])
    reg1 = sb("reg1", [P, 12288])
    work = sb("work", [P, 7168])
    small = sb("small", [P, 32])
    smi = sb("smi", [P, 48], U32)
    pages = sb("pages", [1, NB * NPG], I32)
    wr = sb("wr", [P, KD, 20])
    br = sb("br", [P, 20])

    def view(region, at, shape):
        n = int(np.prod(shape))
        v = region[:, at:at + n]
        if len(shape) == 2:
            return v.rearrange("p (a b) -> p a b", a=shape[0])
        if len(shape) == 3:
            return v.rearrange("p (a b c) -> p a b c", a=shape[0], b=shape[1])
        return v

    win = view(reg0, 0, [3, KD, CHUNK])
    hT = view(reg1, 0, [KD, TOK])
    hn = view(reg1, 4160, [2, D])
    raw = view(reg1, 6208, [4, CHUNK])
    rot = view(reg1, 8256, [2, CHUNK])
    swp = view(reg1, 9280, [2, CHUNK])

    sg = Signals(nc, ctx)
    banks = {"m": [bank[0], bank[1], bank[2]], "t": [bank[3], bank[4]], "o": [bank[5], bank[6]], "x": [bank[7]]}
    uses = {r: [] for r in banks}
    index = {}

    def use(ring, key, free, signals=True):
        index[ring, key] = len(uses[ring])
        uses[ring].append((key, free))
        if signals:
            sg.mark(ring + "_full", key)
        sg.mark(ring + "_" + free, key)

    def at(ring, key):
        return banks[ring][index[ring, key] % len(banks[ring])]

    def acquire(eng, ring, key):
        n = index[ring, key] - len(banks[ring])
        if n >= 0:
            k, free = uses[ring][n]
            sg.wait(eng, ring + "_" + free, k)

    def freed_by(ring, key):
        return uses[ring][index[ring, key]][1]

    PLAN = []

    def step(kind, *key):
        PLAN.append((kind, key))

    turn = [0]

    def tstep(*key):
        turn[0] += 1
        use("t", key, "act" if turn[0] % 2 else "dve")
        step("T", *key)

    for cc in range(3):
        step("load_w", cc)
        sg.mark(f"w{cc % 3}", cc, 16)
    for i in range(TILES):
        step("norm", i)
        sg.mark(f"x{i}", i, 16)
        sg.mark("ssq", ("attn", i))
        sg.mark("rstd", ("attn", i))
        sg.mark("h", i)
        tstep("hT", i, 0)
        tstep("hT", i, 1)
    proj = [(cc, i) for cc in range(NCH) for i in range(TILES)]
    raws = [n for n, (cc, _) in enumerate(proj) if cc != SBV]
    rq = {n: q for q, n in enumerate(raws)}
    blocks = {SBQ: 4, SBK: 4, SBV: 0, NQ: 4, KV4: 1, KV2: 1}

    def finish(n):
        cc, i = proj[n]
        step("store", cc, i)
        if cc == SBK:
            sg.mark(f"st_raw{rq[n] % 4}", n, 16)
        if cc == SBV:
            sg.mark("st_v", n, 16)
        if cc == KV4:
            sg.mark(f"st_raw{rq[n] % 4}", n, 32)
            sg.mark(f"st_rot{n % 2}", n, 32)
        if cc == KV2:
            sg.mark(f"st_raw{rq[n] % 4}", n, 16)
            sg.mark(f"st_rot{n % 2}", n, 16)
        if blocks[cc]:
            tstep("pT", n)

    for n, (cc, i) in enumerate(proj):
        use("m", ("proj", n), "act")
        step("proj", n)
        if i == TILES - 1 and cc + 3 < NCH:
            step("load_w", cc + 3)
            sg.mark(f"w{cc % 3}", cc + 3, 16)
        if cc >= NQ:
            step("rope", n)
            sg.mark("swapped", n)
            sg.mark("rotated", n)
        if n >= 2:
            finish(n - 2)
    finish(len(proj) - 2)
    finish(len(proj) - 1)

    w1 = [view(reg0, 0, [16, P]), view(reg0, 2048, [16, P])]
    xt = [work[:, 0:2576], work[:, 2576:5152]]
    pair = view(work, 5152, [4, 2 * P])
    pe_in = view(work, 6176, [2, P])
    w2 = view(work, 6432, [2, HD])
    hid_a = [reg0[:, 4096 + 1000 * v:4096 + 1000 * v + 322] for v in range(2)]
    hid = [reg0[:, 4432 + 1000 * v:4432 + 1000 * v + 320] for v in range(2)]
    hid_u = [reg0[:, 4760 + 1000 * v:4760 + 1000 * v + 320] for v in range(2)]
    page = view(reg0, 6144, [6, 4, P])
    pageT = view(reg0, 9216, [3, 4, P])
    zt = reg0[:, 10752:10752 + 256]
    sz = view(reg0, 11008, [2, 264])
    pt4 = reg0[:, 11536:11536 + 448]
    ot = view(reg0, 11984, [4, NB])
    smp = reg0[:, 12016:12288]
    qbd = smp[:, 0:64].rearrange("p (j b t) -> p j b t", j=4, b=NB)
    qbn = smp[:, 64:128].rearrange("p (b h) -> p b h", b=NB)
    snew = smp[:, 128:144].rearrange("p (t b) -> p t b", t=2)
    gsp = smp[:, 144:168].rearrange("p (t h) -> p t h", t=3)
    gw = smp[:, 168:171]
    pm = smp[:, 176:192].rearrange("p (t b) -> p t b", t=2)
    soft = view(work, 0, [2, 512])
    plus = view(work, 1024, [2, 512])
    prob = view(work, 2048, [3, 512])
    probT = view(work, 3584, [3, 512])
    o_sb = work[:, 5120:5632]
    o_nsa = work[:, 5632:6144]
    o_part = work[:, 6144:6656]
    cprob = work[:, 6656:6912]
    cprobT = work[:, 6912:7168]
    w_out = view(reg1, 0, [KD, D])
    mix = reg1[:, 8192:9216]
    mixT = view(reg1, 9216, [KD, P])
    h2 = reg1[:, 10240:11264]
    rt = sb("rt", [P, 256])
    weight = sb("weight", [P, TILES, 2])
    onehot = sb("onehot", [P, TILES, NE], BF16)
    slots = sb("slots", [P, TILES, 2], U32)
    token = sb("token", [P, TILES])
    chosen = sb("chosen", [P, TILES, 2, NE])
    expert = sb("expert", [P, TILES, 2])
    slot_f = sb("slot_f", [P, TILES, 2])
    y_slots = sb("y_slots", [P, TILES, 2], U32)
    st = sb("st", [P, 96])
    h2_dram = nc.dram_tensor("h2_rows", [TOK, D], F32, kind="Internal").ap()
    y_dram = nc.dram_tensor("expert_rows", [(NE + EXTRA) * P, D], F32, kind="Internal").ap()
    table = nc.dram_tensor("slot_tokens", [NE * CAP, 1], F32, kind="Internal").ap()

    order = [(kv, t) for kv in range(2) for t in list(range(2, CT)) + [0, 1]]

    def load_pair(q):
        if q < len(order):
            step("pair", q)
            sg.mark(f"pair{q % 4}", q, 32 if order[q][1] < 2 else 64)

    sg.mark("pages", 0, 16)
    PLAN.insert(3, ("pages_in", ()))
    sg.mark("w1_in", 0, 32)
    at_proj = PLAN.index(("proj", (NQ * TILES + TILES - 1,)))
    PLAN.insert(at_proj + 1, ("load_w1", ()))
    sg.mark("cmp_small", 0, 64)
    for q in range(4):
        load_pair(q)
    for v in range(2):
        tstep("peT", v)
    for q, (kv, t) in enumerate(order):
        tstep("XT", q)
        load_pair(q + 4)
        if t == 1:
            use("m", ("hidA", kv), "act")
            use("m", ("hidB", kv), "dve")
            sg.mark("hid_a", kv)
            sg.mark("gelu_in", kv)
            sg.mark("gelu_exp", kv)
            sg.mark("hid", kv)
            step("hid", kv)
    for kv in range(2):
        use("m", ("comp", kv), "act")
        step("comp", kv)

    loads = ([("sbk", j) for j in range(16)] + [("selk", g) for g in range(4)] + [("wink", g) for g in range(4)]
             + [("sbv", j) for j in range(16)] + [("selv", g) for g in range(4)] + [("winv", g) for g in range(4)])
    lq = {k: q for q, k in enumerate(loads)}

    def load_page(q):
        if q < len(loads):
            step("page", q)
            n = 64 if loads[q][0] in ("selk", "selv") else 16
            sg.mark(f"page{q % 6}", q, n)

    for q in range(6):
        load_page(q)
    step("qbd")
    sg.mark("qbd", 0)
    sg.mark("gates_exp", 0)
    sg.mark("gates", 0)
    use("x", ("zsb",), "act", False)

    def score_pages(kind, n):
        steps = [(kind, g) for g in range(n)]
        for s, k in enumerate(steps):
            tstep("KT", *k)
            load_page(lq[k] + 6)
            sg.mark("scored", k)
            if s:
                step("zs", *steps[s - 1])
        step("zs", *steps[-1])

    score_pages("sbk", 16)
    step("zt_sb")
    tstep("zT")
    use("x", ("zn",), "act", False)
    score_pages("selk", 4)
    step("front", "s")
    sg.mark("soft", "s")
    step("mid", "s")
    sg.mark("arg", "s")
    score_pages("wink", 4)
    step("back", "s")
    sg.mark("p_ready", "s")
    step("zt_nsa")
    tstep("znT")
    for key in (("snew",), ("gsp",), ("cs",)):
        use("m", key, "dve")
    step("sample_small")
    sg.mark("s_max", 0)
    sg.mark("s_exp", 0)
    sg.mark("s_prob", 0)
    tstep("aT")
    use("o", ("sbs",), "dve", False)
    for b in range(NB):
        step("pvs", b)
        sg.mark("pvs", b)
        for pg in range(NPG):
            load_page(lq["sbv", 2 * b + pg] + 6)
    step("ots")
    tstep("osb4")
    tstep("pT4")
    use("o", ("nss",), "dve", False)
    for kind in ("selv", "winv"):
        for g in range(4):
            step("pvn", kind, g)
            sg.mark("pvn", (kind, g))
            load_page(lq[kind, g] + 6)
    step("otn")
    tstep("ons4")
    sg.mark("w_out", 0, 16)
    step("load_wout")
    step("win_state")
    sg.mark("st_state", 0, 32)
    sg.mark("gain_in", "out", 32)
    sg.mark("gain_in", "ffn", 16)

    tile_order = [QT] + list(range(QT))

    def output_steps(i):
        def a1():
            step("mix_ssq", i)
            sg.mark("ssq", ("mix", i))
            sg.mark("rstd", ("mix", i))
            step("mix", i)
            sg.mark("mix", i)

        def a2():
            for half in range(2):
                tstep("mixT", i, half)

        def a3():
            for half in range(2):
                use("m", ("wout", i, half), "dve")
            step("wout", i)

        def a4():
            step("ffn_ssq", i)
            sg.mark("ssq", ("ffn", i))
            sg.mark("rstd", ("ffn", i))
            step("h2", i)
            sg.mark("h2", i)
            sg.mark("st_h2", i, 16)

        def a5():
            for half in range(2):
                tstep("h2T", i, half)

        def a6():
            use("x", ("logit", i), "dve")
            step("route", i)
            sg.mark("r_max", (i, 0))
            sg.mark("r_exp", (i, 0))
            sg.mark("r_max", (i, 1))
            sg.mark("r_exp", (i, 1))
            sg.mark("onehot", i)

        def a7():
            use("x", ("rank", i), "dve")
            step("rank", i)
            sg.mark("slots", i)
            sg.mark("scatter", i, 32)
        return [a1, a2, a3, a4, a5, a6, a7]

    SB, SEL, WIN = range(3)
    pending = output_steps(QT)
    steps = [(i, b, h) for i in range(QT) for b in range(3) for h in range(HEADS)]
    for t in range(len(steps) + 4):
        if t < len(steps):
            i, b, h = s = steps[t]
            if b == SB and h == 3:
                use("x", ("cmp", i), "dve")
                step("cmp_score", i)
                sg.mark("c_max", i)
                sg.mark("c_exp", i)
                sg.mark("c_prob", i)
            if b == SB and h == 6:
                tstep("cT", i)
                use("o", (i, "cmp"), "dve", False)
                step("cmp_pv", i)
                sg.mark("o_done", (i, "cmp"))
            use("m", s, "dve" if b == SB else "act")
            step("score", *s)
            if b == SB:
                step("front", *s)
                sg.mark("soft", s)
            step("mid", *s)
            if b != SB:
                sg.mark("arg", s)
        if 1 <= t <= len(steps):
            step("back", *steps[t - 1])
            if steps[t - 1][1] == SB:
                sg.mark("p_ready", steps[t - 1])
        if 2 <= t <= len(steps) + 1:
            tstep("probT", *steps[t - 2])
        if 3 <= t <= len(steps) + 2:
            i, b, h = s = steps[t - 3]
            if h == 0:
                use("o", (i, b), "dve", False)
            step("pv", *s)
            sg.mark("pv", s)
            if h == HEADS - 1:
                step("branch", i, b)
                if b != SB:
                    sg.mark("branch", (i, b))
                if b == WIN:
                    while pending:
                        pending.pop(0)()
                    pending = output_steps(i)
        if t % 3 == 1 and pending and t > 2:
            pending.pop(0)()
    while pending:
        pending.pop(0)()
    order_of = {s: n for n, s in enumerate(steps)}
    sb_order = ["s"] + [s for s in steps if s[1] == SB]
    sb_index = {s: n for n, s in enumerate(sb_order)}
    for name, by in (("const", 16), ("const_b", 16), ("gain_attn", 16), ("table_zero", 16), ("y_zero", 16 * EXTRA), ("router_in", 64),
                     ("iota", 1), ("zero", 1), ("act_chain", 0), ("dve_chain", 0), ("pe_chain", 0)):
        sg.mark(name, 0, by)

    def sb_views(key):
        if key == ("s",):
            r, n, q = 64, 2 * P, 0
            z = sz[0:64, 0, 0:n]
            return r, n, z, soft[0:r, 0, 0:n], plus[0:r, 0, 0:n], prob[0:r, 0, 0:n]
        i, b, h = key
        n, q = (i + 1) * P, sb_index[key]
        return P, n, at("m", key)[:, 0:n], soft[:, q % 2, 0:n], plus[:, q % 2, 0:n], prob[:, order_of[key] % 3, 0:n]

    def wait_arg(eng, key):
        sg.wait(eng, "arg" if key == "s" else "m_dve", key)

    def key_of(key):
        return "s" if key == ("s",) else key

    def before_prob_write(eng, key):
        n = order_of.get(key, 0)
        if n >= 3:
            sg.wait(eng, "t_full", ("probT",) + steps[n - 3])

    def gate_rows(i):
        return gates[0:ROWS[i], i, :].rearrange("p (h t) -> p t h", t=3)

    def more_transposes(key, b):
        kind = key[0]
        if kind == "peT":
            v = key[1]
            return [(b[:, 0:16], pe_in[0:16, v, :])], [(xt[v][:, 2560:2576], b[:, 0:16], 1.0)]
        if kind == "XT":
            q, = key[1:]
            kv, t = order[q]
            dst = xt[kv][:, 0:2560].rearrange("p (g n) -> p g n", g=GROUPS)[:, :, t * P:(t + 1) * P]
            b2 = b[:, 0:256].rearrange("p (g n) -> p g n", g=GROUPS)
            return [(b2[:, g, :], pair[:, q % 4, g * P:(g + 1) * P]) for g in range(GROUPS)], [(dst, b2, 1.0)]
        if kind == "KT":
            q = lq[key[1:]]
            n = kt_index[key[1:]]
            b4 = b[:, :].rearrange("p (s t) -> p s t", s=4)
            return [(b4[:, s, :], page[:, q % 6, s, :]) for s in range(4)], [(pageT[:, n % 3], b4, 1.0)]
        if kind == "zT":
            return ([(b[0:64, pg * P:(pg + 1) * P], zt[:, pg * 64:(pg + 1) * 64]) for pg in range(NPG)],
                    [(sz[0:64, 0, 0:256], b[0:64, 0:256], 1.0)])
        if kind == "znT":
            b2 = b[0:64, :].rearrange("p (r n) -> p r n", r=2)
            return ([(b[0:64, s * P:(s + 1) * P], zt[:, s * 64:(s + 1) * 64]) for s in range(4)],
                    [(sz[0:64, :, 0:256], b2, 1.0)])
        if kind == "aT":
            return ([(b[:, pg * 64:(pg + 1) * 64], prob[0:64, 0, pg * P:(pg + 1) * P]) for pg in range(NPG)],
                    [(probT[:, 0, 0:128], b[:, 0:128], 1.0)])
        if kind == "osb4":
            return ([(b[0:NB, j * P:(j + 1) * P], ot[:, j, :]) for j in range(4)], [(o_sb[0:NB, :], b[0:NB, :], 1.0)])
        if kind == "pT4":
            moves = [(b[:, (2 * s + pg) * 64:(2 * s + pg + 1) * 64], sz[0:64, s, pg * P:(pg + 1) * P])
                     for s in range(2) for pg in range(2)]
            moves += [(b[:, 256:320], cprob[0:64, 0:128])]
            moves += [(b[0:NB, 320 + 64 * s:384 + 64 * s], pm[0:64, s, :]) for s in range(2)]
            return moves, [(pt4[:, 0:320], b[:, 0:320], 1.0), (pt4[0:NB, 320:448], b[0:NB, 320:448], 1.0)]
        if kind == "ons4":
            dst = o_nsa[0:NB, :].rearrange("p (g r d) -> p g r d", g=GROUPS, r=REP)
            return ([(b[0:NB, j * P:(j + 1) * P], ot[:, j, :]) for j in range(4)],
                    [(dst, b[0:NB, :].rearrange("p (r g d) -> p g r d", g=GROUPS, r=REP), 1.0)])
        if kind in ("mixT", "h2T"):
            i, half = key[1:]
            r = ROWS[i]
            src = mix if kind == "mixT" else h2
            b4 = b[:, 0:4 * r].rearrange("p (k t) -> p k t", k=4)
            moves = [(b4[:, k, :], src[0:r, (4 * half + k) * P:(4 * half + k + 1) * P]) for k in range(4)]
            return moves, [(mixT[:, 4 * half:4 * half + 4, 0:r], b4, 1.0)]
        if kind == "cT":
            return ([(b[:, g * P:(g + 1) * P], cprob[:, g * P:(g + 1) * P]) for g in range(GROUPS)],
                    [(cprobT, b[:, 0:256], 1.0)])
        if kind == "probT":
            s = key[1:]
            n, q = s[0] + 1, order_of[s]
            return ([(b[:, k * P:(k + 1) * P], prob[:, q % 3, k * P:(k + 1) * P]) for k in range(n)],
                    [(probT[:, q % 3, 0:n * P], b[:, 0:n * P], 1.0)])
        return expert_transposes(key, b)

    kt_index = {}
    for kind, n in (("sbk", 16), ("selk", 4), ("wink", 4)):
        for g in range(n):
            kt_index[kind, g] = len(kt_index)
    kt_order = list(kt_index)

    def before_transpose(pe, key):
        kind = key[0]
        if kind == "peT":
            pe.wait_ge(sg["cmp_small"], 64)
        elif kind == "XT":
            sg.wait(pe, f"pair{key[1] % 4}", key[1])
        elif kind == "KT":
            sg.wait(pe, f"page{lq[key[1:]] % 6}", lq[key[1:]])
        elif kind == "zT":
            sg.wait(pe, "x_act", ("zsb",))
        elif kind == "znT":
            sg.wait(pe, "x_act", ("zn",))
        elif kind == "aT":
            sg.wait(pe, "p_ready", "s")
        elif kind == "osb4":
            sg.wait(pe, "o_dve", ("sbs",))
        elif kind == "pT4":
            sg.wait(pe, "s_prob", 0)
        elif kind == "ons4":
            sg.wait(pe, "o_dve", ("nss",))
        elif kind == "mixT":
            sg.wait(pe, "mix", key[1])
        elif kind == "h2T":
            sg.wait(pe, "h2", key[1])
        elif kind == "cT":
            sg.wait(pe, "c_prob", key[1])
        elif kind == "probT":
            if key[2] == SB:
                sg.wait(pe, "p_ready", key[1:])
            else:
                sg.wait(pe, "m_act", key[1:])

    def before_copy(eng, key):
        kind = key[0]
        if kind in ("XT", "peT") and key[1] < 2:
            eng.wait_ge(sg["y_zero"], 16 * EXTRA)
        if kind == "KT" and kt_index[key[1:]] >= 3:
            sg.wait(eng, "scored", kt_order[kt_index[key[1:]] - 3])
        elif kind == "znT":
            sg.wait(eng, "arg", "s")
            sg.wait(eng, "soft", "s")
        elif kind == "probT" and order_of[key[1:]] >= 3:
            sg.wait(eng, "pv", steps[order_of[key[1:]] - 3])
        elif kind == "h2T":
            sg.wait(eng, "m_full", ("wout", key[1], 1))
        elif kind == "mixT" and key[1] != QT:
            sg.wait(eng, "x_full", ("logit", tile_order[tile_order.index(key[1]) - 1]))
        elif kind == "cT" and key[1] > 0:
            sg.wait(eng, "o_done", (key[1] - 1, "cmp"))
        elif kind in ("osb4", "ons4"):
            pass
        else:
            expert_before_copy(eng, key)

    page_reg = []

    def load_small(sp):
        sp.dma_start(pages[:, :], a["page_table"].rearrange("(o b) n -> o (b n)", o=1)).then_inc(sg["pages"], 16)
        for kv, n in enumerate("kv"):
            sp.dma_start(pe_in[0:16, kv, :], a[f"cmp_pe_{n}"][0].rearrange("(q l) d -> q (l d)", l=2)
                         ).then_inc(sg["cmp_small"], 16)
            sp.dma_start(w2[:, kv, :], a[f"cmp_{n}_w2"][0]).then_inc(sg["cmp_small"], 16)
        for k, n in (("router_group_w", 0), ("router_expert_w", 4)):
            src = a[k][0] if n == 0 else a[k][0].rearrange("d g e -> d (g e)")
            sp.dma_start(wr[:, :, n:n + src.shape[1]], src.rearrange("(k p) e -> p k e", p=P)
                         ).then_inc(sg["router_in"], 16)
        sp.dma_start(br[:, 0:4], a["router_group_b"][0:1].partition_broadcast(P).rearrange("p o g -> p (o g)")
                     ).then_inc(sg["router_in"], 16)
        sp.dma_start(br[:, 4:20], a["router_expert_b"][0:1].partition_broadcast(P).rearrange("p o g e -> p (o g e)")
                     ).then_inc(sg["router_in"], 16)
        sp.wait_ge(sg["zero"], 1)
        sp.dma_start(table.rearrange("(p n) o -> p (n o)", p=P), rt[:, 0:80]).then_inc(sg["table_zero"], 16)
        for v in range(EXTRA):
            sp.dma_start(y_dram[(NE + v) * P:(NE + v + 1) * P, :], work[:, 0:D]).then_inc(sg["y_zero"], 16)

    def pool_page(name, j):
        return a[name][0, bass.ds(page_reg[j], 1)].rearrange("o t h d -> (o t) (h d)")

    def sync_more(sp, kind, key):
        if kind == "pages_in":
            sp.wait_ge(sg["pages"], 16)
            for j in range(NB * NPG):
                page_reg.append(sp.value_load(pages[0:1, j:j + 1], min_val=0, max_val=19))
        elif kind == "load_w1":
            sg.wait(sp, "m_full", ("proj", NQ * TILES + TILES - 1))
            for kv, n in enumerate("kv"):
                sp.dma_start(w1[kv], a[f"cmp_{n}_w1"][0].rearrange("(t p) h -> p t h", p=P)).then_inc(sg["w1_in"], 16)
        elif kind == "pair":
            q, = key
            kv, t = order[q]
            if q >= 4:
                sg.wait(sp, "t_full", ("XT", q - 4))
            dst = pair[:, q % 4, :].rearrange("p (g l d) -> p l g d", g=GROUPS, l=2)
            name = "cmp_" + "kv"[kv]
            if t < 2:
                if q == len(order) // 2 - 2:
                    for s in range(4):
                        sp.wait_ge(sg[f"st_raw{s}"], sg.total[f"st_raw{s}"])
                    for s in range(2):
                        sp.wait_ge(sg[f"st_rot{s}"], sg.total[f"st_rot{s}"])
                src = out[name + "_p"][0, 0, t * 2 * P:(t + 1) * 2 * P].rearrange("(p l) g d -> p l g d", l=2)
                for l in range(2):
                    sp.dma_start(dst[:, l], src[:, l]).then_inc(sg[f"pair{q % 4}"], 16)
            else:
                for pg in range(NPG):
                    src = a["cache_" + name][0, bass.ds(page_reg[2 * (t - 2) + pg], 1)].rearrange(
                        "o (p l) g d -> (o p) l g d", l=2)
                    for l in range(2):
                        sp.dma_start(dst[64 * pg:64 * pg + 64, l], src[:, l]).then_inc(sg[f"pair{q % 4}"], 16)
        elif kind == "page":
            q, = key
            what, g = loads[q]
            if q == 0:
                sg.wait(sp, "m_full", ("proj", NCH * TILES - 1))
            if q >= 6:
                w, k = loads[q - 6]
                if w in ("sbk", "selk", "wink"):
                    sg.wait(sp, "t_full", ("KT", w, k))
                elif w == "sbv":
                    sg.wait(sp, "pvs", k // 2)
                else:
                    sg.wait(sp, "pvn", (w, k))
            sem = sg[f"page{q % 6}"]
            if what in ("sbk", "sbv"):
                sp.dma_start(page[:, q % 6].rearrange("p s t -> p (s t)"), pool_page("cache_sb_" + what[2], g)
                             ).then_inc(sem, 16)
            elif what in ("selk", "selv"):
                for s in range(4):
                    sp.dma_start(page[:, q % 6, s, :], pool_page("cache_sel_" + what[3], 4 * g + s)).then_inc(sem, 16)
            else:
                src = a["state_win_" + what[3]][0, 2 * g:2 * g + 2].rearrange("b (q t) g d -> t (b q) (g d)", q=NPG)
                sp.dma_start(page[:, q % 6], src).then_inc(sem, 16)
        elif kind == "load_wout":
            sg.wait(sp, "m_full", ("proj", NCH * TILES - 1))
            for n in (28, 29):
                sg.wait(sp, "t_full", ("pT", n))
                sg.wait(sp, "rotated", n)
            for s in range(4):
                sp.wait_ge(sg[f"st_raw{s}"], sg.total[f"st_raw{s}"])
            sp.dma_start(w_out, a["w_out"][0].rearrange("(k p) n -> p k n", p=P)).then_inc(sg["w_out"], 16)
            sp.dma_start(gain_out[:, 0:512], a["norm_sb_out"][0:1].partition_broadcast(P).rearrange("p o d -> p (o d)")
                         ).then_inc(sg["gain_in"], 16)
            sp.dma_start(gain_out[:, 512:D], a["norm_nsa_out"][0:1].partition_broadcast(P).rearrange("p o d -> p (o d)")
                         ).then_inc(sg["gain_in"], 16)
            sg.wait(sp, "h", TILES - 1)
            sp.dma_start(gain[:, :], a["norm_ffn"][0:1].partition_broadcast(P).rearrange("p o d -> p (o d)")
                         ).then_inc(sg["gain_in"], 16)
        elif kind == "win_state":
            for n in "kv":
                sp.dma_start(out[f"win_{n}_s"][0, :, 0:PAST - 1].rearrange("b t g d -> b (t g d)"),
                             a[f"state_win_{n}"][0, :, 1:PAST].rearrange("b t g d -> b (t g d)")
                             ).then_inc(sg["st_state"], 16)
        elif kind == "h2":
            i, = key
            sg.wait(sp, "h2", i)
            sp.dma_start(h2_dram[i * P:i * P + ROWS[i], :], h2[0:ROWS[i], :]).then_inc(sg["st_h2"], 16)
        else:
            expert_sync(sp, kind, key)

    def gps_begin(pool):
        nc.gpsimd.iota(token[:, :], [[P, TILES]], base=0, channel_multiplier=1,
                       allow_small_or_imprecise_dtypes=True).then_inc(sg["iota"], 1)

    def gps_more(pool, kind, key):
        if kind == "rank":
            i, = key
            sg.wait(pool, "slots", i)
            if i == QT:
                pool.wait_ge(sg["iota"], 1)
                pool.wait_ge(sg["table_zero"], 16)
            for k in range(2):
                nc.gpsimd.indirect_dma_start(
                    table, bass.IndirectOffsetOnAxis(ap=slots[0:ROWS[i], i, k:k + 1], axis=0),
                    token[0:ROWS[i], i:i + 1], None).then_inc(sg["scatter"], 16)
        else:
            expert_gps(pool, kind, key)

    def act_more(act, link, inverse_rms, kind, key):
        if kind == "hid":
            kv, = key
            sg.wait(act, "m_full", ("hidA", kv))
            nc.scalar.copy(hid_a[kv], at("m", ("hidA", kv))[:, 0:322]).then_inc(sg["m_act"], 1)
            sg.wait(act, "gelu_in", kv)
            nc.scalar.activation(hid_u[kv], hid_u[kv], ACT.Exp, scale=-1.5957691216057308).then_inc(sg["gelu_exp"], 1)
        elif kind == "comp":
            kv, = key
            sg.wait(act, "m_full", ("comp", kv))
            b = at("m", ("comp", kv))
            dst, src = (kcT[:, :], b[:, 0:NCHUNK]) if kv == 0 else (vc[:, :, :], b[:, 0:256].rearrange(
                "p (a n) -> p a n", a=2))
            nc.scalar.copy(dst, src).then_inc(sg["m_act"], 1)
        elif kind == "qbd":
            for n in range(25, 30):
                sg.wait(act, "swapped", n)
            nc.scalar.activation(gates[:, 0:QT, :], gates[:, 0:QT, :], ACT.Exp, scale=-1.0)
            nc.scalar.activation(gates[0:NB, QT, :], gates[0:NB, QT, :], ACT.Exp, scale=-1.0
                                 ).then_inc(sg["gates_exp"], 1)
        elif kind in ("zt_sb", "zt_nsa"):
            u, n = (("zsb",), 128) if kind == "zt_sb" else (("zn",), 256)
            sg.wait(act, "scored", ("sbk", 15) if kind == "zt_sb" else ("wink", 3))
            if kind == "zt_nsa":
                sg.wait(act, "t_full", ("zT",))
            nc.scalar.copy(zt[:, 0:n], bank[7][:, 0:n]).then_inc(sg["x_act"], 1)
        elif kind == "front":
            _, _, z, so, _, _ = sb_views(key)
            if key == ("s",):
                wait_transposed(act, ("zT",))
            else:
                sg.wait(act, "m_full", key)
                q = sb_index[key]
                if q >= 2:
                    wait_arg(act, sb_order[q - 2])
            link(nc.scalar.activation(so, z, ACT.Abs))
            link(nc.scalar.activation(so, so, ACT.Exp, scale=-1.0))
            nc.scalar.activation(so, so, ACT.Ln, bias=1.0).then_inc(sg["soft"], 1)
        elif kind == "back":
            if key == ("s",) or key[1] == SB:
                r, n, _, _, _, p = sb_views(key)
                wait_arg(act, key_of(key))
                nc.scalar.activation(p, p, ACT.Exp).then_inc(sg["p_ready"], 1)
            else:
                i, b, h = key
                q = order_of[key]
                sg.wait(act, "arg", key)
                before_prob_write(act, key)
                if h == 0 and i > 0:
                    sg.wait(act, "branch", (i - 1, b))
                nc.scalar.activation(prob[:, q % 3, 0:(i + 1) * P], at("m", key)[:, 0:(i + 1) * P], ACT.Exp,
                                     bias=st[:, 32 + q % 4:33 + q % 4],
                                     accum_out=st[:, (b - 1) * 8 + h:(b - 1) * 8 + h + 1]).then_inc(sg["m_act"], 1)
        elif kind == "sample_small":
            sg.wait(act, "s_max", 0)
            for s in range(2):
                nc.scalar.activation(sz[0:64, s, 0:257], sz[0:64, s, 0:257], ACT.Exp, bias=st[0:64, 48 + s:49 + s],
                                     accum_out=st[0:64, 52 + s:53 + s])
            nc.scalar.activation(cprob[0:64, 0:128], cprob[0:64, 0:128], ACT.Exp, bias=st[0:64, 50:51],
                                 accum_out=st[0:64, 54:55]).then_inc(sg["s_exp"], 1)
        elif kind == "cmp_score":
            i, = key
            sg.wait(act, "c_max", i)
            nc.scalar.activation(cprob, cprob, ACT.Exp).then_inc(sg["c_exp"], 1)
        elif kind == "mix_ssq":
            i, = key
            inverse_rms(small[0:ROWS[i], 8:10], 512, "rstd", ("mix", i))
        elif kind == "ffn_ssq":
            i, = key
            inverse_rms(small[0:ROWS[i], 10:11], D, "rstd", ("ffn", i))
        elif kind == "route":
            i, = key
            r = ROWS[i]
            sg.wait(act, "r_max", (i, 0))
            nc.scalar.activation(rt[0:r, 64:68], rt[0:r, 0:4], ACT.Exp, bias=rt[0:r, 70:71],
                                 accum_out=rt[0:r, 71:72]).then_inc(sg["r_exp"], 1)
            sg.wait(act, "r_max", (i, 1))
            nc.scalar.activation(rt[0:r, 73:74], rt[0:r, 72:73], ACT.Exp).then_inc(sg["r_exp"], 1)
        else:
            expert_act(act, link, inverse_rms, kind, key)

    def dve_begin(dve, link):
        nc.vector.memset(chosen[:, :, :, :], 0.0)
        nc.vector.memset(expert[:, :, :], 0.0)
        nc.vector.memset(slot_f[:, :, :], 0.0)
        nc.vector.memset(work[:, 0:D], 0.0)
        nc.vector.memset(rt[:, :], 0.0).then_inc(sg["zero"], 1)

    def dve_more(dve, link, kind, key):
        V = nc.vector
        if kind == "hid":
            kv, = key
            b = at("m", ("hidB", kv))
            v, u = hid[kv], hid_u[kv]
            sg.wait(dve, "m_full", ("hidB", kv))
            sg.wait(dve, "m_act", ("hidA", kv))
            link(V.tensor_tensor(smp[:, 200 + kv:201 + kv], hid_a[kv][:, 320:321], b[:, 321:322], ALU.add))
            V.scalar_tensor_tensor(v, b[:, 1:321], smp[:, 200 + kv:201 + kv], hid_a[kv][:, 0:320], ALU.add, ALU.add
                                   ).then_inc(sg["m_dve"], 1)
            sg.wait(dve, "m_dve", ("hidB", kv))
            link(V.tensor_tensor(u, v, v, ALU.mult))
            link(V.tensor_scalar(u, u, 0.044715, 1.0, ALU.mult, ALU.add))
            V.tensor_tensor(u, u, v, ALU.mult).then_inc(sg["gelu_in"], 1)
            sg.wait(dve, "gelu_exp", kv)
            link(V.tensor_scalar(u, u, 1.0, None, ALU.add))
            link(V.reciprocal(u, u))
            V.tensor_tensor(v, v, u, ALU.mult).then_inc(sg["hid"], 1)
        elif kind == "qbd":
            sg.wait(dve, "m_full", ("comp", 0))
            link(V.memset(smp[:, 0:128], 0.0))
            wait_transposed(dve, ("pT", SBQ * TILES + QT))
            wait_transposed(dve, ("pT", NQ * TILES + QT))
            for e in range(2):
                rows = slice(64 * e, 64 * e + 64)
                V.tensor_copy(qbd[rows, :, :, e], qsbT[rows, :, SEQ:TOK])
                ins = V.tensor_copy(qbn[rows, :, REP * e:REP * e + REP].rearrange("p b h -> p h b"),
                                    qnsaT[rows, :, SEQ:TOK])
            ins.then_inc(sg["qbd"], 1)
            sg.wait(dve, "gates_exp", 0)
            for r, g in ((P, gates[:, 0:QT, :]), (NB, gates[0:NB, QT:TILES, :])):
                link(V.tensor_scalar(g, g, 1.0, None, ALU.add))
                ins = V.reciprocal(g, g)
            ins.then_inc(sg["gates"], 1)
        elif kind == "mid":
            if key == ("s",) or key[1] == SB:
                r, n, z, so, pl, p = sb_views(key)
                sg.wait(dve, "soft", key_of(key))
                link(V.scalar_tensor_tensor(pl, z, 0.0, so, ALU.max, ALU.add))
                if key != ("s",):
                    before_prob_write(dve, key)
                link(V.tensor_tensor_scan(p[:, ::-1], c["one"][0:r].to_broadcast([r, n]), pl[:, ::-1], 0.0,
                                          ALU.mult, ALU.add))
                ins = V.tensor_tensor(p, z, p, ALU.subtract)
                if key == ("s",):
                    ins.then_inc(sg["arg"], 1)
                else:
                    ins.then_inc(sg["m_dve"], 1)
            else:
                i, b, h = key
                q = order_of[key]
                sg.wait(dve, "m_full", key)
                if q >= 4 and steps[q - 4][1] != SB:
                    sg.wait(dve, "m_act", steps[q - 4])
                V.tensor_reduce(st[:, 32 + q % 4:33 + q % 4], at("m", key)[:, 0:(i + 1) * P], AX.X, ALU.max,
                                negate=True).then_inc(sg["arg"], 1)
        elif kind == "sample_small":
            sg.wait(dve, "m_full", ("snew",))
            b = at("m", ("snew",))[0:64, 0:16].rearrange("p (t b) -> p t b", t=2)
            V.tensor_tensor(snew[0:64], b, c["maskb"][0:64].unsqueeze(1).to_broadcast([64, 2, NB]), ALU.mult
                            ).then_inc(sg["m_dve"], 1)
            sg.wait(dve, "m_full", ("gsp",))
            b = at("m", ("gsp",))[0:64, 0:24].rearrange("p (h t) -> p t h", t=3)
            V.tensor_tensor(gsp[0:64], b, c["maskh"][0:64].unsqueeze(1).to_broadcast([64, 3, 8]), ALU.mult
                            ).then_inc(sg["m_dve"], 1)
            sg.wait(dve, "m_full", ("cs",))
            V.tensor_tensor(cprob[0:64, 0:128], at("m", ("cs",))[0:64, 0:128], c["sneg"][0:64], ALU.add
                            ).then_inc(sg["m_dve"], 1)
            sg.wait(dve, "m_dve", ("cs",))
            wait_transposed(dve, ("znT",))
            link(V.tensor_reduce(sz[0:64, :, 256:257].rearrange("p t o -> p (t o)"), snew[0:64], AX.X, ALU.add))
            V.tensor_reduce(gw[0:64], gsp[0:64], AX.X, ALU.add)
            V.tensor_reduce(st[0:64, 50:51], cprob[0:64, 0:128], AX.X, ALU.max, negate=True)
            V.tensor_reduce(st[0:64, 48:50], sz[0:64, :, 0:257], AX.X, ALU.max, negate=True).then_inc(sg["s_max"], 1)
            sg.wait(dve, "s_exp", 0)
            link(V.reciprocal(st[0:64, 52:55], st[0:64, 52:55]))
            V.tensor_tensor(st[0:64, 56:58], st[0:64, 52:54], gw[0:64, 1:3], ALU.mult)
            link(V.tensor_tensor(st[0:64, 58:59], st[0:64, 54:55], gw[0:64, 0:1], ALU.mult))
            for s in range(2):
                link(V.tensor_scalar(sz[0:64, s, 0:257], sz[0:64, s, 0:257], st[0:64, 56 + s:57 + s], None, ALU.mult))
                V.tensor_scalar(pm[0:64, s, :], c["maskb"][0:64], sz[0:64, s, 256:257], None, ALU.mult)
            V.tensor_scalar(cprob[0:64, 0:128], cprob[0:64, 0:128], st[0:64, 58:59], None, ALU.mult
                            ).then_inc(sg["s_prob"], 1)
        elif kind == "ots":
            sg.wait(dve, "pvs", NB - 1)
            b = at("o", ("sbs",))[:, 0:64].rearrange("p (j b t) -> p j b t", j=4, b=NB)
            V.tensor_copy(ot[0:64], b[0:64, :, :, 0])
            V.tensor_copy(ot[64:P], b[64:P, :, :, 1]).then_inc(sg["o_dve"], 1)
        elif kind == "otn":
            sg.wait(dve, "pvn", ("winv", 3))
            sg.wait(dve, "t_full", ("osb4",))
            b = at("o", ("nss",))[:, 0:64].rearrange("p (b h) -> p h b", b=NB)
            V.tensor_copy(ot[0:64], b[0:64, 0:REP])
            V.tensor_copy(ot[64:P], b[64:P, REP:HEADS]).then_inc(sg["o_dve"], 1)
        elif kind == "cmp_score":
            i, = key
            b = bank[7][:, 0:256].rearrange("p (h n) -> p h n", h=HEADS)
            cp = cprob.rearrange("p (h n) -> p h n", h=HEADS)
            sg.wait(dve, "x_full", ("cmp", i))
            if i > 0:
                sg.wait(dve, "t_full", ("cT", i - 1))
            neg = c["cneg"][:, i * 32:(i + 1) * 32].unsqueeze(1).to_broadcast([P, HEADS, 32])
            one = c["cone"][:, i * 32:(i + 1) * 32].unsqueeze(1).to_broadcast([P, HEADS, 32])
            V.tensor_tensor(cp, b, neg, ALU.add).then_inc(sg["x_dve"], 1)
            sg.wait(dve, "x_dve", ("cmp", i))
            link(V.tensor_reduce(st[:, 60:68], cp, AX.X, ALU.max))
            V.tensor_tensor(cp, cp, st[:, 60:68].unsqueeze(2).to_broadcast([P, HEADS, 32]), ALU.subtract
                            ).then_inc(sg["c_max"], 1)
            sg.wait(dve, "c_exp", i)
            link(V.tensor_tensor(cp, cp, one, ALU.mult))
            link(V.tensor_reduce(st[:, 60:68], cp, AX.X, ALU.add))
            link(V.tensor_scalar(st[:, 60:68], st[:, 60:68], 1e-30, None, ALU.max))
            link(V.reciprocal(st[:, 60:68], st[:, 60:68]))
            link(V.tensor_tensor(st[:, 60:68], st[:, 60:68], gate_rows(i)[:, 0], ALU.mult))
            V.tensor_tensor(cp, cp, st[:, 60:68].unsqueeze(2).to_broadcast([P, HEADS, 32]), ALU.mult
                            ).then_inc(sg["c_prob"], 1)
        elif kind == "branch":
            i, b = key
            o3 = at("o", key)[:, :].rearrange("p (h d) -> p h d", h=HEADS)
            sg.wait(dve, "pv", (i, b, HEADS - 1))
            if b == SB:
                V.tensor_copy(o_sb, at("o", key)[:, :]).then_inc(sg["o_dve"], 1)
                ob = at("o", (i, "cmp"))
                sg.wait(dve, "o_done", (i, "cmp"))
                V.tensor_copy(o_nsa, ob[:, :]).then_inc(sg["o_dve"], 1)
                sg.wait(dve, "o_dve", (i, "cmp"))
                return
            w = st[:, 72 + 8 * (b - 1):80 + 8 * (b - 1)]
            link(V.reciprocal(w, st[:, 8 * (b - 1):8 * b]))
            link(V.tensor_tensor(w, w, gate_rows(i)[:, b], ALU.mult))
            V.tensor_tensor(o_part.rearrange("p (h d) -> p h d", h=HEADS), o3,
                            w.unsqueeze(2).to_broadcast([P, HEADS, HD]), ALU.mult).then_inc(sg["o_dve"], 1)
            sg.wait(dve, "o_dve", key)
            V.tensor_tensor(o_nsa, o_nsa, o_part, ALU.add).then_inc(sg["branch"], 1)
        elif kind == "mix_ssq":
            i, = key
            r = ROWS[i]
            if i == QT:
                for n in range(2):
                    dve.wait_ge(sg[f"st_rot{n}"], sg.total[f"st_rot{n}"])
                wait_transposed(dve, ("osb4",))
                wait_transposed(dve, ("ons4",))
            else:
                sg.wait(dve, "branch", (i, WIN))
            if i != QT:
                sg.wait(dve, "t_full", ("mixT", tile_order[tile_order.index(i) - 1], 1))
            V.tensor_tensor_reduce(mix[0:r, 0:512], o_sb[0:r], o_sb[0:r], 1.0, 0.0, ALU.mult, ALU.add, small[0:r, 8:9])
            V.tensor_tensor_reduce(mix[0:r, 512:D], o_nsa[0:r], o_nsa[0:r], 1.0, 0.0, ALU.mult, ALU.add,
                                   small[0:r, 9:10]).then_inc(sg["ssq"], 1)
        elif kind == "mix":
            i, = key
            r = ROWS[i]
            if i == QT:
                dve.wait_ge(sg["gain_in"], 48)
            sg.wait(dve, "rstd", ("mix", i))
            V.scalar_tensor_tensor(mix[0:r, 0:512], o_sb[0:r], small[0:r, 8:9], gain_out[0:r, 0:512],
                                   ALU.mult, ALU.mult)
            V.scalar_tensor_tensor(mix[0:r, 512:D], o_nsa[0:r], small[0:r, 9:10], gain_out[0:r, 512:D],
                                   ALU.mult, ALU.mult).then_inc(sg["mix"], 1)
        elif kind == "wout":
            i, = key
            r = ROWS[i]
            for half in range(2):
                sl = slice(512 * half, 512 * half + 512)
                sg.wait(dve, "m_full", ("wout", i, half))
                V.tensor_tensor(x[0:r, i, sl], x[0:r, i, sl], at("m", ("wout", i, half))[0:r, :], ALU.add
                                ).then_inc(sg["m_dve"], 1)
        elif kind == "ffn_ssq":
            i, = key
            r = ROWS[i]
            sg.wait(dve, "m_dve", ("wout", i, 1))
            if i != QT:
                before = tile_order[tile_order.index(i) - 1]
                sg.wait(dve, "st_h2", before)
                sg.wait(dve, "t_full", ("h2T", before, 1))
            V.tensor_tensor_reduce(h2[0:r], x[0:r, i, :], x[0:r, i, :], 1.0, 0.0, ALU.mult, ALU.add,
                                   small[0:r, 10:11]).then_inc(sg["ssq"], 1)
        elif kind == "h2":
            i, = key
            r = ROWS[i]
            sg.wait(dve, "rstd", ("ffn", i))
            V.scalar_tensor_tensor(h2[0:r], x[0:r, i, :], small[0:r, 10:11], gain[0:r, :], ALU.mult, ALU.mult
                                   ).then_inc(sg["h2"], 1)
        elif kind == "route":
            i, = key
            r = ROWS[i]
            gl, ex, m8, el, n8 = rt[0:r, 0:8], rt[0:r, 16:32], rt[0:r, 32:40], rt[0:r, 8:16], rt[0:r, 40:48]
            prod = rt[0:r, 48:64].rearrange("p (e g) -> p e g", e=4)
            b = bank[7]
            if i == QT:
                dve.wait_ge(sg["router_in"], 64)
                dve.wait_ge(sg["table_zero"], 16)
                link(V.memset(rt[:, 0:16], NEG))
            sg.wait(dve, "x_full", ("logit", i))
            V.tensor_tensor(gl[:, 0:4], b[0:r, 0:4], br[0:r, 0:4], ALU.add)
            V.tensor_tensor(ex, b[0:r, 4:20], br[0:r, 4:20], ALU.add).then_inc(sg["x_dve"], 1)
            sg.wait(dve, "x_dve", ("logit", i))
            link(V.max(m8, gl))
            V.tensor_scalar(rt[0:r, 70:71], m8[:, 0:1], -1.0, None, ALU.mult).then_inc(sg["r_max"], 1)
            link(V.max_index(smi[0:r, 0:8], m8, gl))
            link(V.tensor_copy(rt[0:r, 74:75], smi[0:r, 0:1]))
            link(V.tensor_scalar(rt[0:r, 76:80], c["iota16"][0:r, 0:4], rt[0:r, 74:75], None, ALU.is_equal))
            link(V.tensor_tensor(prod, ex.rearrange("p (g e) -> p e g", g=4),
                                 rt[0:r, 76:80].unsqueeze(1).to_broadcast([r, 4, 4]), ALU.mult))
            link(V.tensor_reduce(el[:, 0:4], prod, AX.X, ALU.add))
            link(V.max(n8, el))
            V.tensor_tensor(rt[0:r, 72:73], n8[:, 1:2], n8[:, 0:1], ALU.subtract).then_inc(sg["r_max"], 1)
            link(V.max_index(smi[0:r, 8:16], n8, el))
            V.tensor_scalar(rt[0:r, 75:76], rt[0:r, 74:75], 4.0, None, ALU.mult)
            link(V.tensor_copy(rt[0:r, 80:82], smi[0:r, 8:10]))
            link(V.tensor_scalar(rt[0:r, 80:82], rt[0:r, 80:82], rt[0:r, 75:76], None, ALU.add))
            V.tensor_copy(expert[0:r, i, :], rt[0:r, 80:82])
            for k in range(2):
                ins = V.tensor_scalar(chosen[0:r, i, k], c["iota16"][0:r], rt[0:r, 80 + k:81 + k],
                                      None, ALU.is_equal)
            link(ins)
            V.tensor_tensor(onehot[0:r, i, :], chosen[0:r, i, 0], chosen[0:r, i, 1], ALU.add
                            ).then_inc(sg["onehot"], 1)
            sg.wait(dve, "r_exp", (i, 1))
            V.tensor_scalar(rt[0:r, 83:84], rt[0:r, 73:74], 1.0, None, ALU.add)
            link(V.tensor_copy(rt[0:r, 82:83], rt[0:r, 71:72]))
            link(V.reciprocal(rt[0:r, 82:84], rt[0:r, 82:84]))
            link(V.tensor_tensor(weight[0:r, i, 0:1], rt[0:r, 82:83], rt[0:r, 83:84], ALU.mult))
            link(V.tensor_tensor(weight[0:r, i, 1:2], weight[0:r, i, 0:1], rt[0:r, 73:74], ALU.mult))
        elif kind == "rank":
            i, = key
            r = ROWS[i]
            b = bank[7]
            sg.wait(dve, "x_full", ("rank", i))
            V.tensor_tensor(rt[0:r, 128:144], b[0:r, 0:16], c["base16"][0:r], ALU.add).then_inc(sg["x_dve"], 1)
            sg.wait(dve, "x_dve", ("rank", i))
            link(V.tensor_tensor(rt[0:r, 144:176].rearrange("p (k e) -> p k e", k=2),
                                 chosen[0:r, i],
                                 rt[0:r, 128:144].unsqueeze(1).to_broadcast([r, 2, 16]), ALU.mult))
            link(V.tensor_reduce(slot_f[0:r, i, :], rt[0:r, 144:176].rearrange("p (k e) -> p k e", k=2), AX.X, ALU.add))
            V.tensor_copy(slots[0:r, i, :], slot_f[0:r, i, :]).then_inc(sg["slots"], 1)
        else:
            expert_dve(dve, link, kind, key)

    pe_chain = [0]

    def pe_link(ins):
        pe_chain[0] += 1
        ins.then_inc(sg["pe_chain"], 1)
        nc.tensor.wait_ge(sg["pe_chain"], pe_chain[0])

    def pe_more(pe, kind, key):
        T = nc.tensor
        if kind == "hid":
            kv, = key
            if kv == 0:
                pe.wait_ge(sg["w1_in"], 32)
            for q in range(len(order)):
                if order[q][0] == kv:
                    wait_transposed(pe, ("XT", q))
            wait_transposed(pe, ("peT", kv))
            for half, name in enumerate(("hidA", "hidB")):
                acquire(pe, "m", (name, kv))
                for lp in range(8):
                    ins = T.matmul(at("m", (name, kv))[:, 0:322], w1[kv][:, 8 * half + lp, :],
                                   xt[kv][:, lp:2576:8], start=(lp == 0), stop=(lp == 7))
                ins.then_inc(sg["m_full"], 1)
        elif kind == "comp":
            kv, = key
            sg.wait(pe, "hid", kv)
            acquire(pe, "m", ("comp", kv))
            b = at("m", ("comp", kv))
            if kv == 0:
                for g in range(GROUPS):
                    ins = T.matmul(b[64 * g:64 * g + 64, 0:NCHUNK], w2[:, 0, :], hid[0][:, g * NCHUNK:(g + 1) * NCHUNK],
                                   start=True, stop=True)
            else:
                for g in range(GROUPS):
                    for copy in range(4):
                        T.matmul(b[32 * copy:32 * copy + 32, g * HD:(g + 1) * HD],
                                 hid[1][:, g * NCHUNK:g * NCHUNK + 32], w2[:, 1, :], start=True, stop=True)
                    ins = T.matmul(b[:, P + g * HD:P + (g + 1) * HD], hid[1][:, g * NCHUNK + 32:(g + 1) * NCHUNK],
                                   w2[:, 1, :], start=True, stop=True)
            ins.then_inc(sg["m_full"], 1)
        elif kind == "zs":
            what, g = key
            if key == ("sbk", 0):
                acquire(pe, "x", ("zsb",))
                sg.wait(pe, "qbd", 0)
            if key == ("selk", 0):
                acquire(pe, "x", ("zn",))
            wait_transposed(pe, ("KT",) + key)
            kt = pageT[:, kt_index[key] % 3]
            for s in range(4):
                if what == "sbk":
                    b_, pg = g // 2, g % 2
                    at_ = pg * 64 + b_ * 8 + 2 * s
                    ins = T.matmul(bank[7][:, at_:at_ + 2], kt[:, s, :], qbd[:, s, b_, :], start=True, stop=True)
                else:
                    j = 4 * g + s
                    b_, pg = j // 2, j % 2
                    at_ = (P if what == "wink" else 0) + pg * 64 + b_ * 8
                    ins = T.matmul(bank[7][:, at_:at_ + 8], kt[:, s, :], qbn[:, b_, :], start=True, stop=True)
            ins.then_inc(sg["scored"], 1)
        elif kind == "sample_small":
            q64 = smp[:, 64:128]
            wait_transposed(pe, ("pT", KV4 * TILES + QT))
            wait_transposed(pe, ("pT", KV2 * TILES + QT))
            sg.wait(pe, "m_act", ("comp", 1))
            sg.wait(pe, "gates", 0)
            acquire(pe, "m", ("snew",))
            T.matmul(at("m", ("snew",))[0:64, 0:8], q64, kselT[:, SEQ:TOK], start=True, stop=True)
            T.matmul(at("m", ("snew",))[0:64, 8:16], q64, kwinT[:, SEQ:TOK], start=True, stop=True
                     ).then_inc(sg["m_full"], 1)
            acquire(pe, "m", ("gsp",))
            T.matmul(at("m", ("gsp",))[0:64, 0:24], c["spread"][0:NB, 0:64], gates[0:NB, QT, :], start=True, stop=True
                     ).then_inc(sg["m_full"], 1)
            acquire(pe, "m", ("cs",))
            T.matmul(at("m", ("cs",))[0:64, 0:P], q64, kcT[:, 32:NCHUNK], start=True, stop=True
                     ).then_inc(sg["m_full"], 1)
        elif kind == "pvs":
            b_, = key
            if b_ == 0:
                acquire(pe, "o", ("sbs",))
                wait_transposed(pe, ("aT",))
            for pg in range(NPG):
                q = lq["sbv", 2 * b_ + pg]
                sg.wait(pe, f"page{q % 6}", q)
            for j in range(4):
                for pg in range(NPG):
                    q = lq["sbv", 2 * b_ + pg]
                    last = T.matmul(at("o", ("sbs",))[:, j * 16 + 2 * b_:j * 16 + 2 * b_ + 2], page[:, q % 6, j, :],
                                    probT[:, 0, pg * 64 + b_ * 8 + 2 * j:pg * 64 + b_ * 8 + 2 * j + 2],
                                    start=(pg == 0), stop=(pg == 1))
            last.then_inc(sg["pvs"], 1)
        elif kind == "pvn":
            what, g = key
            b = at("o", ("nss",))
            if key == ("selv", 0):
                acquire(pe, "o", ("nss",))
                wait_transposed(pe, ("pT4",))
                T.matmul(b[:, 0:64], vsel[0:NB, QT, :], pt4[0:NB, 320:384], start=True, stop=False)
                T.matmul(b[:, 0:64], vwin[0:NB, QT, :], pt4[0:NB, 384:448], start=False, stop=False)
                T.matmul(b[:, 0:64], vc[:, 1, :], pt4[:, 256:320], start=False, stop=False)
            q = lq[key]
            sg.wait(pe, f"page{q % 6}", q)
            for s in range(4):
                j = 4 * g + s
                b_, pg = j // 2, j % 2
                base = (2 * (what == "winv") + pg) * 64 + b_ * 8
                last = T.matmul(b[:, b_ * 8:b_ * 8 + 8], page[:, q % 6, s, :], pt4[:, base:base + 8],
                                start=False, stop=(what == "winv" and j == 15))
            last.then_inc(sg["pvn"], 1)
        elif kind == "otn":
            pass
        elif kind == "score":
            i, b, h = key
            acquire(pe, "m", key)
            t = at("m", key)
            n, qs = (i + 1) * P, slice(i * P, (i + 1) * P)
            if key == steps[0]:
                pe.wait_ge(sg["const_b"], 16)
                for j in range(len(proj)):
                    if blocks[proj[j][0]]:
                        wait_transposed(pe, ("pT", j))
            if b == SB:
                rows = slice(64 * (h % 2), 64 * (h % 2) + 64)
                lhs, rhs = qsbT[rows, h // 2, qs], ksbT[rows, h // 2, 0:n]
            else:
                g, r = h // REP, h % REP
                rows = slice(64 * g, 64 * g + 64)
                lhs, rhs = qnsaT[rows, r, qs], (kselT if b == SEL else kwinT)[rows, 0:n]
            T.matmul(t[:, 0:n], lhs, rhs, start=True, stop=False)
            T.matmul(t[:, qs], c["identb"], c["before"] if b == SB else c["upto"], start=False, stop=True
                     ).then_inc(sg["m_full"], 1)
        elif kind == "pv":
            i, b, h = key
            if h == 0:
                acquire(pe, "o", (i, b))
            wait_transposed(pe, ("probT",) + key)
            q = order_of[key]
            for k in range(i + 1):
                v = vsb[:, k, h * HD:(h + 1) * HD] if b == SB else (vsel if b == SEL else vwin)[
                    :, k, (h // REP) * HD:(h // REP + 1) * HD]
                ins = T.matmul(at("o", (i, b))[:, h * HD:(h + 1) * HD], probT[:, q % 3, k * P:(k + 1) * P], v,
                               start=(k == 0), stop=(k == i))
            ins.then_inc(sg["pv"], 1)
        elif kind == "cmp_score":
            i, = key
            acquire(pe, "x", ("cmp", i))
            for h in range(HEADS):
                g, r = h // REP, h % REP
                rows = slice(64 * g, 64 * g + 64)
                ins = T.matmul(bank[7][:, h * 32:(h + 1) * 32], qnsaT[rows, r, i * P:(i + 1) * P], kcT[rows, 0:32],
                               start=True, stop=True)
                if h == REP - 1:
                    pe_link(ins)
            ins.then_inc(sg["x_full"], 1)
        elif kind == "cmp_pv":
            i, = key
            acquire(pe, "o", (i, "cmp"))
            wait_transposed(pe, ("cT", i))
            for r in range(REP):
                rows = slice(32 * r, 32 * r + 32)
                for g in range(GROUPS):
                    h = g * REP + r
                    ins = T.matmul(at("o", (i, "cmp"))[:, h * HD:(h + 1) * HD], cprobT[rows, g * P:(g + 1) * P],
                                   vc[rows, 0, g * HD:(g + 1) * HD], start=True, stop=True)
                if r < REP - 1:
                    pe_link(ins)
            ins.then_inc(sg["o_done"], 1)
        elif kind == "wout":
            i, = key
            r = ROWS[i]
            if i == QT:
                pe.wait_ge(sg["w_out"], 16)
            for half in range(2):
                wait_transposed(pe, ("mixT", i, half))
            for half in range(2):
                acquire(pe, "m", ("wout", i, half))
                for k in range(KD):
                    ins = T.matmul(at("m", ("wout", i, half))[0:r, :], mixT[:, k, 0:r],
                                   w_out[:, k, 512 * half:512 * half + 512], start=(k == 0), stop=(k == KD - 1))
                ins.then_inc(sg["m_full"], 1)
        elif kind == "route":
            i, = key
            r = ROWS[i]
            acquire(pe, "x", ("logit", i))
            if i == QT:
                pe.wait_ge(sg["router_in"], 64)
            for half in range(2):
                wait_transposed(pe, ("h2T", i, half))
            for k in range(KD):
                ins = T.matmul(bank[7][0:r, 0:20], mixT[:, k, 0:r], wr[:, k, :], start=(k == 0), stop=(k == KD - 1))
            ins.then_inc(sg["x_full"], 1)
        elif kind == "rank":
            i, = key
            r = ROWS[i]
            acquire(pe, "x", ("rank", i))
            sg.wait(pe, "onehot", i)
            done = tile_order[:tile_order.index(i)]
            for n, j in enumerate(done):
                T.matmul(bank[7][0:r, 0:16], c["onesb"][0:ROWS[j], 0:r], onehot[0:ROWS[j], j, :], start=(n == 0),
                         stop=False)
            T.matmul(bank[7][0:r, 0:16], c["earlier"][0:r, 0:r], onehot[0:r, i, :], start=(not done), stop=True
                     ).then_inc(sg["x_full"], 1)
        else:
            expert_pe(pe, kind, key)

    def expert_weights(region):
        return view(region, 0, [KD, FF]), view(region, 4096, [KD, FF]), view(region, 8192, [FF // P, D])

    weights = [expert_weights(reg0), expert_weights(reg1)]
    rows_in = [work[:, 0:1024], work[:, 1024:2048]]
    sig = [work[:, 2048:2560], work[:, 2560:3072]]
    acts = [work[:, 3072:3584], work[:, 3584:4096]]
    actsT = [view(work, 4096, [4, P]), view(work, 4608, [4, P])]

    def flat(t):
        return t[:, :, :].rearrange("p a b -> p (a b)")

    rowsT = [flat(qsbT)[:, 0:1024].rearrange("p (k t) -> p k t", k=KD),
             flat(qsbT)[:, 1024:2048].rearrange("p (k t) -> p k t", k=KD)]
    y_rows = [flat(ksbT)[:, 0:1024], flat(ksbT)[:, 1024:2048]]
    ids_row = flat(qnsaT)[0:NE, 0:P]
    ids = sb("ids", [P, NE], U32)
    more_f = sb("more_f", [P, 1])
    more_ids = sb("more_ids", [P, 1], U32)
    extra = flat(qnsaT)[:, P:P + 704]
    extra_i = sb("extra_i", [1, 24], I32)
    gathered = view(reg0, 0, [2 * TILES, D])

    use("x", ("idx",), "dve")
    step("idx")
    sg.mark("ids_in", 0, 16)
    sg.mark("ids", 0)
    use("x", ("count",), "dve")
    step("count")
    sg.mark("extra", 0)
    sg.mark("y_slots", 0)
    step("experts")
    for n in ("e_rows_a", "e_rows_v", "e_gate", "e_exp", "e_gated", "e_up", "e_act", "e_actT_full", "e_actT",
              "e_down", "e_y_a", "e_y_v", "e_rowsT_full"):
        sg.mark(n, 0)
    for b in range(2):
        for n in ("e_x", "e_wgu", "e_wd", "e_st"):
            sg.mark(f"{n}{b}", 0)
    for n in ("v_w", "v_idx", "v_idc", "v_x", "v_rowsT_full", "v_rows", "v_gu", "v_exp", "v_act", "v_actT_full",
              "v_actT", "v_down", "v_y", "v_st", "v_passed", "v_passed_sp"):
        sg.mark(n, 0)
    sg.mark("gain_final", 0, 16)
    for i in range(TILES):
        step("final", i)
        sg.mark(f"gathered{i}", i, 32)
        sg.mark("combined", i)
        sg.mark("ssq_final", i)
        sg.mark("final", i)
        sg.mark("st_y", i, 16)
    at_load0 = PLAN.index(("otn", ())) + 2
    PLAN.insert(at_load0, ("expert0", ()))
    final_waits = [(n, t) for n, t in sg.total.items() if n.startswith("st_")]
    LAST = NE - 1

    def expert_transposes(key, b):
        raise KeyError(key)

    def expert_before_copy(eng, key):
        pass

    def overflow(eng, one):
        sg.wait(eng, "extra", 0)
        count = eng.value_load(extra_i[0:1, 16:17], min_val=0, max_val=EXTRA)
        with eng.Fori(0, EXTRA) as v:
            with eng.If(v < count):
                one(v)

    def load_gate_up(sp, e, b, sem):
        for name, dst in (("w_gate", weights[b][0]), ("w_up", weights[b][1])):
            src = a[name][0, bass.ds(e, 1)].rearrange("o (k p) f -> p (o k) f", p=P)
            sp.dma_start(dst, src).then_inc(sem, 16)

    def load_down(sp, e, b, sem):
        src = a["w_down"][0, bass.ds(e, 1)].rearrange("o (k p) f -> p (o k) f", p=P)
        sp.dma_start(weights[b][2], src).then_inc(sem, 16)

    def expert_sync(sp, kind, key):
        if kind == "expert0":
            sg.wait(sp, "t_full", ("ons4",))
            load_gate_up(sp, 0, 0, sg["e_wgu0"])
            load_down(sp, 0, 0, sg["e_wd0"])
        elif kind == "experts":
            sg.wait(sp, "x_full", ("logit", QT - 1))
            sg.wait(sp, "m_full", ("wout", QT - 1, 1))
            for n in range(TILES):
                sg.wait(sp, "st_h2", n)
            load_gate_up(sp, 1, 1, sg["e_wgu1"])
            load_down(sp, 1, 1, sg["e_wd1"])

            def one(j, b, n):
                if j is not LAST:
                    sp.wait_ge(sg["e_up"], j)
                    load_gate_up(sp, j + 1, 1 - b, sg[f"e_wgu{1 - b}"])
                    sp.wait_ge(sg["e_down"], j)
                    load_down(sp, j + 1, 1 - b, sg[f"e_wd{1 - b}"])
                store_rows(j - 1, 1 - b, j)

            def store_rows(e, b, done):
                sp.wait_ge(sg["e_y_a"], done)
                sp.wait_ge(sg["e_y_v"], done)
                sp.dma_start(y_dram[bass.ds(e * P, P), :], y_rows[b]).then_inc(sg[f"e_st{b}"], 16)

            with sp.Fori(0, NE // 2 - 1) as it:
                one(2 * it + 1, 1, it)
                one(2 * it + 2, 0, it + 1)
            one(LAST, 1, NE // 2 - 1)
            store_rows(LAST, 1, NE)

            def more(v):
                e = sp.value_load(extra_i[0:1, bass.ds(v, 1)], min_val=0, max_val=NE - 1)
                row = sp.value_load(extra_i[0:1, bass.ds(v + 8, 1)], min_val=0, max_val=NE * CAP - P)
                load_gate_up(sp, e, 0, sg["v_w"])
                load_down(sp, e, 0, sg["v_w"])
                sp.dma_start(more_f[:, :], table[bass.ds(row, P), :]).then_inc(sg["v_idx"], 16)
                sp.wait_ge(sg["v_y"], 2 * v + 2)
                sp.dma_start(y_dram[bass.ds((v + NE) * P, P), :], y_rows[0]).then_inc(sg["v_st"], 16)
                sp.wait_ge(sg["v_st"], 16 * v + 16)
                sp.sem_inc(sg["v_passed_sp"], 1)

            for b in range(2):
                sp.wait_ge(sg[f"e_st{b}"], 16 * NE // 2)
            overflow(sp, more)
            sp.dma_start(gain[:, :], a["norm_final"].rearrange("(o d) -> o d", o=1).partition_broadcast(P).rearrange(
                "p o d -> p (o d)")).then_inc(sg["gain_final"], 16)
        elif kind == "final":
            i, = key
            sg.wait(sp, "final", i)
            dst = out["y_p"][0, i * P:(i + 1) * P, :] if i < QT else out["y_s"][:, 0, :]
            sp.dma_start(dst, x[0:ROWS[i], i, :]).then_inc(sg["st_y"], 16)

    def expert_gps(pool, kind, key):
        if kind == "idx":
            pool.wait_ge(sg["scatter"], sg.total["scatter"])
            pool.dma_start(ids_row, table.rearrange("(e n) o -> e (n o)", e=NE)[:, 0:P]).then_inc(sg["ids_in"], 16)
        elif kind == "experts":
            pool.wait_ge(sg["ids"], 1)
            pool.wait_ge(sg["st_h2"], sg.total["st_h2"])
            sg.wait(pool, "pv", steps[-1])
            sg.wait(pool, "x_full", ("logit", QT - 1))
            for j in range(NE):
                if j >= 2:
                    pool.wait_ge(sg["e_rowsT_full"], 2 * (j - 2) + 2)
                nc.gpsimd.indirect_dma_start(rows_in[j % 2], None, h2_dram,
                                             bass.IndirectOffsetOnAxis(ap=ids[:, j:j + 1], axis=0)
                                             ).then_inc(sg[f"e_x{j % 2}"], 16)

            def more(v):
                pool.wait_ge(sg["v_idx"], 16 * v + 16)
                pool.sem_inc(sg["v_passed"], 1)
                nc.gpsimd.tensor_copy(more_ids[:, :], more_f[:, :]).then_inc(sg["v_idc"], 1)
                pool.wait_ge(sg["v_idc"], v + 1)
                pool.sem_inc(sg["v_passed"], 1)
                nc.gpsimd.indirect_dma_start(rows_in[0], None, h2_dram,
                                             bass.IndirectOffsetOnAxis(ap=more_ids[:, 0:1], axis=0)
                                             ).then_inc(sg["v_x"], 16)
                pool.wait_ge(sg["v_x"], 16 * v + 16)
                pool.sem_inc(sg["v_passed"], 1)

            pool.wait_ge(sg["e_rowsT_full"], 2 * NE)
            overflow(pool, more)
        elif kind == "final":
            i, = key
            if i == 0:
                pool.wait_ge(sg["gain_final"], 16)
                sg.wait(pool, "y_slots", 0)
            for k in range(2):
                nc.gpsimd.indirect_dma_start(gathered[0:ROWS[i], 2 * i + k, :], None, y_dram,
                                             bass.IndirectOffsetOnAxis(ap=y_slots[0:ROWS[i], i, k:k + 1], axis=0)
                                             ).then_inc(sg[f"gathered{i}"], 16)

    def gps_end(pool):
        pass

    def expert_act(act, link, inverse_rms, kind, key):
        A = nc.scalar
        if kind == "experts":
            def rows_out(j, b):
                act.wait_ge(sg["e_rowsT_full"], 2 * j + 1)
                A.copy(rowsT[b][:, 0:4, :], bank[3][:, :].rearrange("p (k t) -> p k t", k=4)
                       ).then_inc(sg["e_rows_a"], 1)

            def exp_gate(j, b):
                act.wait_ge(sg["e_gate"], j + 1)
                A.activation(sig[b], bank[0][:, :], ACT.Exp, scale=-1.0).then_inc(sg["e_exp"], 1)

            def acts_out(j, b):
                act.wait_ge(sg["e_actT_full"], j + 1)
                A.copy(actsT[b], bank[5][:, :].rearrange("p (k t) -> p k t", k=4)).then_inc(sg["e_actT"], 1)

            def y_out(j, b, n):
                act.wait_ge(sg["e_down"], j + 1)
                if n is not 0:
                    act.wait_ge(sg[f"e_st{b}"], 16 * n)
                A.copy(y_rows[b][:, 0:512], bank[2][:, :]).then_inc(sg["e_y_a"], 1)

            def one(j, b, n):
                exp_gate(j, b)
                if j is not 0:
                    acts_out(j - 1, 1 - b)
                    y_out(j - 1, 1 - b, n if b else n - 1)
                if j is not LAST:
                    rows_out(j + 1, 1 - b)

            rows_out(0, 0)
            one(0, 0, 0)
            one(1, 1, 0)
            with act.Fori(1, NE // 2 - 1) as it:
                one(2 * it, 0, it)
                one(2 * it + 1, 1, it)
            one(NE - 2, 0, NE // 2 - 1)
            one(LAST, 1, NE // 2 - 1)
            acts_out(LAST, 1)
            y_out(LAST, 1, NE // 2 - 1)

            def more(v):
                act.wait_ge(sg["v_rowsT_full"], v + 1)
                A.copy(rowsT[0][:, 0:4, :], bank[3][:, :].rearrange("p (k t) -> p k t", k=4)).then_inc(sg["v_rows"], 1)
                act.wait_ge(sg["v_gu"], v + 1)
                A.activation(sig[0], bank[0][:, :], ACT.Exp, scale=-1.0).then_inc(sg["v_exp"], 1)
                act.wait_ge(sg["v_actT_full"], v + 1)
                A.copy(actsT[0], bank[5][:, :].rearrange("p (k t) -> p k t", k=4)).then_inc(sg["v_actT"], 1)
                act.wait_ge(sg["v_down"], v + 1)
                A.copy(y_rows[0][:, 0:512], bank[2][:, :]).then_inc(sg["v_y"], 1)
            overflow(act, more)
        elif kind == "final":
            i, = key
            r = ROWS[i]
            sg.wait(act, "combined", i)
            link(A.activation(gathered[0:r, 2 * i, :], x[0:r, i, :], ACT.Square, accum_out=small[0:r, 16 + i:17 + i]))
            link(A.activation(small[0:r, 16 + i:17 + i], small[0:r, 16 + i:17 + i], ACT.Ln, bias=c["eps"][0:r],
                              scale=1.0 / D))
            A.activation(small[0:r, 16 + i:17 + i], small[0:r, 16 + i:17 + i], ACT.Exp, scale=-0.5
                         ).then_inc(sg["ssq_final"], 1)

    def expert_dve(dve, link, kind, key):
        V = nc.vector
        if kind == "idx":
            sg.wait(dve, "x_full", ("idx",))
            V.tensor_copy(ids[:, :], bank[7][:, 0:NE]).then_inc(sg["x_dve"], 1)
            sg.wait(dve, "x_dve", ("idx",))
            V.memset(smi[:, 40:41], 0).then_inc(sg["ids"], 1)
        elif kind == "count":
            sg.wait(dve, "x_full", ("count",))
            cnt, t0, cum, n = (extra[:, 16 * q:16 * q + 16] for q in range(4))
            le = extra[0:1, 64:192].rearrange("p (v e) -> p v e", v=8)
            prod = extra[0:1, 192:320].rearrange("p (v e) -> p v e", v=8)
            ex, tl, rowf = extra[0:1, 320:328], extra[0:1, 328:336], extra[0:1, 336:344]
            V.tensor_copy(cnt, bank[7][:, 0:16]).then_inc(sg["x_dve"], 1)
            sg.wait(dve, "x_dve", ("count",))
            link(V.tensor_scalar(n, cnt, float(P), None, ALU.is_gt))
            for k in range(2, 5):
                link(V.tensor_scalar(t0, cnt, float(k * P), None, ALU.is_gt))
                link(V.tensor_tensor(n, n, t0, ALU.add))
            link(V.tensor_tensor_scan(cum, c["one"].to_broadcast([P, 16]), n, 0.0, ALU.mult, ALU.add))
            link(V.tensor_tensor(le, cum[0:1].unsqueeze(1).to_broadcast([1, 8, 16]),
                                 c["iota16"][0:1, 0:8].unsqueeze(2).to_broadcast([1, 8, 16]), ALU.is_le))
            link(V.tensor_tensor(prod, le, n[0:1].unsqueeze(1).to_broadcast([1, 8, 16]), ALU.mult))
            V.tensor_reduce(ex, le, AX.X, ALU.add)
            link(V.tensor_reduce(tl, prod, AX.X, ALU.add))
            link(V.tensor_scalar(ex, ex, float(NE - 1), None, ALU.min))
            link(V.tensor_tensor(tl, c["iota16"][0:1, 0:8], tl, ALU.subtract))
            link(V.tensor_scalar(tl, tl, 1.0, float(P), ALU.add, ALU.mult))
            link(V.scalar_tensor_tensor(rowf, ex, float(CAP), tl, ALU.mult, ALU.add))
            link(V.tensor_scalar(rowf, rowf, float(NE * CAP - P), None, ALU.min))
            V.tensor_copy(extra_i[0:1, 0:8], ex)
            V.tensor_copy(extra_i[0:1, 8:16], rowf)
            V.tensor_copy(extra_i[0:1, 16:17], cum[0:1, 15:16]).then_inc(sg["extra"], 1)
        elif kind == "experts":
            def rows_out(j, b):
                dve.wait_ge(sg["e_rowsT_full"], 2 * j + 2)
                V.tensor_copy(rowsT[b][:, 4:8, :], bank[4][:, :].rearrange("p (k t) -> p k t", k=4)
                              ).then_inc(sg["e_rows_v"], 1)

            def gated(j, b):
                dve.wait_ge(sg["e_exp"], j + 1)
                link_loop(V.tensor_scalar(sig[b], sig[b], 1.0, None, ALU.add), 3 * j + 1)
                link_loop(V.reciprocal(sig[b], sig[b]), 3 * j + 2)
                link_loop(V.tensor_tensor(sig[b], sig[b], bank[0][:, :], ALU.mult), 3 * j + 3)
                dve.wait_ge(sg["e_up"], j + 1)
                V.tensor_tensor(acts[b], sig[b], bank[1][:, :], ALU.mult).then_inc(sg["e_act"], 1)

            def link_loop(ins, value):
                ins.then_inc(sg["e_gated"], 1)
                dve.wait_ge(sg["e_gated"], value)

            def place_results():
                n10 = 2 * TILES
                cum, n = extra[:, 32:48], extra[:, 48:64]
                shift, rank = extra[:, 64:80], extra[:, 80:80 + n10]
                over, base = extra[:, 96:96 + n10], extra[:, 112:112 + n10]
                prod = extra[:, 344:344 + n10 * NE].rearrange("p (k e) -> p k e", e=NE)
                e_ = expert[:, :, :].rearrange("p i k -> p (i k)")
                link(V.tensor_tensor(shift, cum, n, ALU.subtract))
                link(V.tensor_scalar(shift, shift, float(NE - 1), None, ALU.add))
                link(V.tensor_tensor(shift, shift, c["iota16"], ALU.subtract))
                link(V.tensor_tensor(prod, chosen[:, :, :, :].rearrange("p i k e -> p (i k) e"),
                                     shift.unsqueeze(1).to_broadcast([P, n10, NE]), ALU.mult))
                V.tensor_reduce(base, prod, AX.X, ALU.add)
                link(V.scalar_tensor_tensor(rank, e_, float(-CAP), slot_f[:, :, :].rearrange("p i k -> p (i k)"),
                                            ALU.mult, ALU.add))
                link(V.tensor_scalar(over, rank, float(P), None, ALU.is_ge))
                link(V.tensor_tensor(base, base, over, ALU.mult))
                link(V.tensor_tensor(base, base, e_, ALU.add))
                link(V.scalar_tensor_tensor(rank, base, float(P), rank, ALU.mult, ALU.add))
                V.tensor_copy(y_slots[:, :, :].rearrange("p i k -> p (i k)"), rank).then_inc(sg["y_slots"], 1)

            def y_out(j, b, n):
                dve.wait_ge(sg["e_down"], j + 1)
                if n is not 0:
                    dve.wait_ge(sg[f"e_st{b}"], 16 * n)
                V.tensor_copy(y_rows[b][:, 512:D], bank[6][:, :]).then_inc(sg["e_y_v"], 1)

            def one(j, b, n):
                gated(j, b)
                if j is not 0:
                    y_out(j - 1, 1 - b, n if b else n - 1)
                if j is not LAST:
                    rows_out(j + 1, 1 - b)

            rows_out(0, 0)
            one(0, 0, 0)
            place_results()
            one(1, 1, 0)
            with dve.Fori(1, NE // 2 - 1) as it:
                one(2 * it, 0, it)
                one(2 * it + 1, 1, it)
            one(NE - 2, 0, NE // 2 - 1)
            one(LAST, 1, NE // 2 - 1)
            y_out(LAST, 1, NE // 2 - 1)

            def more(v):
                dve.wait_ge(sg["v_rowsT_full"], v + 1)
                V.tensor_copy(rowsT[0][:, 4:8, :], bank[4][:, :].rearrange("p (k t) -> p k t", k=4)
                              ).then_inc(sg["v_rows"], 1)
                dve.wait_ge(sg["v_exp"], v + 1)
                base = 3 * NE + 3 * v
                link_loop(V.tensor_scalar(sig[0], sig[0], 1.0, None, ALU.add), base + 1)
                link_loop(V.reciprocal(sig[0], sig[0]), base + 2)
                link_loop(V.tensor_tensor(sig[0], sig[0], bank[0][:, :], ALU.mult), base + 3)
                V.tensor_tensor(acts[0], sig[0], bank[1][:, :], ALU.mult).then_inc(sg["v_act"], 1)
                dve.wait_ge(sg["v_down"], v + 1)
                V.tensor_copy(y_rows[0][:, 512:D], bank[6][:, :]).then_inc(sg["v_y"], 1)
            overflow(dve, more)
        elif kind == "final":
            i, = key
            r = ROWS[i]
            sg.wait(dve, f"gathered{i}", i)
            xi = x[0:r, i, :]
            link(V.scalar_tensor_tensor(xi, gathered[0:r, 2 * i, :], weight[0:r, i, 0:1], xi, ALU.mult, ALU.add))
            V.scalar_tensor_tensor(xi, gathered[0:r, 2 * i + 1, :], weight[0:r, i, 1:2], xi, ALU.mult, ALU.add
                                   ).then_inc(sg["combined"], 1)
            if i > 0:
                finish_rows(dve, i - 1)
            if i == TILES - 1:
                finish_rows(dve, i)

    def finish_rows(dve, i):
        r = ROWS[i]
        if i == 0:
            dve.wait_ge(sg["gain_final"], 16)
        sg.wait(dve, "ssq_final", i)
        nc.vector.scalar_tensor_tensor(x[0:r, i, :], x[0:r, i, :], small[0:r, 16 + i:17 + i], gain[0:r, :],
                                       ALU.mult, ALU.mult).then_inc(sg["final"], 1)

    def expert_pe(pe, kind, key):
        T = nc.tensor
        if kind == "idx":
            acquire(pe, "x", ("idx",))
            pe.wait_ge(sg["ids_in"], 16)
            T.transpose(bank[7][:, 0:NE], ids_row, ident[0:NE, 0:NE]).then_inc(sg["x_full"], 1)
        elif kind == "count":
            acquire(pe, "x", ("count",))
            for n, i in enumerate(tile_order):
                ins = T.matmul(bank[7][:, 0:NE], c["onesb"][0:ROWS[i], :], onehot[0:ROWS[i], i, :],
                               start=(n == 0), stop=(n == TILES - 1))
            ins.then_inc(sg["x_full"], 1)
        elif kind == "experts":
            def transpose_rows(b, sem, both):
                for half in range(2):
                    for k in range(4):
                        kk = 4 * half + k
                        ins = T.transpose(bank[3 + half][:, k * P:(k + 1) * P], rows_in[b][:, kk * P:(kk + 1) * P],
                                          ident)
                    if half or both:
                        ins.then_inc(sem, 1)

            def product(out_bank, lhs, rhs):
                n = len(lhs)
                for k in range(n):
                    ins = T.matmul(out_bank[:, :], lhs[k], rhs[k], start=(k == 0), stop=(k == n - 1))
                return ins

            def gate_or_up(b, which, sem):
                product(bank[which], [rowsT[b][:, k, :] for k in range(KD)],
                        [weights[b][which][:, k, :] for k in range(KD)]).then_inc(sem, 1)

            def transpose_acts(b, sem):
                for k in range(4):
                    ins = T.transpose(bank[5][:, k * P:(k + 1) * P], acts[b][:, k * P:(k + 1) * P], ident)
                ins.then_inc(sem, 1)

            def down(b, sem):
                for half, t in ((0, bank[2]), (1, bank[6])):
                    ins = product(t, [actsT[b][:, k, :] for k in range(4)],
                                  [weights[b][2][:, k, 512 * half:512 * half + 512] for k in range(4)])
                ins.then_inc(sem, 1)

            def rows_of(b, n):
                pe.wait_ge(sg[f"e_x{b}"], 16 * n + 16)
                transpose_rows(b, sg["e_rowsT_full"], True)

            def finish_down(j, b, n):
                pe.wait_ge(sg["e_actT"], j + 1)
                pe.wait_ge(sg[f"e_wd{b}"], 16 * n + 16)
                if j is not 0:
                    pe.wait_ge(sg["e_y_a"], j)
                    pe.wait_ge(sg["e_y_v"], j)
                down(b, sg["e_down"])

            def one(j, b, n):
                pe.wait_ge(sg["e_rows_a"], j + 1)
                pe.wait_ge(sg["e_rows_v"], j + 1)
                pe.wait_ge(sg[f"e_wgu{b}"], 32 * n + 32)
                if j is not 0:
                    pe.wait_ge(sg["e_gated"], 3 * j)
                gate_or_up(b, 0, sg["e_gate"])
                if j is not 0:
                    pe.wait_ge(sg["e_act"], j)
                    transpose_acts(1 - b, sg["e_actT_full"])
                gate_or_up(b, 1, sg["e_up"])
                if j is not 0:
                    finish_down(j - 1, 1 - b, n if b else n - 1)
                if j is not LAST:
                    rows_of(1 - b, n if not b else n + 1)

            acquire_all(pe)
            rows_of(0, 0)
            one(0, 0, 0)
            one(1, 1, 0)
            with pe.Fori(1, NE // 2 - 1) as it:
                one(2 * it, 0, it)
                one(2 * it + 1, 1, it)
            one(NE - 2, 0, NE // 2 - 1)
            one(LAST, 1, NE // 2 - 1)
            pe.wait_ge(sg["e_act"], NE)
            transpose_acts(1, sg["e_actT_full"])
            finish_down(LAST, 1, NE // 2 - 1)

            def more(v):
                pe.wait_ge(sg["v_x"], 16 * v + 16)
                transpose_rows(0, sg["v_rowsT_full"], False)
                pe.wait_ge(sg["v_rows"], 2 * v + 2)
                pe.wait_ge(sg["v_w"], 48 * v + 48)
                product(bank[0], [rowsT[0][:, k, :] for k in range(KD)], [weights[0][0][:, k, :] for k in range(KD)])
                gate_or_up(0, 1, sg["v_gu"])
                pe.wait_ge(sg["v_act"], v + 1)
                transpose_acts(0, sg["v_actT_full"])
                pe.wait_ge(sg["v_actT"], v + 1)
                down(0, sg["v_down"])
            pe.wait_ge(sg["e_y_a"], NE)
            pe.wait_ge(sg["e_y_v"], NE)
            overflow(pe, more)

    def acquire_all(pe):
        for ring in banks:
            for n in range(max(0, len(uses[ring]) - len(banks[ring])), len(uses[ring])):
                k, free = uses[ring][n]
                sg.wait(pe, ring + "_" + free, k)

    def transposes(key):
        b = at("t", key)
        kind = key[0]
        if kind == "hT":
            _, i, half = key
            r = ROWS[i]
            b4 = b[:, 0:4 * r].rearrange("p (k t) -> p k t", k=4)
            moves = [(b4[:, k, :], hn[0:r, i % 2, (4 * half + k) * P:(4 * half + k + 1) * P]) for k in range(4)]
            return moves, [(hT[:, 4 * half:4 * half + 4, i * P:i * P + r], b4, 1.0)]
        if kind == "pT":
            n = key[1]
            cc, i = proj[n]
            r, t0 = ROWS[i], i * P
            b4 = b[:, 0:4 * r].rearrange("p (k t) -> p k t", k=4)
            if cc in (SBQ, SBK):
                dst = qsbT if cc == SBQ else ksbT
                moves = [(b4[:, j, :], raw[0:r, rq[n] % 4, j * P:(j + 1) * P]) for j in range(4)]
                return moves, [(dst[:, :, t0:t0 + r], b4, 0.125 if cc == SBQ else 1.0)]
            if cc == NQ:
                src = rot[0:r, n % 2, :]
                return [(b4[:, j, :], src[:, j * P:(j + 1) * P]) for j in range(REP)], [(qnsaT[:, :, t0:t0 + r], b4, 0.125)]
            src, dst = (rot[0:r, n % 2, 256:384], kselT) if cc == KV4 else (rot[0:r, n % 2, 0:128], kwinT)
            return [(b[:, 0:r], src)], [(dst[:, t0:t0 + r], b[:, 0:r], 1.0)]
        return more_transposes(key, b)

    def wait_transposed(eng, key):
        sg.wait(eng, "t_" + freed_by("t", key), key)

    def heads(tile, n, r, cc):
        v = tile[0:r, n, :]
        if cc == NQ:
            return v.rearrange("p (g r d) -> p g r d" if tile is raw else "p (r g d) -> p g r d", g=GROUPS, r=REP)
        if cc == KV4:
            return v.rearrange("p (s x h d) -> p s x h d", s=2, x=2, h=GROUPS)[:, :, 0]
        return v[:, 0:P].rearrange("p (s h d) -> p s h d", s=1, h=GROUPS)

    def store(sp, cc, i):
        n, r = cc * TILES + i, ROWS[i]
        side = "p" if i < QT else "s"

        def rows(name, width):
            o = out[f"{name}_{side}"]
            if i < QT:
                return o[0, 0, i * P:(i + 1) * P].rearrange("t h d -> t (h d)")
            if name[:3] == "win":
                return o[0, :, PAST - 1].rearrange("b h d -> b (h d)")
            return o[0, :, 0].rearrange("b h d -> b (h d)")

        if cc in (SBK, SBV, KV4, KV2):
            sg.wait(sp, "m_act", ("proj", n))
        if cc == SBK:
            sp.dma_start(rows("sb_k", 512), raw[0:r, rq[n] % 4, :]).then_inc(sg[f"st_raw{rq[n] % 4}"], 16)
        if cc == SBV:
            sp.dma_start(rows("sb_v", 512), vsb[0:r, i, :]).then_inc(sg["st_v"], 16)
        if cc in (KV4, KV2):
            sg.wait(sp, "rotated", n)
        if cc == KV4:
            for name, src, sem in (("cmp_k", rot[0:r, n % 2, 0:128], f"st_rot{n % 2}"),
                                   ("cmp_v", raw[0:r, rq[n] % 4, 128:256], f"st_raw{rq[n] % 4}"),
                                   ("sel_k", rot[0:r, n % 2, 256:384], f"st_rot{n % 2}"),
                                   ("sel_v", raw[0:r, rq[n] % 4, 384:512], f"st_raw{rq[n] % 4}")):
                sp.dma_start(rows(name, 128), src).then_inc(sg[sem], 16)
        if cc == KV2:
            sp.dma_start(rows("win_k", 128), rot[0:r, n % 2, 0:128]).then_inc(sg[f"st_rot{n % 2}"], 16)
            sp.dma_start(rows("win_v", 128), raw[0:r, rq[n] % 4, 128:256]).then_inc(sg[f"st_raw{rq[n] % 4}"], 16)

    block = ctx.enter_context(nc.Block())

    @block.sync
    def _(sp):
        sp.dma_start(cf[:, :], a["const_f"]).then_inc(sg["const"], 16)
        sp.dma_start(gain[:, :], a["norm_attn"][0:1, :].partition_broadcast(P).rearrange("p o d -> p (o d)")
                     ).then_inc(sg["gain_attn"], 16)
        for kind, key in PLAN:
            if kind == "load_w":
                cc = key[0]
                if cc >= 3:
                    sg.wait(sp, "m_full", ("proj", (cc - 3) * TILES + TILES - 1))
                n = min(CHUNK, COLS - cc * CHUNK)
                sp.dma_start(win[:, cc % 3, :, 0:n], a["w_in"][0, :, cc * CHUNK:cc * CHUNK + n].rearrange(
                    "(k p) n -> p k n", p=P)).then_inc(sg[f"w{cc % 3}"], 16)
                if cc == 0:
                    for i in range(TILES):
                        src = a["x_prompt"][0, i * P:(i + 1) * P, :] if i < QT else a["x_sample"][:, 0, :]
                        sp.dma_start(x[0:ROWS[i], i, :], src).then_inc(sg[f"x{i}"], 16)
                    sp.dma_start(cb[:, :], a["const_b"]).then_inc(sg["const_b"], 16)
                    load_small(sp)
            elif kind == "store":
                store(sp, *key)
            else:
                sync_more(sp, kind, key)
        for name, total in final_waits:
            sp.wait_ge(sg[name], total)

    @block.gpsimd
    def _(pool):
        gps_begin(pool)
        for kind, key in PLAN:
            if kind == "rope":
                n, = key
                cc, i = proj[n]
                r = ROWS[i]
                sg.wait(pool, "m_act", ("proj", n))
                if cc > NQ or i >= 2:
                    sg.wait(pool, "rotated", n - 2)
                src, dst = heads(raw, rq[n] % 4, r, cc), heads(swp, n % 2, r, cc)
                s, h = src.shape[1:3]
                if n == NQ * TILES:
                    pool.wait_ge(sg["const"], 16)
                for to, frm in ((0, 32), (32, 0)):
                    sin = rope[0:r, i, HD + to:HD + to + 32].unsqueeze(1).unsqueeze(1).to_broadcast([r, s, h, 32])
                    ins = nc.gpsimd.tensor_tensor(dst[:, :, :, to:to + 32], src[:, :, :, frm:frm + 32], sin, ALU.mult)
                if cc == KV4:
                    ins = nc.gpsimd.tensor_copy(vsel[0:r, i, :], raw[0:r, rq[n] % 4, 384:512])
                if cc == KV2:
                    nc.gpsimd.tensor_copy(vwin[0:r, i, :], raw[0:r, rq[n] % 4, 128:256])
                    ins = nc.gpsimd.tensor_copy(gates[0:r, i, :], raw[0:r, rq[n] % 4, 256:280])
                ins.then_inc(sg["swapped"], 1)
            else:
                gps_more(pool, kind, key)
        gps_end(pool)

    @block.scalar
    def _(act):
        chain = [0]

        def link(ins):
            chain[0] += 1
            ins.then_inc(sg["act_chain"], 1)
            act.wait_ge(sg["act_chain"], chain[0])

        def inverse_rms(dst, width, name, key):
            sg.wait(act, "ssq", key)
            rows = dst.shape[0]
            link(nc.scalar.activation(dst, dst, ACT.Ln, bias=c["eps"][0:rows], scale=1.0 / width))
            nc.scalar.activation(dst, dst, ACT.Exp, scale=-0.5).then_inc(sg[name], 1)

        def copy_out(key):
            _, moves = transposes(key)
            sg.wait(act, "t_full", key)
            before_copy(act, key)
            for dst, src, scale in moves:
                ins = nc.scalar.activation(dst, src, ACT.Copy, scale=scale)
            ins.then_inc(sg["t_act"], 1)

        act.preload_act_table_set("natural_log_exp_and_others")
        act.wait_ge(sg["const"], 16)
        for kind, key in PLAN:
            if kind == "norm":
                i, = key
                inverse_rms(small[0:ROWS[i], i:i + 1], D, "rstd", ("attn", i))
            elif kind == "T":
                if freed_by("t", key) == "act":
                    copy_out(key)
            elif kind == "proj":
                n, = key
                cc, i = proj[n]
                r, w = ROWS[i], min(CHUNK, COLS - cc * CHUNK)
                sg.wait(act, "m_full", ("proj", n))
                if cc == SBV:
                    dst = vsb[0:r, i, :]
                else:
                    dst = raw[0:r, rq[n] % 4, 0:w]
                    if rq[n] >= 4:
                        before = raws[rq[n] - 4]
                        pc = proj[before][0]
                        if pc in (SBQ, SBK):
                            sg.wait(act, "t_full", ("pT", before))
                        if pc in (SBK, KV4, KV2):
                            sg.wait(act, f"st_raw{rq[n] % 4}", before)
                        if pc in (NQ, KV4, KV2):
                            sg.wait(act, "rotated", before)
                nc.scalar.copy(dst, at("m", ("proj", n))[0:r, 0:w]).then_inc(sg["m_act"], 1)
            else:
                act_more(act, link, inverse_rms, kind, key)

    @block.vector
    def _(dve):
        chain = [0]

        def link(ins):
            chain[0] += 1
            ins.then_inc(sg["dve_chain"], 1)
            dve.wait_ge(sg["dve_chain"], chain[0])

        dve_begin(dve, link)
        for kind, key in PLAN:
            if kind == "norm":
                i, = key
                r = ROWS[i]
                dve.wait_ge(sg[f"x{i}"], 16)
                if i >= 2:
                    sg.wait(dve, "t_full", ("hT", i - 2, 1))
                h = hn[0:r, i % 2, :]
                nc.vector.tensor_tensor_reduce(h, x[0:r, i, :], x[0:r, i, :], 1.0, 0.0, ALU.mult, ALU.add,
                                               small[0:r, i:i + 1]).then_inc(sg["ssq"], 1)
                if i == 0:
                    dve.wait_ge(sg["gain_attn"], 16)
                sg.wait(dve, "rstd", ("attn", i))
                sg.wait(dve, "ssq", ("attn", i))
                nc.vector.scalar_tensor_tensor(h, x[0:r, i, :], small[0:r, i:i + 1], gain[0:r, :],
                                               ALU.mult, ALU.mult).then_inc(sg["h"], 1)
            elif kind == "T":
                if freed_by("t", key) == "dve":
                    _, moves = transposes(key)
                    sg.wait(dve, "t_full", key)
                    before_copy(dve, key)
                    for dst, src, scale in moves:
                        if scale == 1.0:
                            ins = nc.vector.tensor_copy(dst, src)
                        else:
                            ins = nc.vector.tensor_scalar(dst, src, scale, None, ALU.mult)
                    ins.then_inc(sg["t_dve"], 1)
            elif kind == "rope":
                n, = key
                cc, i = proj[n]
                r = ROWS[i]
                sg.wait(dve, "m_act", ("proj", n))
                if cc > NQ or i >= 2:
                    sg.wait(dve, "t_full", ("pT", n - 2))
                    if proj[n - 2][0] in (KV4, KV2):
                        sg.wait(dve, f"st_rot{n % 2}", n - 2)
                src, dst, sw = heads(raw, rq[n] % 4, r, cc), heads(rot, n % 2, r, cc), heads(swp, n % 2, r, cc)
                s, h = src.shape[1:3]
                cos = rope[0:r, i, 0:HD].unsqueeze(1).unsqueeze(1).to_broadcast([r, s, h, HD])
                if n == NQ * TILES:
                    dve.wait_ge(sg["const"], 16)
                link(nc.vector.tensor_tensor(dst, src, cos, ALU.mult))
                sg.wait(dve, "swapped", n)
                nc.vector.tensor_tensor(dst, dst, sw, ALU.add).then_inc(sg["rotated"], 1)
            else:
                dve_more(dve, link, kind, key)

    @block.tensor
    def _(pe):
        pe.wait_ge(sg["const"], 16)
        for kind, key in PLAN:
            if kind == "T":
                if key[0] == "hT":
                    sg.wait(pe, "h", key[1])
                elif key[0] == "pT":
                    sg.wait(pe, "rotated" if proj[key[1]][0] >= NQ else "m_act",
                            key[1] if proj[key[1]][0] >= NQ else ("proj", key[1]))
                else:
                    before_transpose(pe, key)
                acquire(pe, "t", key)
                moves, _ = transposes(key)
                for dst, src in moves:
                    ins = nc.tensor.transpose(dst, src, ident[0:src.shape[0], 0:src.shape[0]])
                ins.then_inc(sg["t_full"], 1)
            elif kind == "proj":
                n, = key
                cc, i = proj[n]
                r, w = ROWS[i], min(CHUNK, COLS - cc * CHUNK)
                if i == 0:
                    sg.wait(pe, f"w{cc % 3}", cc)
                if cc == 0:
                    wait_transposed(pe, ("hT", i, 0))
                    wait_transposed(pe, ("hT", i, 1))
                acquire(pe, "m", ("proj", n))
                for k in range(KD):
                    ins = nc.tensor.matmul(at("m", ("proj", n))[0:r, 0:w], hT[:, k, i * P:i * P + r],
                                           win[:, cc % 3, k, 0:w], start=(k == 0), stop=(k == KD - 1))
                ins.then_inc(sg["m_full"], 1)
            else:
                pe_more(pe, kind, key)


OUTS = [("y_p", (1, SEQ, D)), ("y_s", (NB, 1, D)), ("sb_k_p", (1, 1, SEQ, HEADS, HD)), ("sb_v_p", (1, 1, SEQ, HEADS, HD)),
        ("cmp_k_p", (1, 1, SEQ, GROUPS, HD)), ("cmp_v_p", (1, 1, SEQ, GROUPS, HD)),
        ("sel_k_p", (1, 1, SEQ, GROUPS, HD)), ("sel_v_p", (1, 1, SEQ, GROUPS, HD)),
        ("win_k_p", (1, 1, SEQ, GROUPS, HD)), ("win_v_p", (1, 1, SEQ, GROUPS, HD)),
        ("sb_k_s", (1, NB, 1, HEADS, HD)), ("sb_v_s", (1, NB, 1, HEADS, HD)),
        ("cmp_k_s", (1, NB, 1, GROUPS, HD)), ("cmp_v_s", (1, NB, 1, GROUPS, HD)),
        ("sel_k_s", (1, NB, 1, GROUPS, HD)), ("sel_v_s", (1, NB, 1, GROUPS, HD)),
        ("win_k_s", (1, NB, PAST, GROUPS, HD)), ("win_v_s", (1, NB, PAST, GROUPS, HD))]


def kernel(**inputs):
    import concourse.bacc as bacc
    from concourse.bass_utils import run_bass_kernel_spmd

    nc = bacc.Bacc("TRN2", target_bir_lowering=False, num_devices=1)
    parts, bparts = host_constants()
    constants = {"const_f": np.concatenate(list(parts.values()), 1).astype(np.float32),
                 "const_b": np.concatenate(list(bparts.values()), 1).astype(mybir.dt.np(BF16))}
    arrays, a, out = {}, {}, {}
    for name, v in list(inputs.items()) + list(constants.items()):
        v = np.ascontiguousarray(v)
        arrays[name] = v
        a[name] = nc.dram_tensor(name, v.shape, mybir.dt.from_np(v.dtype), kind="ExternalInput").ap()
    for name, shape in OUTS:
        out[name] = nc.dram_tensor("out_" + name, shape, F32, kind="ExternalOutput").ap()
    build(nc, a, out)
    r = run_bass_kernel_spmd(nc, [arrays], core_ids=[0])
    return tuple(r.results[0]["out_" + name] for name, _ in OUTS)
```

```python
import numpy as np
from contextlib import ExitStack

import concourse.bass as bass
import concourse.mybir as mybir

ALU = mybir.AluOpType
ACT = mybir.ActivationFunctionType
AX = mybir.AxisListType
F32 = mybir.dt.float32
BF16 = mybir.dt.bfloat16
I32 = mybir.dt.int32
U32 = mybir.dt.uint32

P = 128
D = 1024
SEQ = 512
NB = 8
PAST = 256
PAGE = 128
NPG = PAST // PAGE
HD = 64
HEADS = 8
GROUPS = 2
REP = HEADS // GROUPS
KD = D // P
QT = SEQ // P
TILES = QT + 1
ROWS = [P] * QT + [NB]
TOK = SEQ + NB
COLS = 2840
CHUNK = 512
NCH = 6
SBQ, SBK, SBV, NQ, KV4, KV2 = range(NCH)
CT = QT // 2 + NB
NCHUNK = CT * 16
NEG = -1.0e30
EPS = 1e-6
NE = 16
FF = 512
CAP = 5 * P
POOL_FINAL = (1, 3)
FIRST_PAIR = 4
ZEROS_AT = 26
OUTPUT_AFTER = 7
WOUT_PARTS = ((0, 1), (2, 3), (4, 5), (6, 7))
PROBS = 5
SLOTS = 8
EXTRA = 8


def host_constants():
    pos = np.concatenate([np.arange(SEQ), np.full(NB, PAST), np.zeros(P - NB)]).astype(np.float32)
    half = HD // 2
    inv = (np.float32(10000.0) ** (-np.arange(half, dtype=np.float32) / np.float32(half))).astype(np.float32)
    ang = pos[:, None] * inv[None, :]
    cos, sin = np.cos(ang), np.sin(ang)
    rope = np.concatenate([cos, cos, -sin, sin], 1).reshape(TILES, P, 2 * HD).transpose(1, 0, 2)
    p = np.arange(P)
    qpos = np.arange(SEQ).reshape(QT, P).T
    ends = 16 * np.arange(32) + 31
    ends[31] = 10 ** 6
    seen = ends[None, None, :] <= qpos[:, :, None]
    own = (p[:, None] // 8 == p[None, :] // 16) & (p[None, :] % 16 < 15)
    parts = {
        "ident": np.eye(P),
        "rope": rope.reshape(P, -1),
        "cneg": np.where(seen, 0.0, NEG).reshape(P, -1),
        "cone": seen.reshape(P, -1),
        "iota16": np.tile(np.arange(16), (P, 1)),
        "base16": np.tile(np.arange(16) * CAP, (P, 1)),
        "maskb": p[:, None] // 8 == np.arange(8)[None],
        "maskh": p[:, None] % 8 == np.arange(8)[None],
        "sneg": np.where(own, 0.0, NEG),
        "spread": p[:, None] == np.arange(64)[None] // 8,
        "eps": np.full((P, 1), EPS),
        "one": np.ones((P, 1)),
    }
    q, k = p[:, None], p[None, :]
    bparts = {
        "identb": np.eye(P),
        "before": np.where(k >= q, NEG, 0.0),
        "upto": np.where(k > q, NEG, 0.0),
        "earlier": q < k,
        "onesb": np.ones((P, P)),
    }
    return parts, bparts


def columns(parts):
    at, n = {}, 0
    for name, a in parts.items():
        at[name] = (n, n + a.shape[1])
        n += a.shape[1]
    return at, n



class Signals:

    def __init__(self, nc, ctx):
        self.nc, self.ctx, self.sem, self.total, self.marks = nc, ctx, {}, {}, {}

    def mark(self, name, key, by=1):
        if name not in self.sem:
            self.sem[name] = self.ctx.enter_context(self.nc.semaphore(name))
            self.total[name] = 0
        self.total[name] += by
        self.marks[name, key] = self.total[name]

    def wait(self, eng, name, key):
        eng.wait_ge(self.sem[name], self.marks[name, key])

    def __getitem__(self, name):
        return self.sem[name]


def build(nc, a, out):
    cf_at, cf_n = columns(host_constants()[0])
    cb_at, cb_n = columns(host_constants()[1])
    with ExitStack() as ctx:
        body(nc, ctx, a, out, cf_at, cf_n, cb_at, cb_n)


def body(nc, ctx, a, out, cf_at, cf_n, cb_at, cb_n):
    def sb(name, shape, dt=F32):
        return ctx.enter_context(nc.sbuf_tensor(name, shape, dt))

    bank = [ctx.enter_context(nc.psum_tensor(f"bank{n}", [P, 512], F32)) for n in range(8)]
    cf = sb("cf", [P, cf_n])
    cb = sb("cb", [P, cb_n], BF16)
    c = {k: cf[:, v[0]:v[1]] for k, v in cf_at.items()}
    c.update({k: cb[:, v[0]:v[1]] for k, v in cb_at.items()})
    ident = c["ident"]
    rope = c["rope"].rearrange("p (i n) -> p i n", i=TILES)
    gain = sb("gain", [P, D])
    gain_out = sb("gain_out", [P, D])
    x = sb("x", [P, TILES, D])
    qsbT = sb("qsbT", [P, 4, TOK])
    ksbT = sb("ksbT", [P, 4, TOK])
    qnsaT = sb("qnsaT", [P, REP, TOK])
    kselT = sb("kselT", [P, TOK])
    kwinT = sb("kwinT", [P, TOK])
    vsb = sb("vsb", [P, TILES, 512])
    vsel = sb("vsel", [P, TILES, P])
    vwin = sb("vwin", [P, TILES, P])
    gates = sb("gates", [P, TILES, 24])
    kcT = sb("kcT", [P, NCHUNK])
    vc = sb("vc", [P, 2, P])
    reg0 = sb("reg0", [P, 12288])
    reg1 = sb("reg1", [P, 12288])
    work = sb("work", [P, 7168])
    small = sb("small", [P, 32])
    smi = sb("smi", [P, 48], U32)
    pages = sb("pages", [1, NB * NPG], I32)
    wr = sb("wr", [P, KD, 20])
    br = sb("br", [P, 20])

    def view(region, at, shape):
        n = int(np.prod(shape))
        v = region[:, at:at + n]
        if len(shape) == 2:
            return v.rearrange("p (a b) -> p a b", a=shape[0])
        if len(shape) == 3:
            return v.rearrange("p (a b c) -> p a b c", a=shape[0], b=shape[1])
        return v

    win = view(reg0, 0, [2, KD, CHUNK])
    hT = view(reg1, 0, [KD, TOK])
    hn = view(reg1, 4160, [2, D])
    raw = view(reg1, 6208, [4, CHUNK])
    rot = view(reg1, 8256, [2, CHUNK])
    swp = view(reg1, 9280, [2, CHUNK])

    sg = Signals(nc, ctx)
    banks = {"m": [bank[0], bank[1], bank[2]], "t": [bank[3], bank[4]], "o": [bank[5], bank[6]], "x": [bank[7]]}
    uses = {r: [] for r in banks}
    index = {}

    def use(ring, key, free, signals=True):
        index[ring, key] = len(uses[ring])
        uses[ring].append((key, free))
        if signals:
            sg.mark(ring + "_full", key)
        sg.mark(ring + "_" + free, key)

    def at(ring, key):
        return banks[ring][index[ring, key] % len(banks[ring])]

    def acquire(eng, ring, key):
        n = index[ring, key] - len(banks[ring])
        if n >= 0:
            k, free = uses[ring][n]
            sg.wait(eng, ring + "_" + free, k)

    def freed_by(ring, key):
        return uses[ring][index[ring, key]][1]

    PLAN = []

    def step(kind, *key):
        PLAN.append((kind, key))

    turn = [0]

    def tstep(*key):
        turn[0] += 1
        eng = "act" if turn[0] % 2 else "dve"
        if key[0] in ("probT", "mixT", "h2T", "cT"):
            eng = "act"
        use("t", key, eng)
        step("T", *key)

    ORDER = (KV4, KV2, SBQ, NQ, SBK, SBV)
    proj = [(cc, i) for cc in ORDER for i in range(TILES)]
    pn = {key: n for n, key in enumerate(proj)}
    raws = [n for n, (cc, _) in enumerate(proj) if cc != SBV]
    rq = {n: q for q, n in enumerate(raws)}
    ropes = [n for n, (cc, _) in enumerate(proj) if cc >= NQ]
    ri = {n: q for q, n in enumerate(ropes)}
    blocks = {SBQ: 4, SBK: 4, SBV: 0, NQ: 4, KV4: 1, KV2: 1}

    order = [(kv, t) for kv in range(2) for t in range(2, CT)] + [(kv, t) for kv in range(2) for t in range(2)]

    def load_pair(q):
        if q < len(order):
            step("pair", q)
            sg.mark(f"pair{q % 4}", q, 32 if order[q][1] < 2 else 64)

    def pair_step(q):
        tstep("XT", q)
        load_pair(q + 4)

    def hid_step(kv):
        use("m", ("hidA", kv), "act")
        use("m", ("hidB", kv), "dve")
        sg.mark("hid_a", kv)
        sg.mark("gelu_in", kv)
        sg.mark("gelu_exp", kv)
        sg.mark("hid", kv)
        step("hid", kv)

    def comp_step(kv):
        use("m", ("comp", kv), "act")
        step("comp", kv)

    kt_order = [("sbk", j) for j in range(16)] + [(kind, g) for kind in ("selk", "wink") for g in range(4)]
    kt_index = {key: q for q, key in enumerate(kt_order)}
    loads = kt_order[0:18]
    for b in range(NB):
        loads += kt_order[18 + b:19 + b] + [("sbv", 2 * b), ("sbv", 2 * b + 1)]
    loads += [(kind, g) for kind in ("selv", "winv") for g in range(4)]
    lq = {key: q for q, key in enumerate(loads)}

    def load_page(q):
        if q < len(loads):
            step("page", q)
            sg.mark(f"page{q % SLOTS}", q, 64 if loads[q][0] in ("selk", "selv") else 16)

    def key_pages(s):
        tstep("KT", *kt_order[s])
        load_page(lq[kt_order[s]] + SLOTS)
        sg.mark("scored", kt_order[s])
        if kt_order[s] == ("selk", 0):
            use("x", ("zn",), "act", False)
        if kt_order[s] == ("sbk", 0):
            use("x", ("zsb",), "act", False)

    def value_pages(kind, g):
        step("pvn", kind, g)
        sg.mark("pvn", (kind, g))
        load_page(lq[kind, g] + SLOTS)

    def value_pages_sb(b):
        step("pvs", b)
        sg.mark("pvs", b)
        for pg in range(NPG):
            load_page(lq["sbv", 2 * b + pg] + SLOTS)

    def sample_small():
        for key in (("snew",), ("gsp",), ("cs",)):
            use("m", key, "dve")
        step("sample_small")
        sg.mark("s_max", 0)
        sg.mark("s_exp", 0)
        sg.mark("s_prob", 0)

    def sample_sb():
        step("front", "s")
        sg.mark("soft", "s")
        step("mid", "s")
        sg.mark("arg", "s")
        step("back", "s")
        sg.mark("p_ready", "s")

    def marked(kind, *sems):
        def go():
            step(kind)
            for name in sems:
                sg.mark(name, 0)
        return go

    side = {}

    def put(slot, f, *args):
        side.setdefault(slot, []).append((f, args))

    for q in range(16):
        put(FIRST_PAIR + q, pair_step, q)
    for v in range(2):
        put(FIRST_PAIR + 14 + v, tstep, "peT", v)
    for q in range(16, 20):
        put(FIRST_PAIR + 1 + q, pair_step, q)
    put(ZEROS_AT, step, "load_zeros")
    put(27, hid_step, 0)
    put(29, hid_step, 1)
    for q in range(SLOTS):
        put(29, load_page, q)
    put(31, comp_step, 0)
    put(33, comp_step, 1)
    put(35, marked("qbd", "qbd", "gates_exp", "gates"))
    for s in range(16):
        put(35 + s // 2, key_pages, s)
        put(36 + s // 2, step, "zs", *kt_order[s])
    put(44, step, "zt_sb")
    put(44, tstep, "zT")
    put(45, sample_sb)
    put(46, tstep, "aT")
    put(45, marked("qbn", "qbn"))
    for s in range(16, 24):
        put(29 + s, key_pages, s)
        put(30 + s, step, "zs", *kt_order[s])
    put(47, use, "o", ("sbs",), "dve", False)
    for b in range(NB):
        put(47 + b, value_pages_sb, b)
    put(54, step, "zt_nsa")
    put(54, tstep, "znT")
    put(55, sample_small)
    put(55, step, "ots")
    put(56, tstep, "osb4")
    put(57, tstep, "pT4")
    put(57, use, "o", ("nss",), "dve", False)
    for q, key in enumerate([(kind, g) for kind in ("selv", "winv") for g in range(4)]):
        put(57 + q // 3, value_pages, *key)
    put(60, step, "otn")
    put(60, tstep, "ons4")

    def load_w(pos):
        step("load_w", pos)
        sg.mark(f"w{pos % 2}", pos, 16)

    step("load_x", 0)
    load_w(0)
    step("load_x", 1)
    load_w(1)
    sg.mark("pages", 0, 16)
    sg.mark("cmp_small", 0, 64)
    sg.mark("w1_in", 0, 32)
    step("load_small")
    for q in range(4):
        load_pair(q)
    step("load_more")

    def norm(i):
        if i < TILES:
            step("norm", i)
            sg.mark(f"x{i}", i, 16)
            sg.mark("ssq", ("attn", i))
            sg.mark("rstd", ("attn", i))
            sg.mark("h", i)

    def transpose_h(i):
        if i < TILES:
            tstep("hT", i, 0)
            tstep("hT", i, 1)

    for i in range(2):
        norm(i)
        transpose_h(i)

    def finish(n):
        cc, i = proj[n]
        step("store", cc, i)
        if cc == SBK:
            sg.mark(f"st_raw{rq[n] % 4}", n, 16)
        if cc == SBV:
            sg.mark("st_v", n, 16)
        if cc == KV4:
            sg.mark(f"st_raw{rq[n] % 4}", n, 32)
            sg.mark(f"st_rot{ri[n] % 2}", n, 32)
        if cc == KV2:
            sg.mark(f"st_raw{rq[n] % 4}", n, 16)
            sg.mark(f"st_rot{ri[n] % 2}", n, 16)
        if blocks[cc]:
            tstep("pT", n)

    for n, (cc, i) in enumerate(proj):
        use("m", ("proj", n), "act")
        norm(n + 2)
        for half in range(2):
            step("proj", n, half)
            if half:
                transpose_h(n + 2)
            if half and i == TILES - 1 and n // TILES + 2 < NCH:
                load_w(n // TILES + 2)
            if half and cc >= NQ:
                step("rope", n)
                sg.mark("swapped", n)
                sg.mark("rotated", n)
            for f, args in side.pop(2 * n + half, ()):
                f(*args)
            if not half and n >= 2:
                finish(n - 2)
    finish(len(proj) - 2)
    finish(len(proj) - 1)
    for slot in sorted(side):
        for f, args in side[slot]:
            f(*args)

    w1 = [view(reg0, 8192, [16, P]), view(reg0, 10240, [16, P])]
    xt = [work[:, 0:2576], work[:, 2576:5152]]
    pair = view(work, 5152, [4, 2 * P])
    pe_in = view(work, 6176, [2, P])
    w2 = view(work, 6432, [2, HD])
    hid_a = [xt[v][:, 0:322] for v in range(2)]
    hid = [xt[v][:, 322:642] for v in range(2)]
    hid_u = [xt[v][:, 642:962] for v in range(2)]
    page = view(reg0, 8192, [SLOTS, 4, P])
    pageT = view(work, 0, [3, 4, P])
    zt = work[:, 1536:1792]
    sz = view(work, 1792, [2, 264])
    s_z, s_soft, s_prob = (work[:, 2320 + 256 * q:2576 + 256 * q] for q in range(3))
    s_cprob = work[:, 3344:3472]
    s_probT = reg1[:, 11056:11184]
    pt4 = reg1[:, 10304:10304 + 448]
    ot = view(reg1, 10752, [4, NB])
    smp = reg1[:, 10784:11056]
    qbd = smp[:, 0:64].rearrange("p (j b t) -> p j b t", j=4, b=NB)
    qbn = smp[:, 64:128].rearrange("p (b h) -> p b h", b=NB)
    snew = smp[:, 128:144].rearrange("p (t b) -> p t b", t=2)
    gsp = smp[:, 144:168].rearrange("p (t h) -> p t h", t=3)
    gw = smp[:, 168:171]
    pm = smp[:, 176:192].rearrange("p (t b) -> p t b", t=2)
    soft = view(work, 0, [2, 512])
    prob = view(work, 1024, [PROBS, 512])
    probT = view(work, 3584, [3, 512])
    o_sb = work[:, 5120:5632]
    o_nsa = work[:, 5632:6144]
    o_part = work[:, 6144:6656]
    cprob = work[:, 6656:6912]
    cprobT = work[:, 6912:7168]
    w_out = view(reg1, 0, [KD, D])
    mix = reg1[:, 8192:9216]
    mixT = view(reg1, 9216, [KD, P])
    h2 = reg1[:, 10240:11264]
    rt = sb("rt", [P, 256])
    weight = sb("weight", [P, TILES, 2])
    onehot = sb("onehot", [P, TILES, NE], BF16)
    slots = sb("slots", [P, TILES, 2], U32)
    token = sb("token", [P, TILES])
    chosen = sb("chosen", [P, TILES, 2, NE])
    expert = sb("expert", [P, TILES, 2])
    slot_f = sb("slot_f", [P, TILES, 2])
    y_slots = sb("y_slots", [P, TILES, 2], U32)
    st = sb("st", [P, 96])
    h2_dram = nc.dram_tensor("h2_rows", [TOK, D], F32, kind="Internal").ap()
    y_dram = nc.dram_tensor("expert_rows", [(NE + EXTRA) * P, D], F32, kind="Internal").ap()
    table = nc.dram_tensor("slot_tokens", [NE * CAP, 1], F32, kind="Internal").ap()

    def load_output():
        sg.mark("w_out", 0, 16)
        step("load_wout")
        step("win_state")
        sg.mark("st_state", 0, 32)
        sg.mark("gain_in", "out", 32)
        sg.mark("gain_in", "ffn", 16)

    tile_order = [QT] + list(range(QT))

    def nothing():
        pass

    def output_steps(i):
        def mix_sums():
            step("mix_ssq", i)
            sg.mark("ssq", ("mix", i))

        def mix_scales():
            step("mix_rstd", i)
            sg.mark("rstd", ("mix", i))

        def mix_rows():
            step("mix", i)
            sg.mark("mix", i)

        def transpose_mix():
            for half in range(2):
                tstep("mixT", i, half)

        def product(half, part):
            def go():
                if part == 0:
                    use("x", ("wout", i, half), "dve")
                step("wout", i, half, part)
            return go

        def ffn_sums():
            step("ffn_ssq", i)
            sg.mark("ssq", ("ffn", i))

        def ffn_scales():
            step("ffn_rstd", i)
            sg.mark("rstd", ("ffn", i))

        def ffn_rows():
            step("h2", i)
            sg.mark("h2", i)
            sg.mark("st_h2", i, 16)

        def transpose_ffn():
            for half in range(2):
                tstep("h2T", i, half)

        def route_group():
            use("x", ("logit", i), "dve")
            step("route", i)
            sg.mark("r_max", (i, 0))
            sg.mark("r_exp", (i, 0))

        def route_experts():
            step("route_experts", i)
            sg.mark("r_max", (i, 1))
            sg.mark("r_exp", (i, 1))

        def route_choice():
            step("route_choice", i)
            sg.mark("onehot", i)

        def rank():
            use("x", ("rank", i), "dve")
            step("rank", i)
            sg.mark("slots", i)
            sg.mark("scatter", i, 32)
        return ([mix_sums, mix_scales, mix_rows, transpose_mix] + [product(half, part) for half in range(2) for part in range(len(WOUT_PARTS))]
                + [ffn_sums, ffn_scales, ffn_rows, transpose_ffn, route_group, route_experts, route_choice, rank])

    SB, SEL, WIN = range(3)
    AT_T, AT_PV = 2, 3
    steps = [(i, b, h) for i in range(QT) for b in range(3) for h in range(HEADS)]
    load_output()
    pending = [nothing] * OUTPUT_AFTER + output_steps(QT)
    for t in range(len(steps) + AT_PV + 1):
        if t < len(steps):
            i, b, h = s = steps[t]
            tile_slot = b * HEADS + h
            if tile_slot == 2:
                use("x", ("cmp", i), "dve")
                step("cmp_score", i)
                sg.mark("c_max", i)
                sg.mark("c_exp", i)
            if tile_slot == 3:
                step("cmp_norm", i)
                sg.mark("c_prob", i)
            if tile_slot == 5:
                tstep("cT", i)
                use("o", (i, "cmp"), "dve", False)
                step("cmp_pv", i)
                sg.mark("o_done", (i, "cmp"))
            use("m", s, "dve" if b == SB else "act")
            step("score", *s)
            if b == SB:
                step("front", *s)
                sg.mark("soft", s)
            step("mid", *s)
            if b != SB:
                sg.mark("arg", s)
        if 1 <= t <= len(steps):
            step("back", *steps[t - 1])
            if steps[t - 1][1] == SB:
                sg.mark("p_ready", steps[t - 1])
        if 0 <= t - AT_T < len(steps):
            tstep("probT", *steps[t - AT_T])
        if 0 <= t - AT_PV < len(steps):
            i, b, h = s = steps[t - AT_PV]
            if h == 0:
                use("o", (i, b), "dve", False)
            step("pv", *s)
            sg.mark("pv", s)
            if h == HEADS - 1:
                step("branch", i, b)
                if b != SB:
                    sg.mark("branch", (i, b))
                if b == WIN:
                    while pending:
                        pending.pop(0)()
                    pending = output_steps(i)
        if pending:
            pending.pop(0)()
    while pending:
        pending.pop(0)()
    order_of = {s: n for n, s in enumerate(steps)}
    sb_order = [s for s in steps if s[1] == SB]
    sb_index = {s: n for n, s in enumerate(sb_order)}
    for name, by in (("const", 16), ("const_b", 16), ("gain_attn", 16), ("table_zero", 16), ("y_zero", 16 * EXTRA), ("router_in", 64),
                     ("iota", 1), ("zero", 1), ("act_chain", 0), ("dve_chain", 0), ("pe_chain", 0)):
        sg.mark(name, 0, by)

    def sb_views(key):
        if key == ("s",):
            return 64, 2 * P, s_z[0:64], s_soft[0:64], s_prob[0:64]
        i, b, h = key
        n, q = (i + 1) * P, sb_index[key]
        return P, n, at("m", key)[:, 0:n], soft[:, q % 2, 0:n], prob[:, order_of[key] % PROBS, 0:n]

    def wait_arg(eng, key):
        sg.wait(eng, "arg" if key == "s" else "m_dve", key)

    def key_of(key):
        return "s" if key == ("s",) else key

    def before_prob_write(eng, key):
        n = order_of.get(key, 0)
        if n >= PROBS:
            sg.wait(eng, "t_full", ("probT",) + steps[n - PROBS])

    def sample_done(eng):
        sg.wait(eng, "t_full", ("pT4",))

    def gate_rows(i):
        return gates[0:ROWS[i], i, :].rearrange("p (h t) -> p t h", t=3)

    def more_transposes(key, b):
        kind = key[0]
        if kind == "peT":
            v = key[1]
            return [(b[:, 0:16], pe_in[0:16, v, :])], [(xt[v][:, 2560:2576], b[:, 0:16], 1.0)]
        if kind == "XT":
            q, = key[1:]
            kv, t = order[q]
            dst = xt[kv][:, 0:2560].rearrange("p (g n) -> p g n", g=GROUPS)[:, :, t * P:(t + 1) * P]
            b2 = b[:, 0:256].rearrange("p (g n) -> p g n", g=GROUPS)
            return [(b2[:, g, :], pair[:, q % 4, g * P:(g + 1) * P]) for g in range(GROUPS)], [(dst, b2, 1.0)]
        if kind == "KT":
            q = lq[key[1:]]
            n = kt_index[key[1:]]
            b4 = b[:, :].rearrange("p (s t) -> p s t", s=4)
            return [(b4[:, s, :], page[:, q % SLOTS, s, :]) for s in range(4)], [(pageT[:, n % 3], b4, 1.0)]
        if kind == "zT":
            return ([(b[0:64, pg * P:(pg + 1) * P], zt[:, pg * 64:(pg + 1) * 64]) for pg in range(NPG)],
                    [(s_z[0:64], b[0:64, 0:256], 1.0)])
        if kind == "znT":
            b2 = b[0:64, :].rearrange("p (r n) -> p r n", r=2)
            return ([(b[0:64, s * P:(s + 1) * P], zt[:, s * 64:(s + 1) * 64]) for s in range(4)],
                    [(sz[0:64, :, 0:256], b2, 1.0)])
        if kind == "aT":
            return ([(b[:, pg * 64:(pg + 1) * 64], s_prob[0:64, pg * P:(pg + 1) * P]) for pg in range(NPG)],
                    [(s_probT, b[:, 0:128], 1.0)])
        if kind == "osb4":
            return ([(b[0:NB, j * P:(j + 1) * P], ot[:, j, :]) for j in range(4)], [(o_sb[0:NB, :], b[0:NB, :], 1.0)])
        if kind == "pT4":
            moves = [(b[:, (2 * s + pg) * 64:(2 * s + pg + 1) * 64], sz[0:64, s, pg * P:(pg + 1) * P])
                     for s in range(2) for pg in range(2)]
            moves += [(b[:, 256:320], s_cprob[0:64])]
            moves += [(b[0:NB, 320 + 64 * s:384 + 64 * s], pm[0:64, s, :]) for s in range(2)]
            return moves, [(pt4[:, 0:320], b[:, 0:320], 1.0), (pt4[0:NB, 320:448], b[0:NB, 320:448], 1.0)]
        if kind == "ons4":
            dst = o_nsa[0:NB, :].rearrange("p (g r d) -> p g r d", g=GROUPS, r=REP)
            return ([(b[0:NB, j * P:(j + 1) * P], ot[:, j, :]) for j in range(4)],
                    [(dst, b[0:NB, :].rearrange("p (r g d) -> p g r d", g=GROUPS, r=REP), 1.0)])
        if kind in ("mixT", "h2T"):
            i, half = key[1:]
            r = ROWS[i]
            src = mix if kind == "mixT" else h2
            b4 = b[:, 0:4 * r].rearrange("p (k t) -> p k t", k=4)
            moves = [(b4[:, k, :], src[0:r, (4 * half + k) * P:(4 * half + k + 1) * P]) for k in range(4)]
            return moves, [(mixT[:, 4 * half:4 * half + 4, 0:r], b4, 1.0)]
        if kind == "cT":
            return ([(b[:, g * P:(g + 1) * P], cprob[:, g * P:(g + 1) * P]) for g in range(GROUPS)],
                    [(cprobT, b[:, 0:256], 1.0)])
        if kind == "probT":
            s = key[1:]
            n, q = s[0] + 1, order_of[s]
            return ([(b[:, k * P:(k + 1) * P], prob[:, q % PROBS, k * P:(k + 1) * P]) for k in range(n)],
                    [(probT[:, q % 3, 0:n * P], b[:, 0:n * P], 1.0)])
        raise KeyError(key)

    def before_transpose(pe, key):
        kind = key[0]
        if kind == "peT":
            pe.wait_ge(sg["cmp_small"], 64)
        elif kind == "XT":
            sg.wait(pe, f"pair{key[1] % 4}", key[1])
        elif kind == "KT":
            sg.wait(pe, f"page{lq[key[1:]] % SLOTS}", lq[key[1:]])
        elif kind == "zT":
            sg.wait(pe, "x_act", ("zsb",))
        elif kind == "znT":
            sg.wait(pe, "x_act", ("zn",))
        elif kind == "aT":
            sg.wait(pe, "p_ready", "s")
        elif kind == "osb4":
            sg.wait(pe, "o_dve", ("sbs",))
        elif kind == "pT4":
            sg.wait(pe, "s_prob", 0)
        elif kind == "ons4":
            sg.wait(pe, "o_dve", ("nss",))
        elif kind == "mixT":
            sg.wait(pe, "mix", key[1])
        elif kind == "h2T":
            sg.wait(pe, "h2", key[1])
        elif kind == "cT":
            sg.wait(pe, "c_prob", key[1])
        elif kind == "probT":
            if key[2] == SB:
                sg.wait(pe, "p_ready", key[1:])
            else:
                sg.wait(pe, "m_act", key[1:])

    def before_copy(eng, key):
        kind = key[0]
        if kind == "KT" and kt_index[key[1:]] >= 3:
            sg.wait(eng, "scored", kt_order[kt_index[key[1:]] - 3])
        elif kind == "KT":
            sg.wait(eng, "m_full", ("comp", 1))
        elif kind == "probT" and order_of[key[1:]] >= 3:
            sg.wait(eng, "pv", steps[order_of[key[1:]] - 3])
        elif kind == "h2T":
            sg.wait(eng, "x_full", ("wout", key[1], 1))
        elif kind == "mixT" and key[1] != QT:
            sg.wait(eng, "x_full", ("logit", tile_order[tile_order.index(key[1]) - 1]))
        elif kind == "cT" and key[1] > 0:
            sg.wait(eng, "o_done", (key[1] - 1, "cmp"))

    page_reg = []

    def load_small(sp):
        sp.dma_start(pages[:, :], a["page_table"].rearrange("(o b) n -> o (b n)", o=1)).then_inc(sg["pages"], 16)
        for kv, n in enumerate("kv"):
            sp.dma_start(pe_in[0:16, kv, :], a[f"cmp_pe_{n}"][0].rearrange("(q l) d -> q (l d)", l=2)
                         ).then_inc(sg["cmp_small"], 16)
            sp.dma_start(w2[:, kv, :], a[f"cmp_{n}_w2"][0]).then_inc(sg["cmp_small"], 16)
        sp.wait_ge(sg["pages"], 16)
        for j in range(NB * NPG):
            page_reg.append(sp.value_load(pages[0:1, j:j + 1], min_val=0, max_val=19))

    def load_more(sp):
        for kv, n in enumerate("kv"):
            sp.dma_start(w1[kv], a[f"cmp_{n}_w1"][0].rearrange("(t p) h -> p t h", p=P)).then_inc(sg["w1_in"], 16)
        sp.dma_start(cb[:, :], a["const_b"]).then_inc(sg["const_b"], 16)
        for k, n in (("router_group_w", 0), ("router_expert_w", 4)):
            src = a[k][0] if n == 0 else a[k][0].rearrange("d g e -> d (g e)")
            sp.dma_start(wr[:, :, n:n + src.shape[1]], src.rearrange("(k p) e -> p k e", p=P)
                         ).then_inc(sg["router_in"], 16)
        sp.dma_start(br[:, 0:4], a["router_group_b"][0:1].partition_broadcast(P).rearrange("p o g -> p (o g)")
                     ).then_inc(sg["router_in"], 16)
        sp.dma_start(br[:, 4:20], a["router_expert_b"][0:1].partition_broadcast(P).rearrange("p o g e -> p (o g e)")
                     ).then_inc(sg["router_in"], 16)

    def load_zeros(sp):
        sp.wait_ge(sg["zero"], 1)
        sp.dma_start(table.rearrange("(p n) o -> p (n o)", p=P), rt[:, 0:80]).then_inc(sg["table_zero"], 16)
        for v in range(EXTRA):
            sp.dma_start(y_dram[(NE + v) * P:(NE + v + 1) * P, :], vsb[:, 0:2, :].rearrange("p a b -> p (a b)")
                         ).then_inc(sg["y_zero"], 16)

    def pool_page(name, j):
        return a[name][0, bass.ds(page_reg[j], 1)].rearrange("o t h d -> (o t) (h d)")

    def sync_more(sp, kind, key):
        if kind == "load_small":
            load_small(sp)
        elif kind == "load_more":
            load_more(sp)
        elif kind == "load_zeros":
            load_zeros(sp)
        elif kind == "pair":
            q, = key
            kv, t = order[q]
            if q >= 4:
                sg.wait(sp, "t_full", ("XT", q - 4))
            dst = pair[:, q % 4, :].rearrange("p (g l d) -> p l g d", g=GROUPS, l=2)
            name = "cmp_" + "kv"[kv]
            if t < 2:
                if (kv, t) == (0, 0):
                    for i in range(QT):
                        n = pn[KV4, i]
                        sg.wait(sp, f"st_raw{rq[n] % 4}", n)
                        sg.wait(sp, f"st_rot{ri[n] % 2}", n)
                src = out[name + "_p"][0, 0, t * 2 * P:(t + 1) * 2 * P].rearrange("(p l) g d -> p l g d", l=2)
                for l in range(2):
                    sp.dma_start(dst[:, l], src[:, l]).then_inc(sg[f"pair{q % 4}"], 16)
            else:
                for pg in range(NPG):
                    src = a["cache_" + name][0, bass.ds(page_reg[2 * (t - 2) + pg], 1)].rearrange(
                        "o (p l) g d -> (o p) l g d", l=2)
                    for l in range(2):
                        sp.dma_start(dst[64 * pg:64 * pg + 64, l], src[:, l]).then_inc(sg[f"pair{q % 4}"], 16)
        elif kind == "page":
            q, = key
            what, g = loads[q]
            if q == 0:
                sg.wait(sp, "m_full", ("hidB", 1))
            if q >= SLOTS:
                w, k = loads[q - SLOTS]
                if w in ("sbk", "selk", "wink"):
                    sg.wait(sp, "t_full", ("KT", w, k))
                elif w == "sbv":
                    sg.wait(sp, "pvs", k // 2)
                else:
                    sg.wait(sp, "pvn", (w, k))
            sem = sg[f"page{q % SLOTS}"]
            if what in ("sbk", "sbv"):
                sp.dma_start(page[:, q % SLOTS].rearrange("p s t -> p (s t)"), pool_page("cache_sb_" + what[2], g)
                             ).then_inc(sem, 16)
            elif what in ("selk", "selv"):
                for s in range(4):
                    sp.dma_start(page[:, q % SLOTS, s, :], pool_page("cache_sel_" + what[3], 4 * g + s)).then_inc(sem, 16)
            else:
                src = a["state_win_" + what[3]][0, 2 * g:2 * g + 2].rearrange("b (q t) g d -> t (b q) (g d)", q=NPG)
                sp.dma_start(page[:, q % SLOTS], src).then_inc(sem, 16)
        elif kind == "load_wout":
            sg.wait(sp, "m_full", ("proj", NCH * TILES - 1))
            sg.wait(sp, "t_full", ("pT", pn[SBK, QT]))
            sg.wait(sp, "rotated", pn[NQ, QT])
            for s in range(4):
                sp.wait_ge(sg[f"st_raw{s}"], sg.total[f"st_raw{s}"])
            sp.dma_start(w_out, a["w_out"][0].rearrange("(k p) n -> p k n", p=P)).then_inc(sg["w_out"], 16)
            sp.dma_start(gain_out[:, 0:512], a["norm_sb_out"][0:1].partition_broadcast(P).rearrange("p o d -> p (o d)")
                         ).then_inc(sg["gain_in"], 16)
            sp.dma_start(gain_out[:, 512:D], a["norm_nsa_out"][0:1].partition_broadcast(P).rearrange("p o d -> p (o d)")
                         ).then_inc(sg["gain_in"], 16)
            sg.wait(sp, "h", TILES - 1)
            sp.dma_start(gain[:, :], a["norm_ffn"][0:1].partition_broadcast(P).rearrange("p o d -> p (o d)")
                         ).then_inc(sg["gain_in"], 16)
        elif kind == "win_state":
            for n in "kv":
                sp.dma_start(out[f"win_{n}_s"][0, :, 0:PAST - 1].rearrange("b t g d -> b (t g d)"),
                             a[f"state_win_{n}"][0, :, 1:PAST].rearrange("b t g d -> b (t g d)")
                             ).then_inc(sg["st_state"], 16)
        elif kind == "h2":
            i, = key
            sg.wait(sp, "h2", i)
            sp.dma_start(h2_dram[i * P:i * P + ROWS[i], :], h2[0:ROWS[i], :]).then_inc(sg["st_h2"], 16)
        else:
            expert_sync(sp, kind, key)

    def gps_begin(pool):
        nc.gpsimd.iota(token[:, :], [[P, TILES]], base=0, channel_multiplier=1,
                       allow_small_or_imprecise_dtypes=True).then_inc(sg["iota"], 1)

    def gps_more(pool, kind, key):
        if kind == "rank":
            i, = key
            sg.wait(pool, "slots", i)
            if i == QT:
                pool.wait_ge(sg["iota"], 1)
                pool.wait_ge(sg["table_zero"], 16)
            for k in range(2):
                nc.gpsimd.indirect_dma_start(
                    table, bass.IndirectOffsetOnAxis(ap=slots[0:ROWS[i], i, k:k + 1], axis=0),
                    token[0:ROWS[i], i:i + 1], None).then_inc(sg["scatter"], 16)
        else:
            expert_gps(pool, kind, key)

    def act_more(act, link, inverse_rms, kind, key):
        if kind == "hid":
            kv, = key
            sg.wait(act, "m_full", ("hidB", kv))
            nc.scalar.copy(hid_a[kv], at("m", ("hidA", kv))[:, 0:322]).then_inc(sg["m_act"], 1)
            sg.wait(act, "gelu_in", kv)
            nc.scalar.activation(hid_u[kv], hid_u[kv], ACT.Exp, scale=-1.5957691216057308).then_inc(sg["gelu_exp"], 1)
        elif kind == "comp":
            kv, = key
            sg.wait(act, "m_full", ("comp", kv))
            b = at("m", ("comp", kv))
            dst, src = (kcT[:, :], b[:, 0:NCHUNK]) if kv == 0 else (vc[:, :, :], b[:, 0:256].rearrange(
                "p (a n) -> p a n", a=2))
            nc.scalar.copy(dst, src).then_inc(sg["m_act"], 1)
        elif kind == "qbd":
            sg.wait(act, "swapped", pn[KV2, QT])
            nc.scalar.activation(gates[:, 0:QT, :], gates[:, 0:QT, :], ACT.Exp, scale=-1.0)
            nc.scalar.activation(gates[0:NB, QT, :], gates[0:NB, QT, :], ACT.Exp, scale=-1.0
                                 ).then_inc(sg["gates_exp"], 1)
        elif kind in ("zt_sb", "zt_nsa"):
            u, n = (("zsb",), 128) if kind == "zt_sb" else (("zn",), 256)
            sg.wait(act, "scored", ("sbk", 15) if kind == "zt_sb" else ("wink", 3))
            if kind == "zt_nsa":
                sg.wait(act, "t_full", ("zT",))
            nc.scalar.copy(zt[:, 0:n], bank[7][:, 0:n]).then_inc(sg["x_act"], 1)
        elif kind == "front":
            _, _, z, so, _ = sb_views(key)
            if key == ("s",):
                wait_transposed(act, ("zT",))
            else:
                sg.wait(act, "m_full", key)
                q = sb_index[key]
                if q == 0:
                    sample_done(act)
                if q >= 2:
                    wait_arg(act, sb_order[q - 2])
            link(nc.scalar.activation(so, z, ACT.Abs))
            link(nc.scalar.activation(so, so, ACT.Exp, scale=-1.0))
            nc.scalar.activation(so, so, ACT.Ln, bias=1.0).then_inc(sg["soft"], 1)
        elif kind == "back":
            if key == ("s",) or key[1] == SB:
                _, _, _, _, p = sb_views(key)
                wait_arg(act, key_of(key))
                nc.scalar.activation(p, p, ACT.Exp).then_inc(sg["p_ready"], 1)
            else:
                i, b, h = key
                q = order_of[key]
                sg.wait(act, "arg", key)
                before_prob_write(act, key)
                if h == 0 and i > 0:
                    sg.wait(act, "branch", (i - 1, b))
                nc.scalar.activation(prob[:, q % PROBS, 0:(i + 1) * P], at("m", key)[:, 0:(i + 1) * P], ACT.Exp,
                                     bias=st[:, 32 + q % 4:33 + q % 4],
                                     accum_out=st[:, (b - 1) * 8 + h:(b - 1) * 8 + h + 1]).then_inc(sg["m_act"], 1)
        elif kind == "sample_small":
            sg.wait(act, "s_max", 0)
            for s in range(2):
                nc.scalar.activation(sz[0:64, s, 0:257], sz[0:64, s, 0:257], ACT.Exp, bias=st[0:64, 48 + s:49 + s],
                                     accum_out=st[0:64, 52 + s:53 + s])
            nc.scalar.activation(s_cprob[0:64], s_cprob[0:64], ACT.Exp, bias=st[0:64, 50:51],
                                 accum_out=st[0:64, 54:55]).then_inc(sg["s_exp"], 1)
        elif kind == "cmp_score":
            i, = key
            sg.wait(act, "c_max", i)
            nc.scalar.activation(cprob, cprob, ACT.Exp).then_inc(sg["c_exp"], 1)
        elif kind == "mix_rstd":
            i, = key
            inverse_rms(small[0:ROWS[i], 8:10], 512, "rstd", ("mix", i))
        elif kind == "ffn_rstd":
            i, = key
            inverse_rms(small[0:ROWS[i], 10:11], D, "rstd", ("ffn", i))
        elif kind == "route":
            i, = key
            r = ROWS[i]
            sg.wait(act, "r_max", (i, 0))
            nc.scalar.activation(rt[0:r, 64:68], rt[0:r, 0:4], ACT.Exp, bias=rt[0:r, 70:71],
                                 accum_out=rt[0:r, 71:72]).then_inc(sg["r_exp"], 1)
        elif kind == "route_experts":
            i, = key
            r = ROWS[i]
            sg.wait(act, "r_max", (i, 1))
            nc.scalar.activation(rt[0:r, 73:74], rt[0:r, 72:73], ACT.Exp).then_inc(sg["r_exp"], 1)
        else:
            expert_act(act, link, inverse_rms, kind, key)

    def dve_begin(dve, link):
        nc.vector.memset(chosen[:, :, :, :], 0.0)
        nc.vector.memset(expert[:, :, :], 0.0)
        nc.vector.memset(slot_f[:, :, :], 0.0)
        nc.vector.memset(vsb[:, 0:2, :], 0.0)
        nc.vector.memset(rt[:, :], 0.0).then_inc(sg["zero"], 1)

    def route_experts(link, r, ex, n8, el, prod):
        V = nc.vector
        link(V.tensor_tensor(prod, ex.rearrange("p (g e) -> p e g", g=4),
                             rt[0:r, 76:80].unsqueeze(1).to_broadcast([r, 4, 4]), ALU.mult))
        link(V.tensor_reduce(el[:, 0:4], prod, AX.X, ALU.add))
        link(V.max(n8, el))
        V.tensor_tensor(rt[0:r, 72:73], n8[:, 1:2], n8[:, 0:1], ALU.subtract).then_inc(sg["r_max"], 1)

    def route_choice(dve, link, i, r, n8, el):
        V = nc.vector
        link(V.max_index(smi[0:r, 8:16], n8, el))
        V.tensor_scalar(rt[0:r, 75:76], rt[0:r, 74:75], 4.0, None, ALU.mult)
        link(V.tensor_copy(rt[0:r, 80:82], smi[0:r, 8:10]))
        link(V.tensor_scalar(rt[0:r, 80:82], rt[0:r, 80:82], rt[0:r, 75:76], None, ALU.add))
        V.tensor_copy(expert[0:r, i, :], rt[0:r, 80:82])
        for k in range(2):
            ins = V.tensor_scalar(chosen[0:r, i, k], c["iota16"][0:r], rt[0:r, 80 + k:81 + k],
                                  None, ALU.is_equal)
        link(ins)
        V.tensor_tensor(onehot[0:r, i, :], chosen[0:r, i, 0], chosen[0:r, i, 1], ALU.add
                        ).then_inc(sg["onehot"], 1)
        sg.wait(dve, "r_exp", (i, 1))
        V.tensor_scalar(rt[0:r, 83:84], rt[0:r, 73:74], 1.0, None, ALU.add)
        link(V.tensor_copy(rt[0:r, 82:83], rt[0:r, 71:72]))
        link(V.reciprocal(rt[0:r, 82:84], rt[0:r, 82:84]))
        link(V.tensor_tensor(weight[0:r, i, 0:1], rt[0:r, 82:83], rt[0:r, 83:84], ALU.mult))
        link(V.tensor_tensor(weight[0:r, i, 1:2], weight[0:r, i, 0:1], rt[0:r, 73:74], ALU.mult))

    def dve_more(dve, link, kind, key):
        V = nc.vector
        if kind == "hid":
            kv, = key
            b = at("m", ("hidB", kv))
            v, u = hid[kv], hid_u[kv]
            sg.wait(dve, "m_full", ("hidB", kv))
            sg.wait(dve, "m_act", ("hidA", kv))
            link(V.tensor_tensor(smp[:, 200 + kv:201 + kv], hid_a[kv][:, 320:321], b[:, 321:322], ALU.add))
            V.scalar_tensor_tensor(v, b[:, 1:321], smp[:, 200 + kv:201 + kv], hid_a[kv][:, 0:320], ALU.add, ALU.add
                                   ).then_inc(sg["m_dve"], 1)
            sg.wait(dve, "m_dve", ("hidB", kv))
            link(V.tensor_tensor(u, v, v, ALU.mult))
            link(V.tensor_scalar(u, u, 0.044715, 1.0, ALU.mult, ALU.add))
            V.tensor_tensor(u, u, v, ALU.mult).then_inc(sg["gelu_in"], 1)
            sg.wait(dve, "gelu_exp", kv)
            link(V.tensor_scalar(u, u, 1.0, None, ALU.add))
            link(V.reciprocal(u, u))
            V.tensor_tensor(v, v, u, ALU.mult).then_inc(sg["hid"], 1)
        elif kind == "qbd":
            link(V.memset(smp[:, 0:128], 0.0))
            wait_transposed(dve, ("pT", pn[SBQ, QT]))
            for e in range(2):
                rows = slice(64 * e, 64 * e + 64)
                ins = V.tensor_copy(qbd[rows, :, :, e], qsbT[rows, :, SEQ:TOK])
            ins.then_inc(sg["qbd"], 1)
            sg.wait(dve, "gates_exp", 0)
            for r, g in ((P, gates[:, 0:QT, :]), (NB, gates[0:NB, QT:TILES, :])):
                link(V.tensor_scalar(g, g, 1.0, None, ALU.add))
                ins = V.reciprocal(g, g)
            ins.then_inc(sg["gates"], 1)
        elif kind == "qbn":
            wait_transposed(dve, ("pT", pn[NQ, QT]))
            for e in range(2):
                rows = slice(64 * e, 64 * e + 64)
                ins = V.tensor_copy(qbn[rows, :, REP * e:REP * e + REP].rearrange("p b h -> p h b"),
                                    qnsaT[rows, :, SEQ:TOK])
            ins.then_inc(sg["qbn"], 1)
        elif kind == "mid":
            if key == ("s",) or key[1] == SB:
                r, n, z, so, p = sb_views(key)
                sg.wait(dve, "soft", key_of(key))
                link(V.scalar_tensor_tensor(so, z, 0.0, so, ALU.max, ALU.add))
                if key != ("s",):
                    before_prob_write(dve, key)
                link(V.tensor_tensor_scan(p[:, ::-1], c["one"][0:r].to_broadcast([r, n]), so[:, ::-1], 0.0,
                                          ALU.mult, ALU.add))
                ins = V.tensor_tensor(p, z, p, ALU.subtract)
                if key == ("s",):
                    ins.then_inc(sg["arg"], 1)
                else:
                    ins.then_inc(sg["m_dve"], 1)
            else:
                i, b, h = key
                q = order_of[key]
                sg.wait(dve, "m_full", key)
                if q >= 4 and steps[q - 4][1] != SB:
                    sg.wait(dve, "m_act", steps[q - 4])
                V.tensor_reduce(st[:, 32 + q % 4:33 + q % 4], at("m", key)[:, 0:(i + 1) * P], AX.X, ALU.max,
                                negate=True).then_inc(sg["arg"], 1)
        elif kind == "sample_small":
            sg.wait(dve, "m_full", ("snew",))
            b = at("m", ("snew",))[0:64, 0:16].rearrange("p (t b) -> p t b", t=2)
            V.tensor_tensor(snew[0:64], b, c["maskb"][0:64].unsqueeze(1).to_broadcast([64, 2, NB]), ALU.mult
                            ).then_inc(sg["m_dve"], 1)
            sg.wait(dve, "m_full", ("gsp",))
            b = at("m", ("gsp",))[0:64, 0:24].rearrange("p (h t) -> p t h", t=3)
            V.tensor_tensor(gsp[0:64], b, c["maskh"][0:64].unsqueeze(1).to_broadcast([64, 3, 8]), ALU.mult
                            ).then_inc(sg["m_dve"], 1)
            sg.wait(dve, "m_full", ("cs",))
            V.tensor_tensor(s_cprob[0:64], at("m", ("cs",))[0:64, 0:128], c["sneg"][0:64], ALU.add
                            ).then_inc(sg["m_dve"], 1)
            sg.wait(dve, "m_dve", ("cs",))
            wait_transposed(dve, ("znT",))
            link(V.tensor_reduce(sz[0:64, :, 256:257].rearrange("p t o -> p (t o)"), snew[0:64], AX.X, ALU.add))
            V.tensor_reduce(gw[0:64], gsp[0:64], AX.X, ALU.add)
            V.tensor_reduce(st[0:64, 50:51], s_cprob[0:64], AX.X, ALU.max, negate=True)
            V.tensor_reduce(st[0:64, 48:50], sz[0:64, :, 0:257], AX.X, ALU.max, negate=True).then_inc(sg["s_max"], 1)
            sg.wait(dve, "s_exp", 0)
            link(V.reciprocal(st[0:64, 52:55], st[0:64, 52:55]))
            V.tensor_tensor(st[0:64, 56:58], st[0:64, 52:54], gw[0:64, 1:3], ALU.mult)
            link(V.tensor_tensor(st[0:64, 58:59], st[0:64, 54:55], gw[0:64, 0:1], ALU.mult))
            for s in range(2):
                link(V.tensor_scalar(sz[0:64, s, 0:257], sz[0:64, s, 0:257], st[0:64, 56 + s:57 + s], None, ALU.mult))
                V.tensor_scalar(pm[0:64, s, :], c["maskb"][0:64], sz[0:64, s, 256:257], None, ALU.mult)
            V.tensor_scalar(s_cprob[0:64], s_cprob[0:64], st[0:64, 58:59], None, ALU.mult
                            ).then_inc(sg["s_prob"], 1)
        elif kind == "ots":
            sg.wait(dve, "pvs", NB - 1)
            b = at("o", ("sbs",))[:, 0:64].rearrange("p (j b t) -> p j b t", j=4, b=NB)
            V.tensor_copy(ot[0:64], b[0:64, :, :, 0])
            V.tensor_copy(ot[64:P], b[64:P, :, :, 1]).then_inc(sg["o_dve"], 1)
        elif kind == "otn":
            sg.wait(dve, "pvn", ("winv", 3))
            sg.wait(dve, "t_full", ("osb4",))
            b = at("o", ("nss",))[:, 0:64].rearrange("p (b h) -> p h b", b=NB)
            V.tensor_copy(ot[0:64], b[0:64, 0:REP])
            V.tensor_copy(ot[64:P], b[64:P, REP:HEADS]).then_inc(sg["o_dve"], 1)
        elif kind == "cmp_score":
            i, = key
            b = bank[7][:, 0:256].rearrange("p (h n) -> p h n", h=HEADS)
            cp = cprob.rearrange("p (h n) -> p h n", h=HEADS)
            sg.wait(dve, "x_full", ("cmp", i))
            if i > 0:
                sg.wait(dve, "t_full", ("cT", i - 1))
            neg = c["cneg"][:, i * 32:(i + 1) * 32].unsqueeze(1).to_broadcast([P, HEADS, 32])
            V.tensor_tensor(cp, b, neg, ALU.add).then_inc(sg["x_dve"], 1)
            sg.wait(dve, "x_dve", ("cmp", i))
            link(V.tensor_reduce(st[:, 60:68], cp, AX.X, ALU.max))
            V.tensor_tensor(cp, cp, st[:, 60:68].unsqueeze(2).to_broadcast([P, HEADS, 32]), ALU.subtract
                            ).then_inc(sg["c_max"], 1)
        elif kind == "cmp_norm":
            i, = key
            cp = cprob.rearrange("p (h n) -> p h n", h=HEADS)
            one = c["cone"][:, i * 32:(i + 1) * 32].unsqueeze(1).to_broadcast([P, HEADS, 32])
            sg.wait(dve, "c_exp", i)
            link(V.tensor_tensor(cp, cp, one, ALU.mult))
            link(V.tensor_reduce(st[:, 60:68], cp, AX.X, ALU.add))
            link(V.tensor_scalar(st[:, 60:68], st[:, 60:68], 1e-30, None, ALU.max))
            link(V.reciprocal(st[:, 60:68], st[:, 60:68]))
            link(V.tensor_tensor(st[:, 60:68], st[:, 60:68], gate_rows(i)[:, 0], ALU.mult))
            V.tensor_tensor(cp, cp, st[:, 60:68].unsqueeze(2).to_broadcast([P, HEADS, 32]), ALU.mult
                            ).then_inc(sg["c_prob"], 1)
        elif kind == "branch":
            i, b = key
            o3 = at("o", key)[:, :].rearrange("p (h d) -> p h d", h=HEADS)
            sg.wait(dve, "pv", (i, b, HEADS - 1))
            if b == SB:
                sg.wait(dve, "mix", tile_order[tile_order.index(i) - 1])
                V.tensor_copy(o_sb, at("o", key)[:, :]).then_inc(sg["o_dve"], 1)
                ob = at("o", (i, "cmp"))
                sg.wait(dve, "o_done", (i, "cmp"))
                V.tensor_copy(o_nsa, ob[:, :]).then_inc(sg["o_dve"], 1)
                sg.wait(dve, "o_dve", (i, "cmp"))
                return
            w = st[:, 72 + 8 * (b - 1):80 + 8 * (b - 1)]
            link(V.reciprocal(w, st[:, 8 * (b - 1):8 * b]))
            link(V.tensor_tensor(w, w, gate_rows(i)[:, b], ALU.mult))
            V.tensor_tensor(o_part.rearrange("p (h d) -> p h d", h=HEADS), o3,
                            w.unsqueeze(2).to_broadcast([P, HEADS, HD]), ALU.mult).then_inc(sg["o_dve"], 1)
            sg.wait(dve, "o_dve", key)
            V.tensor_tensor(o_nsa, o_nsa, o_part, ALU.add).then_inc(sg["branch"], 1)
        elif kind == "mix_ssq":
            i, = key
            r = ROWS[i]
            if i == QT:
                for n in range(2):
                    dve.wait_ge(sg[f"st_rot{n}"], sg.total[f"st_rot{n}"])
                wait_transposed(dve, ("osb4",))
                wait_transposed(dve, ("ons4",))
            else:
                sg.wait(dve, "branch", (i, WIN))
            if i != QT:
                sg.wait(dve, "t_full", ("mixT", tile_order[tile_order.index(i) - 1], 1))
            V.tensor_tensor_reduce(mix[0:r, 0:512], o_sb[0:r], o_sb[0:r], 1.0, 0.0, ALU.mult, ALU.add, small[0:r, 8:9])
            V.tensor_tensor_reduce(mix[0:r, 512:D], o_nsa[0:r], o_nsa[0:r], 1.0, 0.0, ALU.mult, ALU.add,
                                   small[0:r, 9:10]).then_inc(sg["ssq"], 1)
        elif kind == "mix":
            i, = key
            r = ROWS[i]
            if i == QT:
                dve.wait_ge(sg["gain_in"], 48)
            sg.wait(dve, "rstd", ("mix", i))
            V.scalar_tensor_tensor(mix[0:r, 0:512], o_sb[0:r], small[0:r, 8:9], gain_out[0:r, 0:512],
                                   ALU.mult, ALU.mult)
            V.scalar_tensor_tensor(mix[0:r, 512:D], o_nsa[0:r], small[0:r, 9:10], gain_out[0:r, 512:D],
                                   ALU.mult, ALU.mult).then_inc(sg["mix"], 1)
        elif kind == "wout":
            i, half, part = key
            if part == len(WOUT_PARTS) - 1:
                r, sl = ROWS[i], slice(512 * half, 512 * half + 512)
                sg.wait(dve, "x_full", ("wout", i, half))
                V.tensor_tensor(x[0:r, i, sl], x[0:r, i, sl], bank[7][0:r, :], ALU.add).then_inc(sg["x_dve"], 1)
        elif kind == "ffn_ssq":
            i, = key
            r = ROWS[i]
            sg.wait(dve, "x_dve", ("wout", i, 1))
            if i != QT:
                before = tile_order[tile_order.index(i) - 1]
                sg.wait(dve, "st_h2", before)
                sg.wait(dve, "t_full", ("h2T", before, 1))
            V.tensor_tensor_reduce(h2[0:r], x[0:r, i, :], x[0:r, i, :], 1.0, 0.0, ALU.mult, ALU.add,
                                   small[0:r, 10:11]).then_inc(sg["ssq"], 1)
        elif kind == "h2":
            i, = key
            r = ROWS[i]
            sg.wait(dve, "rstd", ("ffn", i))
            V.scalar_tensor_tensor(h2[0:r], x[0:r, i, :], small[0:r, 10:11], gain[0:r, :], ALU.mult, ALU.mult
                                   ).then_inc(sg["h2"], 1)
        elif kind in ("route", "route_experts", "route_choice"):
            i, = key
            r = ROWS[i]
            gl, ex, m8, el, n8 = rt[0:r, 0:8], rt[0:r, 16:32], rt[0:r, 32:40], rt[0:r, 8:16], rt[0:r, 40:48]
            prod = rt[0:r, 48:64].rearrange("p (e g) -> p e g", e=4)
            b = bank[7]
            if kind == "route_experts":
                route_experts(link, r, ex, n8, el, prod)
                return
            if kind == "route_choice":
                route_choice(dve, link, i, r, n8, el)
                return
            if i == QT:
                dve.wait_ge(sg["router_in"], 64)
                dve.wait_ge(sg["table_zero"], 16)
                link(V.memset(rt[:, 0:16], NEG))
            sg.wait(dve, "x_full", ("logit", i))
            V.tensor_tensor(gl[:, 0:4], b[0:r, 0:4], br[0:r, 0:4], ALU.add)
            V.tensor_tensor(ex, b[0:r, 4:20], br[0:r, 4:20], ALU.add).then_inc(sg["x_dve"], 1)
            sg.wait(dve, "x_dve", ("logit", i))
            link(V.max(m8, gl))
            V.tensor_scalar(rt[0:r, 70:71], m8[:, 0:1], -1.0, None, ALU.mult).then_inc(sg["r_max"], 1)
            link(V.max_index(smi[0:r, 0:8], m8, gl))
            link(V.tensor_copy(rt[0:r, 74:75], smi[0:r, 0:1]))
            link(V.tensor_scalar(rt[0:r, 76:80], c["iota16"][0:r, 0:4], rt[0:r, 74:75], None, ALU.is_equal))
        elif kind == "rank":
            i, = key
            r = ROWS[i]
            b = bank[7]
            sg.wait(dve, "x_full", ("rank", i))
            V.tensor_tensor(rt[0:r, 128:144], b[0:r, 0:16], c["base16"][0:r], ALU.add).then_inc(sg["x_dve"], 1)
            sg.wait(dve, "x_dve", ("rank", i))
            link(V.tensor_tensor(rt[0:r, 144:176].rearrange("p (k e) -> p k e", k=2),
                                 chosen[0:r, i],
                                 rt[0:r, 128:144].unsqueeze(1).to_broadcast([r, 2, 16]), ALU.mult))
            link(V.tensor_reduce(slot_f[0:r, i, :], rt[0:r, 144:176].rearrange("p (k e) -> p k e", k=2), AX.X, ALU.add))
            V.tensor_copy(slots[0:r, i, :], slot_f[0:r, i, :]).then_inc(sg["slots"], 1)
        else:
            expert_dve(dve, link, kind, key)

    pe_chain = [0]

    def pe_link(ins):
        pe_chain[0] += 1
        ins.then_inc(sg["pe_chain"], 1)
        nc.tensor.wait_ge(sg["pe_chain"], pe_chain[0])

    def pe_more(pe, kind, key):
        T = nc.tensor
        if kind == "hid":
            kv, = key
            if kv == 0:
                pe.wait_ge(sg["w1_in"], 32)
            for q in range(len(order)):
                if order[q][0] == kv:
                    wait_transposed(pe, ("XT", q))
            wait_transposed(pe, ("peT", kv))
            for half, name in enumerate(("hidA", "hidB")):
                acquire(pe, "m", (name, kv))
                for lp in range(8):
                    ins = T.matmul(at("m", (name, kv))[:, 0:322], w1[kv][:, 8 * half + lp, :],
                                   xt[kv][:, lp:2576:8], start=(lp == 0), stop=(lp == 7))
                ins.then_inc(sg["m_full"], 1)
        elif kind == "comp":
            kv, = key
            sg.wait(pe, "hid", kv)
            acquire(pe, "m", ("comp", kv))
            b = at("m", ("comp", kv))
            if kv == 0:
                for g in range(GROUPS):
                    ins = T.matmul(b[64 * g:64 * g + 64, 0:NCHUNK], w2[:, 0, :], hid[0][:, g * NCHUNK:(g + 1) * NCHUNK],
                                   start=True, stop=True)
            else:
                for g in range(GROUPS):
                    for copy in range(4):
                        T.matmul(b[32 * copy:32 * copy + 32, g * HD:(g + 1) * HD],
                                 hid[1][:, g * NCHUNK:g * NCHUNK + 32], w2[:, 1, :], start=True, stop=True)
                    ins = T.matmul(b[:, P + g * HD:P + (g + 1) * HD], hid[1][:, g * NCHUNK + 32:(g + 1) * NCHUNK],
                                   w2[:, 1, :], start=True, stop=True)
            ins.then_inc(sg["m_full"], 1)
        elif kind == "zs":
            what, g = key
            if key == ("sbk", 0):
                acquire(pe, "x", ("zsb",))
                sg.wait(pe, "qbd", 0)
            if key == ("selk", 0):
                acquire(pe, "x", ("zn",))
                sg.wait(pe, "qbn", 0)
            wait_transposed(pe, ("KT",) + key)
            kt = pageT[:, kt_index[key] % 3]
            for s in range(4):
                if what == "sbk":
                    b_, pg = g // 2, g % 2
                    at_ = pg * 64 + b_ * 8 + 2 * s
                    ins = T.matmul(bank[7][:, at_:at_ + 2], kt[:, s, :], qbd[:, s, b_, :], start=True, stop=True)
                else:
                    j = 4 * g + s
                    b_, pg = j // 2, j % 2
                    at_ = (P if what == "wink" else 0) + pg * 64 + b_ * 8
                    ins = T.matmul(bank[7][:, at_:at_ + 8], kt[:, s, :], qbn[:, b_, :], start=True, stop=True)
            ins.then_inc(sg["scored"], 1)
        elif kind == "sample_small":
            q64 = smp[:, 64:128]
            wait_transposed(pe, ("pT", pn[KV4, QT]))
            wait_transposed(pe, ("pT", pn[KV2, QT]))
            sg.wait(pe, "m_act", ("comp", 1))
            sg.wait(pe, "gates", 0)
            acquire(pe, "m", ("snew",))
            T.matmul(at("m", ("snew",))[0:64, 0:8], q64, kselT[:, SEQ:TOK], start=True, stop=True)
            T.matmul(at("m", ("snew",))[0:64, 8:16], q64, kwinT[:, SEQ:TOK], start=True, stop=True
                     ).then_inc(sg["m_full"], 1)
            acquire(pe, "m", ("gsp",))
            T.matmul(at("m", ("gsp",))[0:64, 0:24], c["spread"][0:NB, 0:64], gates[0:NB, QT, :], start=True, stop=True
                     ).then_inc(sg["m_full"], 1)
            acquire(pe, "m", ("cs",))
            T.matmul(at("m", ("cs",))[0:64, 0:P], q64, kcT[:, 32:NCHUNK], start=True, stop=True
                     ).then_inc(sg["m_full"], 1)
        elif kind == "pvs":
            b_, = key
            if b_ == 0:
                acquire(pe, "o", ("sbs",))
                wait_transposed(pe, ("aT",))
            for pg in range(NPG):
                q = lq["sbv", 2 * b_ + pg]
                sg.wait(pe, f"page{q % SLOTS}", q)
            for j in range(4):
                for pg in range(NPG):
                    q = lq["sbv", 2 * b_ + pg]
                    last = T.matmul(at("o", ("sbs",))[:, j * 16 + 2 * b_:j * 16 + 2 * b_ + 2], page[:, q % SLOTS, j, :],
                                    s_probT[:, pg * 64 + b_ * 8 + 2 * j:pg * 64 + b_ * 8 + 2 * j + 2],
                                    start=(pg == 0), stop=(pg == 1))
            last.then_inc(sg["pvs"], 1)
        elif kind == "pvn":
            what, g = key
            b = at("o", ("nss",))
            if key == ("selv", 0):
                acquire(pe, "o", ("nss",))
                wait_transposed(pe, ("pT4",))
                T.matmul(b[:, 0:64], vsel[0:NB, QT, :], pt4[0:NB, 320:384], start=True, stop=False)
                T.matmul(b[:, 0:64], vwin[0:NB, QT, :], pt4[0:NB, 384:448], start=False, stop=False)
                T.matmul(b[:, 0:64], vc[:, 1, :], pt4[:, 256:320], start=False, stop=False)
            q = lq[key]
            sg.wait(pe, f"page{q % SLOTS}", q)
            for s in range(4):
                j = 4 * g + s
                b_, pg = j // 2, j % 2
                base = (2 * (what == "winv") + pg) * 64 + b_ * 8
                last = T.matmul(b[:, b_ * 8:b_ * 8 + 8], page[:, q % SLOTS, s, :], pt4[:, base:base + 8],
                                start=False, stop=(what == "winv" and j == 15))
            last.then_inc(sg["pvn"], 1)
        elif kind == "score":
            i, b, h = key
            acquire(pe, "m", key)
            t = at("m", key)
            n, qs = (i + 1) * P, slice(i * P, (i + 1) * P)
            if key == steps[0]:
                pe.wait_ge(sg["const_b"], 16)
                for j in range(len(proj)):
                    if blocks[proj[j][0]]:
                        wait_transposed(pe, ("pT", j))
            if b == SB:
                rows = slice(64 * (h % 2), 64 * (h % 2) + 64)
                lhs, rhs = qsbT[rows, h // 2, qs], ksbT[rows, h // 2, 0:n]
            else:
                g, r = h // REP, h % REP
                rows = slice(64 * g, 64 * g + 64)
                lhs, rhs = qnsaT[rows, r, qs], (kselT if b == SEL else kwinT)[rows, 0:n]
            T.matmul(t[:, 0:n], lhs, rhs, start=True, stop=False)
            T.matmul(t[:, qs], c["identb"], c["before"] if b == SB else c["upto"], start=False, stop=True
                     ).then_inc(sg["m_full"], 1)
        elif kind == "pv":
            i, b, h = key
            if h == 0:
                acquire(pe, "o", (i, b))
            wait_transposed(pe, ("probT",) + key)
            q = order_of[key]
            for k in range(i + 1):
                v = vsb[:, k, h * HD:(h + 1) * HD] if b == SB else (vsel if b == SEL else vwin)[
                    :, k, (h // REP) * HD:(h // REP + 1) * HD]
                ins = T.matmul(at("o", (i, b))[:, h * HD:(h + 1) * HD], probT[:, q % 3, k * P:(k + 1) * P], v,
                               start=(k == 0), stop=(k == i))
            ins.then_inc(sg["pv"], 1)
        elif kind == "cmp_score":
            i, = key
            acquire(pe, "x", ("cmp", i))
            for h in range(HEADS):
                g, r = h // REP, h % REP
                rows = slice(64 * g, 64 * g + 64)
                ins = T.matmul(bank[7][:, h * 32:(h + 1) * 32], qnsaT[rows, r, i * P:(i + 1) * P], kcT[rows, 0:32],
                               start=True, stop=True)
                if h == REP - 1:
                    pe_link(ins)
            ins.then_inc(sg["x_full"], 1)
        elif kind == "cmp_pv":
            i, = key
            acquire(pe, "o", (i, "cmp"))
            wait_transposed(pe, ("cT", i))
            for r in range(REP):
                rows = slice(32 * r, 32 * r + 32)
                for g in range(GROUPS):
                    h = g * REP + r
                    ins = T.matmul(at("o", (i, "cmp"))[:, h * HD:(h + 1) * HD], cprobT[rows, g * P:(g + 1) * P],
                                   vc[rows, 0, g * HD:(g + 1) * HD], start=True, stop=True)
                if r < REP - 1:
                    pe_link(ins)
            ins.then_inc(sg["o_done"], 1)
        elif kind == "wout":
            i, half, part = key
            r = ROWS[i]
            if part == 0:
                if i == QT:
                    pe.wait_ge(sg["w_out"], 16)
                for h in range(2):
                    wait_transposed(pe, ("mixT", i, h))
                acquire(pe, "x", ("wout", i, half))
            for k in WOUT_PARTS[part]:
                ins = T.matmul(bank[7][0:r, :], mixT[:, k, 0:r], w_out[:, k, 512 * half:512 * half + 512],
                               start=(k == 0), stop=(k == KD - 1))
            if part == len(WOUT_PARTS) - 1:
                ins.then_inc(sg["x_full"], 1)
        elif kind == "route":
            i, = key
            r = ROWS[i]
            acquire(pe, "x", ("logit", i))
            if i == QT:
                pe.wait_ge(sg["router_in"], 64)
            for half in range(2):
                wait_transposed(pe, ("h2T", i, half))
            for k in range(KD):
                ins = T.matmul(bank[7][0:r, 0:20], mixT[:, k, 0:r], wr[:, k, :], start=(k == 0), stop=(k == KD - 1))
            ins.then_inc(sg["x_full"], 1)
        elif kind == "rank":
            i, = key
            r = ROWS[i]
            acquire(pe, "x", ("rank", i))
            sg.wait(pe, "onehot", i)
            done = tile_order[:tile_order.index(i)]
            for n, j in enumerate(done):
                T.matmul(bank[7][0:r, 0:16], c["onesb"][0:ROWS[j], 0:r], onehot[0:ROWS[j], j, :], start=(n == 0),
                         stop=False)
            T.matmul(bank[7][0:r, 0:16], c["earlier"][0:r, 0:r], onehot[0:r, i, :], start=(not done), stop=True
                     ).then_inc(sg["x_full"], 1)
        else:
            expert_pe(pe, kind, key)

    def expert_weights(region):
        return view(region, 0, [KD, FF]), view(region, 4096, [KD, FF]), view(region, 8192, [FF // P, D])

    weights = [expert_weights(reg0), expert_weights(reg1)]
    rows_in = [work[:, 0:1024], work[:, 1024:2048]]
    sig = [work[:, 2048:2560], work[:, 2560:3072]]
    acts = [work[:, 3072:3584], work[:, 3584:4096]]
    actsT = [view(work, 4096, [4, P]), view(work, 4608, [4, P])]

    def flat(t):
        return t[:, :, :].rearrange("p a b -> p (a b)")

    rowsT = [flat(qsbT)[:, 0:1024].rearrange("p (k t) -> p k t", k=KD),
             flat(qsbT)[:, 1024:2048].rearrange("p (k t) -> p k t", k=KD)]
    y_rows = [flat(ksbT)[:, 0:1024], flat(ksbT)[:, 1024:2048]]
    ids_row = flat(qnsaT)[0:NE, 0:P]
    ids = sb("ids", [P, NE], U32)
    more_f = sb("more_f", [P, 1])
    more_ids = sb("more_ids", [P, 1], U32)
    extra = flat(qnsaT)[:, P:P + 704]
    extra_i = sb("extra_i", [1, 24], I32)
    gathered = view(reg0, 0, [2 * TILES, D])

    use("x", ("idx",), "dve")
    step("idx")
    sg.mark("ids_in", 0, 16)
    sg.mark("ids", 0)
    use("x", ("count",), "dve")
    step("count")
    sg.mark("extra", 0)
    sg.mark("y_slots", 0)
    step("experts")
    for n in ("e_rows_a", "e_rows_v", "e_gate", "e_exp", "e_gated", "e_up", "e_act", "e_actT_full", "e_actT",
              "e_down", "e_y_a", "e_y_v", "e_rowsT_full"):
        sg.mark(n, 0)
    for b in range(2):
        for n in ("e_x", "e_wgu", "e_wd", "e_st"):
            sg.mark(f"{n}{b}", 0)
    for n in ("v_w", "v_idx", "v_idc", "v_x", "v_rowsT_full", "v_rows", "v_gu", "v_exp", "v_act", "v_actT_full",
              "v_actT", "v_down", "v_y", "v_st", "v_passed", "v_passed_sp"):
        sg.mark(n, 0)
    sg.mark("gain_final", 0, 16)
    sg.mark("rows_stored", 0)
    for i in range(TILES):
        step("final", i)
        sg.mark(f"gathered{i}", i, 32)
        sg.mark("combined", i)
        sg.mark("ssq_final", i)
        sg.mark("final_pool" if i in POOL_FINAL else "final", i)
        sg.mark("st_y", i, 16)
    PLAN.insert(PLAN.index(("load_wout", ())) + 1, ("expert0", ()))
    final_waits = [(n, t) for n, t in sg.total.items() if n.startswith("st_")]
    LAST = NE - 1

    def same(j, n):
        return isinstance(j, int) and j == n

    def overflow(eng, one):
        sg.wait(eng, "extra", 0)
        count = eng.value_load(extra_i[0:1, 16:17], min_val=0, max_val=EXTRA)
        with eng.If(count > 0):
            with eng.Fori(0, EXTRA) as v:
                with eng.If(v < count):
                    one(v)

    def load_gate_up(sp, e, b, sem):
        for name, dst in (("w_gate", weights[b][0]), ("w_up", weights[b][1])):
            src = a[name][0, bass.ds(e, 1)].rearrange("o (k p) f -> p (o k) f", p=P)
            sp.dma_start(dst, src).then_inc(sem, 16)

    def load_down(sp, e, b, sem):
        src = a["w_down"][0, bass.ds(e, 1)].rearrange("o (k p) f -> p (o k) f", p=P)
        sp.dma_start(weights[b][2], src).then_inc(sem, 16)

    def expert_sync(sp, kind, key):
        if kind == "expert0":
            sg.wait(sp, "m_full", ("proj", len(proj) - 1))
            sg.wait(sp, "t_full", ("ons4",))
            load_gate_up(sp, 0, 0, sg["e_wgu0"])
            load_down(sp, 0, 0, sg["e_wd0"])
        elif kind == "experts":
            sg.wait(sp, "x_full", ("logit", QT - 1))
            for n in range(TILES):
                sg.wait(sp, "st_h2", n)
            sp.wait_ge(sg["e_x0"], 16)
            load_gate_up(sp, 1, 1, sg["e_wgu1"])
            load_down(sp, 1, 1, sg["e_wd1"])

            def one(j, b, n):
                if not same(j, LAST):
                    sp.wait_ge(sg["e_up"], j)
                    load_gate_up(sp, j + 1, 1 - b, sg[f"e_wgu{1 - b}"])
                    sp.wait_ge(sg["e_down"], j)
                    load_down(sp, j + 1, 1 - b, sg[f"e_wd{1 - b}"])
                store_rows(j - 1, 1 - b, j)

            def store_rows(e, b, done):
                sp.wait_ge(sg["e_y_a"], done)
                sp.wait_ge(sg["e_y_v"], done)
                sp.dma_start(y_dram[bass.ds(e * P, P), :], y_rows[b]).then_inc(sg[f"e_st{b}"], 16)

            with sp.Fori(0, NE // 2 - 1) as it:
                one(2 * it + 1, 1, it)
                one(2 * it + 2, 0, it + 1)
            one(LAST, 1, NE // 2 - 1)
            store_rows(LAST, 1, NE)

            def more(v):
                e = sp.value_load(extra_i[0:1, bass.ds(v, 1)], min_val=0, max_val=NE - 1)
                row = sp.value_load(extra_i[0:1, bass.ds(v + 8, 1)], min_val=0, max_val=NE * CAP - P)
                load_gate_up(sp, e, 0, sg["v_w"])
                load_down(sp, e, 0, sg["v_w"])
                sp.dma_start(more_f[:, :], table[bass.ds(row, P), :]).then_inc(sg["v_idx"], 16)
                sp.wait_ge(sg["v_y"], 2 * v + 2)
                sp.dma_start(y_dram[bass.ds((v + NE) * P, P), :], y_rows[0]).then_inc(sg["v_st"], 16)
                sp.wait_ge(sg["v_st"], 16 * v + 16)
                sp.sem_inc(sg["v_passed_sp"], 1)

            sp.dma_start(gain[:, :], a["norm_final"].rearrange("(o d) -> o d", o=1).partition_broadcast(P).rearrange(
                "p o d -> p (o d)")).then_inc(sg["gain_final"], 16)
            for b in range(2):
                sp.wait_ge(sg[f"e_st{b}"], 16 * NE // 2)
            overflow(sp, more)
            sp.sem_inc(sg["rows_stored"], 1)
        elif kind == "final":
            i, = key
            sg.wait(sp, "final_pool" if i in POOL_FINAL else "final", i)
            dst = out["y_p"][0, i * P:(i + 1) * P, :] if i < QT else out["y_s"][:, 0, :]
            sp.dma_start(dst, x[0:ROWS[i], i, :]).then_inc(sg["st_y"], 16)

    def expert_gps(pool, kind, key):
        if kind == "idx":
            pool.wait_ge(sg["scatter"], sg.total["scatter"])
            pool.dma_start(ids_row, table.rearrange("(e n) o -> e (n o)", e=NE)[:, 0:P]).then_inc(sg["ids_in"], 16)
        elif kind == "experts":
            pool.wait_ge(sg["ids"], 1)
            pool.wait_ge(sg["st_h2"], sg.total["st_h2"])
            sg.wait(pool, "pv", steps[-1])
            sg.wait(pool, "x_full", ("logit", QT - 1))
            for j in range(NE):
                if j >= 2:
                    pool.wait_ge(sg["e_rowsT_full"], 2 * (j - 2) + 2)
                nc.gpsimd.indirect_dma_start(rows_in[j % 2], None, h2_dram,
                                             bass.IndirectOffsetOnAxis(ap=ids[:, j:j + 1], axis=0)
                                             ).then_inc(sg[f"e_x{j % 2}"], 16)

            def more(v):
                pool.wait_ge(sg["v_idx"], 16 * v + 16)
                pool.sem_inc(sg["v_passed"], 1)
                nc.gpsimd.tensor_copy(more_ids[:, :], more_f[:, :]).then_inc(sg["v_idc"], 1)
                pool.wait_ge(sg["v_idc"], v + 1)
                pool.sem_inc(sg["v_passed"], 1)
                nc.gpsimd.indirect_dma_start(rows_in[0], None, h2_dram,
                                             bass.IndirectOffsetOnAxis(ap=more_ids[:, 0:1], axis=0)
                                             ).then_inc(sg["v_x"], 16)
                pool.wait_ge(sg["v_x"], 16 * v + 16)
                pool.sem_inc(sg["v_passed"], 1)

            pool.wait_ge(sg["e_rowsT_full"], 2 * NE)
            overflow(pool, more)
        elif kind == "final":
            i, = key
            if i == 0:
                pool.wait_ge(sg["rows_stored"], 1)
                sg.wait(pool, "y_slots", 0)
            for k in range(2):
                nc.gpsimd.indirect_dma_start(gathered[0:ROWS[i], 2 * i + k, :], None, y_dram,
                                             bass.IndirectOffsetOnAxis(ap=y_slots[0:ROWS[i], i, k:k + 1], axis=0)
                                             ).then_inc(sg[f"gathered{i}"], 16)
            if i == TILES - 1:
                for j in POOL_FINAL:
                    finish_rows(pool, nc.gpsimd, "final_pool", j)

    def expert_act(act, link, inverse_rms, kind, key):
        A = nc.scalar
        if kind == "experts":
            def rows_out(j, b):
                act.wait_ge(sg["e_rowsT_full"], 2 * j + 1)
                A.copy(rowsT[b][:, 0:4, :], bank[3][:, :].rearrange("p (k t) -> p k t", k=4)
                       ).then_inc(sg["e_rows_a"], 1)

            def exp_gate(j, b):
                act.wait_ge(sg["e_gate"], j + 1)
                A.activation(sig[b], bank[0][:, :], ACT.Exp, scale=-1.0).then_inc(sg["e_exp"], 1)

            def acts_out(j, b):
                act.wait_ge(sg["e_actT_full"], j + 1)
                A.copy(actsT[b], bank[5][:, :].rearrange("p (k t) -> p k t", k=4)).then_inc(sg["e_actT"], 1)

            def y_out(j, b, n):
                act.wait_ge(sg["e_down"], j + 1)
                if not same(n, 0):
                    act.wait_ge(sg[f"e_st{b}"], 16 * n)
                A.copy(y_rows[b][:, 0:512], bank[2][:, :]).then_inc(sg["e_y_a"], 1)

            def one(j, b, n):
                exp_gate(j, b)
                if not same(j, 0):
                    acts_out(j - 1, 1 - b)
                if not same(j, LAST):
                    rows_out(j + 1, 1 - b)
                if not same(j, 0):
                    y_out(j - 1, 1 - b, n if b else n - 1)

            rows_out(0, 0)
            one(0, 0, 0)
            one(1, 1, 0)
            one(2, 0, 1)
            one(3, 1, 1)
            with act.Fori(2, NE // 2 - 1) as it:
                one(2 * it, 0, it)
                one(2 * it + 1, 1, it)
            one(NE - 2, 0, NE // 2 - 1)
            one(LAST, 1, NE // 2 - 1)
            acts_out(LAST, 1)
            y_out(LAST, 1, NE // 2 - 1)

            def more(v):
                act.wait_ge(sg["v_rowsT_full"], v + 1)
                A.copy(rowsT[0][:, 0:4, :], bank[3][:, :].rearrange("p (k t) -> p k t", k=4)).then_inc(sg["v_rows"], 1)
                act.wait_ge(sg["v_gu"], v + 1)
                A.activation(sig[0], bank[0][:, :], ACT.Exp, scale=-1.0).then_inc(sg["v_exp"], 1)
                act.wait_ge(sg["v_actT_full"], v + 1)
                A.copy(actsT[0], bank[5][:, :].rearrange("p (k t) -> p k t", k=4)).then_inc(sg["v_actT"], 1)
                act.wait_ge(sg["v_down"], v + 1)
                A.copy(y_rows[0][:, 0:512], bank[2][:, :]).then_inc(sg["v_y"], 1)
            overflow(act, more)
        elif kind == "final":
            i, = key
            r = ROWS[i]
            sg.wait(act, "combined", i)
            link(A.activation(gathered[0:r, 2 * i, :], x[0:r, i, :], ACT.Square, accum_out=small[0:r, 16 + i:17 + i]))
            link(A.activation(small[0:r, 16 + i:17 + i], small[0:r, 16 + i:17 + i], ACT.Ln, bias=c["eps"][0:r],
                              scale=1.0 / D))
            last = A.activation(small[0:r, 16 + i:17 + i], small[0:r, 16 + i:17 + i], ACT.Exp, scale=-0.5)
            if i in POOL_FINAL:
                link(last)
                last = A.activation(x[0:r, i, :], x[0:r, i, :], ACT.Copy, scale=small[0:r, 16 + i:17 + i])
            last.then_inc(sg["ssq_final"], 1)

    def expert_dve(dve, link, kind, key):
        V = nc.vector
        if kind == "idx":
            sg.wait(dve, "x_full", ("idx",))
            V.tensor_copy(ids[:, :], bank[7][:, 0:NE]).then_inc(sg["x_dve"], 1)
            sg.wait(dve, "x_dve", ("idx",))
            V.memset(smi[:, 40:41], 0).then_inc(sg["ids"], 1)
        elif kind == "count":
            sg.wait(dve, "x_full", ("count",))
            cnt, t0, cum, n = (extra[:, 16 * q:16 * q + 16] for q in range(4))
            le = extra[0:1, 64:192].rearrange("p (v e) -> p v e", v=8)
            prod = extra[0:1, 192:320].rearrange("p (v e) -> p v e", v=8)
            ex, tl, rowf = extra[0:1, 320:328], extra[0:1, 328:336], extra[0:1, 336:344]
            V.tensor_copy(cnt, bank[7][:, 0:16]).then_inc(sg["x_dve"], 1)
            sg.wait(dve, "x_dve", ("count",))
            link(V.tensor_scalar(n, cnt, float(P), None, ALU.is_gt))
            for k in range(2, 5):
                link(V.tensor_scalar(t0, cnt, float(k * P), None, ALU.is_gt))
                link(V.tensor_tensor(n, n, t0, ALU.add))
            link(V.tensor_tensor_scan(cum, c["one"].to_broadcast([P, 16]), n, 0.0, ALU.mult, ALU.add))
            link(V.tensor_tensor(le, cum[0:1].unsqueeze(1).to_broadcast([1, 8, 16]),
                                 c["iota16"][0:1, 0:8].unsqueeze(2).to_broadcast([1, 8, 16]), ALU.is_le))
            link(V.tensor_tensor(prod, le, n[0:1].unsqueeze(1).to_broadcast([1, 8, 16]), ALU.mult))
            V.tensor_reduce(ex, le, AX.X, ALU.add)
            link(V.tensor_reduce(tl, prod, AX.X, ALU.add))
            link(V.tensor_scalar(ex, ex, float(NE - 1), None, ALU.min))
            link(V.tensor_tensor(tl, c["iota16"][0:1, 0:8], tl, ALU.subtract))
            link(V.tensor_scalar(tl, tl, 1.0, float(P), ALU.add, ALU.mult))
            link(V.scalar_tensor_tensor(rowf, ex, float(CAP), tl, ALU.mult, ALU.add))
            link(V.tensor_scalar(rowf, rowf, float(NE * CAP - P), None, ALU.min))
            V.tensor_copy(extra_i[0:1, 0:8], ex)
            V.tensor_copy(extra_i[0:1, 8:16], rowf)
            V.tensor_copy(extra_i[0:1, 16:17], cum[0:1, 15:16]).then_inc(sg["extra"], 1)
        elif kind == "experts":
            def rows_out(j, b):
                dve.wait_ge(sg["e_rowsT_full"], 2 * j + 2)
                V.tensor_copy(rowsT[b][:, 4:8, :], bank[4][:, :].rearrange("p (k t) -> p k t", k=4)
                              ).then_inc(sg["e_rows_v"], 1)

            def gated(j, b):
                dve.wait_ge(sg["e_exp"], j + 1)
                link_loop(V.tensor_scalar(sig[b], sig[b], 1.0, None, ALU.add), 3 * j + 1)
                link_loop(V.reciprocal(sig[b], sig[b]), 3 * j + 2)
                link_loop(V.tensor_tensor(sig[b], sig[b], bank[0][:, :], ALU.mult), 3 * j + 3)
                dve.wait_ge(sg["e_up"], j + 1)
                V.tensor_tensor(acts[b], sig[b], bank[1][:, :], ALU.mult).then_inc(sg["e_act"], 1)

            def link_loop(ins, value):
                ins.then_inc(sg["e_gated"], 1)
                dve.wait_ge(sg["e_gated"], value)

            def place_results():
                n10 = 2 * TILES
                cum, n = extra[:, 32:48], extra[:, 48:64]
                shift, rank = extra[:, 64:80], extra[:, 80:80 + n10]
                over, base = extra[:, 96:96 + n10], extra[:, 112:112 + n10]
                prod = extra[:, 344:344 + n10 * NE].rearrange("p (k e) -> p k e", e=NE)
                e_ = expert[:, :, :].rearrange("p i k -> p (i k)")
                link(V.tensor_tensor(shift, cum, n, ALU.subtract))
                link(V.tensor_scalar(shift, shift, float(NE - 1), None, ALU.add))
                link(V.tensor_tensor(shift, shift, c["iota16"], ALU.subtract))
                link(V.tensor_tensor(prod, chosen[:, :, :, :].rearrange("p i k e -> p (i k) e"),
                                     shift.unsqueeze(1).to_broadcast([P, n10, NE]), ALU.mult))
                V.tensor_reduce(base, prod, AX.X, ALU.add)
                link(V.scalar_tensor_tensor(rank, e_, float(-CAP), slot_f[:, :, :].rearrange("p i k -> p (i k)"),
                                            ALU.mult, ALU.add))
                link(V.tensor_scalar(over, rank, float(P), None, ALU.is_ge))
                link(V.tensor_tensor(base, base, over, ALU.mult))
                link(V.tensor_tensor(base, base, e_, ALU.add))
                link(V.scalar_tensor_tensor(rank, base, float(P), rank, ALU.mult, ALU.add))
                V.tensor_copy(y_slots[:, :, :].rearrange("p i k -> p (i k)"), rank).then_inc(sg["y_slots"], 1)

            def y_out(j, b, n):
                dve.wait_ge(sg["e_down"], j + 1)
                if not same(n, 0):
                    dve.wait_ge(sg[f"e_st{b}"], 16 * n)
                V.tensor_copy(y_rows[b][:, 512:D], bank[6][:, :]).then_inc(sg["e_y_v"], 1)

            def one(j, b, n):
                gated(j, b)
                if not same(j, LAST):
                    rows_out(j + 1, 1 - b)
                if not same(j, 0):
                    y_out(j - 1, 1 - b, n if b else n - 1)

            rows_out(0, 0)
            one(0, 0, 0)
            place_results()
            one(1, 1, 0)
            one(2, 0, 1)
            one(3, 1, 1)
            with dve.Fori(2, NE // 2 - 1) as it:
                one(2 * it, 0, it)
                one(2 * it + 1, 1, it)
            one(NE - 2, 0, NE // 2 - 1)
            one(LAST, 1, NE // 2 - 1)
            y_out(LAST, 1, NE // 2 - 1)

            def more(v):
                dve.wait_ge(sg["v_rowsT_full"], v + 1)
                V.tensor_copy(rowsT[0][:, 4:8, :], bank[4][:, :].rearrange("p (k t) -> p k t", k=4)
                              ).then_inc(sg["v_rows"], 1)
                dve.wait_ge(sg["v_exp"], v + 1)
                base = 3 * NE + 3 * v
                link_loop(V.tensor_scalar(sig[0], sig[0], 1.0, None, ALU.add), base + 1)
                link_loop(V.reciprocal(sig[0], sig[0]), base + 2)
                link_loop(V.tensor_tensor(sig[0], sig[0], bank[0][:, :], ALU.mult), base + 3)
                V.tensor_tensor(acts[0], sig[0], bank[1][:, :], ALU.mult).then_inc(sg["v_act"], 1)
                dve.wait_ge(sg["v_down"], v + 1)
                V.tensor_copy(y_rows[0][:, 512:D], bank[6][:, :]).then_inc(sg["v_y"], 1)
            overflow(dve, more)
        elif kind == "final":
            i, = key
            r = ROWS[i]
            sg.wait(dve, f"gathered{i}", i)
            xi = x[0:r, i, :]
            link(V.scalar_tensor_tensor(xi, gathered[0:r, 2 * i, :], weight[0:r, i, 0:1], xi, ALU.mult, ALU.add))
            V.scalar_tensor_tensor(xi, gathered[0:r, 2 * i + 1, :], weight[0:r, i, 1:2], xi, ALU.mult, ALU.add
                                   ).then_inc(sg["combined"], 1)
            for j in ([i - 1] if i > 0 else []) + ([i] if i == TILES - 1 else []):
                if j not in POOL_FINAL:
                    finish_rows(dve, nc.vector, "final", j)

    def finish_rows(eng, ops, done, i):
        r = ROWS[i]
        eng.wait_ge(sg["gain_final"], 16)
        sg.wait(eng, "ssq_final", i)
        if i not in POOL_FINAL:
            ops.scalar_tensor_tensor(x[0:r, i, :], x[0:r, i, :], small[0:r, 16 + i:17 + i], gain[0:r, :],
                                     ALU.mult, ALU.mult).then_inc(sg[done], 1)
        else:
            ops.tensor_tensor(x[0:r, i, :], x[0:r, i, :], gain[0:r, :], ALU.mult).then_inc(sg[done], 1)

    def expert_pe(pe, kind, key):
        T = nc.tensor
        if kind == "idx":
            acquire(pe, "x", ("idx",))
            pe.wait_ge(sg["ids_in"], 16)
            T.transpose(bank[7][:, 0:NE], ids_row, ident[0:NE, 0:NE]).then_inc(sg["x_full"], 1)
        elif kind == "count":
            acquire(pe, "x", ("count",))
            for n, i in enumerate(tile_order):
                ins = T.matmul(bank[7][:, 0:NE], c["onesb"][0:ROWS[i], :], onehot[0:ROWS[i], i, :],
                               start=(n == 0), stop=(n == TILES - 1))
            ins.then_inc(sg["x_full"], 1)
        elif kind == "experts":
            def transpose_rows(b, sem, both):
                for half in range(2):
                    for k in range(4):
                        kk = 4 * half + k
                        ins = T.transpose(bank[3 + half][:, k * P:(k + 1) * P], rows_in[b][:, kk * P:(kk + 1) * P],
                                          ident)
                    if half or both:
                        ins.then_inc(sem, 1)

            def product(out_bank, lhs, rhs):
                n = len(lhs)
                for k in range(n):
                    ins = T.matmul(out_bank[:, :], lhs[k], rhs[k], start=(k == 0), stop=(k == n - 1))
                return ins

            def gate_or_up(b, which, sem):
                product(bank[which], [rowsT[b][:, k, :] for k in range(KD)],
                        [weights[b][which][:, k, :] for k in range(KD)]).then_inc(sem, 1)

            def transpose_acts(b, sem):
                for k in range(4):
                    ins = T.transpose(bank[5][:, k * P:(k + 1) * P], acts[b][:, k * P:(k + 1) * P], ident)
                ins.then_inc(sem, 1)

            def down(b, sem):
                for half, t in ((0, bank[2]), (1, bank[6])):
                    ins = product(t, [actsT[b][:, k, :] for k in range(4)],
                                  [weights[b][2][:, k, 512 * half:512 * half + 512] for k in range(4)])
                ins.then_inc(sem, 1)

            def rows_of(b, n):
                pe.wait_ge(sg[f"e_x{b}"], 16 * n + 16)
                transpose_rows(b, sg["e_rowsT_full"], True)

            def finish_down(j, b, n):
                pe.wait_ge(sg["e_actT"], j + 1)
                pe.wait_ge(sg[f"e_wd{b}"], 16 * n + 16)
                if not same(j, 0):
                    pe.wait_ge(sg["e_y_a"], j)
                    pe.wait_ge(sg["e_y_v"], j)
                down(b, sg["e_down"])

            def one(j, b, n):
                pe.wait_ge(sg["e_rows_a"], j + 1)
                pe.wait_ge(sg["e_rows_v"], j + 1)
                pe.wait_ge(sg[f"e_wgu{b}"], 32 * n + 32)
                if not same(j, 0):
                    pe.wait_ge(sg["e_gated"], 3 * j)
                gate_or_up(b, 0, sg["e_gate"])
                if not same(j, 0):
                    pe.wait_ge(sg["e_act"], j)
                    transpose_acts(1 - b, sg["e_actT_full"])
                gate_or_up(b, 1, sg["e_up"])
                if not same(j, LAST):
                    rows_of(1 - b, n if not b else n + 1)
                if not same(j, 0):
                    finish_down(j - 1, 1 - b, n if b else n - 1)

            acquire_all(pe)
            rows_of(0, 0)
            one(0, 0, 0)
            one(1, 1, 0)
            one(2, 0, 1)
            one(3, 1, 1)
            with pe.Fori(2, NE // 2 - 1) as it:
                one(2 * it, 0, it)
                one(2 * it + 1, 1, it)
            one(NE - 2, 0, NE // 2 - 1)
            one(LAST, 1, NE // 2 - 1)
            pe.wait_ge(sg["e_act"], NE)
            transpose_acts(1, sg["e_actT_full"])
            finish_down(LAST, 1, NE // 2 - 1)

            def more(v):
                pe.wait_ge(sg["v_x"], 16 * v + 16)
                transpose_rows(0, sg["v_rowsT_full"], False)
                pe.wait_ge(sg["v_rows"], 2 * v + 2)
                pe.wait_ge(sg["v_w"], 48 * v + 48)
                product(bank[0], [rowsT[0][:, k, :] for k in range(KD)], [weights[0][0][:, k, :] for k in range(KD)])
                gate_or_up(0, 1, sg["v_gu"])
                pe.wait_ge(sg["v_act"], v + 1)
                transpose_acts(0, sg["v_actT_full"])
                pe.wait_ge(sg["v_actT"], v + 1)
                down(0, sg["v_down"])
            pe.wait_ge(sg["e_y_a"], NE)
            pe.wait_ge(sg["e_y_v"], NE)
            overflow(pe, more)

    def acquire_all(pe):
        for ring in banks:
            for n in range(max(0, len(uses[ring]) - len(banks[ring])), len(uses[ring])):
                k, free = uses[ring][n]
                sg.wait(pe, ring + "_" + free, k)

    def transposes(key):
        b = at("t", key)
        kind = key[0]
        if kind == "hT":
            _, i, half = key
            r = ROWS[i]
            b4 = b[:, 0:4 * r].rearrange("p (k t) -> p k t", k=4)
            moves = [(b4[:, k, :], hn[0:r, i % 2, (4 * half + k) * P:(4 * half + k + 1) * P]) for k in range(4)]
            return moves, [(hT[:, 4 * half:4 * half + 4, i * P:i * P + r], b4, 1.0)]
        if kind == "pT":
            n = key[1]
            cc, i = proj[n]
            r, t0 = ROWS[i], i * P
            b4 = b[:, 0:4 * r].rearrange("p (k t) -> p k t", k=4)
            if cc in (SBQ, SBK):
                dst = qsbT if cc == SBQ else ksbT
                moves = [(b4[:, j, :], raw[0:r, rq[n] % 4, j * P:(j + 1) * P]) for j in range(4)]
                return moves, [(dst[:, :, t0:t0 + r], b4, 0.125 if cc == SBQ else 1.0)]
            if cc == NQ:
                src = rot[0:r, ri[n] % 2, :]
                return [(b4[:, j, :], src[:, j * P:(j + 1) * P]) for j in range(REP)], [(qnsaT[:, :, t0:t0 + r], b4, 0.125)]
            src, dst = (rot[0:r, ri[n] % 2, 256:384], kselT) if cc == KV4 else (rot[0:r, ri[n] % 2, 0:128], kwinT)
            return [(b[:, 0:r], src)], [(dst[:, t0:t0 + r], b[:, 0:r], 1.0)]
        return more_transposes(key, b)

    def wait_transposed(eng, key):
        sg.wait(eng, "t_" + freed_by("t", key), key)

    def heads(tile, n, r, cc):
        v = tile[0:r, n, :]
        if cc == NQ:
            return v.rearrange("p (g r d) -> p g r d" if tile is raw else "p (r g d) -> p g r d", g=GROUPS, r=REP)
        if cc == KV4:
            return v.rearrange("p (s x h d) -> p s x h d", s=2, x=2, h=GROUPS)[:, :, 0]
        return v[:, 0:P].rearrange("p (s h d) -> p s h d", s=1, h=GROUPS)

    def store(sp, cc, i):
        n, r = pn[cc, i], ROWS[i]
        side = "p" if i < QT else "s"

        def rows(name, width):
            o = out[f"{name}_{side}"]
            if i < QT:
                return o[0, 0, i * P:(i + 1) * P].rearrange("t h d -> t (h d)")
            if name[:3] == "win":
                return o[0, :, PAST - 1].rearrange("b h d -> b (h d)")
            return o[0, :, 0].rearrange("b h d -> b (h d)")

        if cc in (SBK, SBV, KV4, KV2):
            sg.wait(sp, "m_act", ("proj", n))
        if cc == SBK:
            sp.dma_start(rows("sb_k", 512), raw[0:r, rq[n] % 4, :]).then_inc(sg[f"st_raw{rq[n] % 4}"], 16)
        if cc == SBV:
            sp.dma_start(rows("sb_v", 512), vsb[0:r, i, :]).then_inc(sg["st_v"], 16)
        if cc in (KV4, KV2):
            sg.wait(sp, "rotated", n)
        if cc == KV4:
            for name, src, sem in (("cmp_k", rot[0:r, ri[n] % 2, 0:128], f"st_rot{ri[n] % 2}"),
                                   ("cmp_v", raw[0:r, rq[n] % 4, 128:256], f"st_raw{rq[n] % 4}"),
                                   ("sel_k", rot[0:r, ri[n] % 2, 256:384], f"st_rot{ri[n] % 2}"),
                                   ("sel_v", raw[0:r, rq[n] % 4, 384:512], f"st_raw{rq[n] % 4}")):
                sp.dma_start(rows(name, 128), src).then_inc(sg[sem], 16)
        if cc == KV2:
            sp.dma_start(rows("win_k", 128), rot[0:r, ri[n] % 2, 0:128]).then_inc(sg[f"st_rot{n % 2}"], 16)
            sp.dma_start(rows("win_v", 128), raw[0:r, rq[n] % 4, 128:256]).then_inc(sg[f"st_raw{rq[n] % 4}"], 16)

    block = ctx.enter_context(nc.Block())

    @block.sync
    def _(sp):
        for kind, key in PLAN:
            if kind == "load_w":
                pos, = key
                cc = ORDER[pos]
                if pos >= 2:
                    sg.wait(sp, "m_full", ("proj", (pos - 1) * TILES - 1))
                n = min(CHUNK, COLS - cc * CHUNK)
                sp.dma_start(win[:, pos % 2, :, 0:n], a["w_in"][0, :, cc * CHUNK:cc * CHUNK + n].rearrange(
                    "(k p) n -> p k n", p=P)).then_inc(sg[f"w{pos % 2}"], 16)
            elif kind == "load_x":
                for i in range(1) if key[0] == 0 else range(1, TILES):
                    src = a["x_prompt"][0, i * P:(i + 1) * P, :] if i < QT else a["x_sample"][:, 0, :]
                    sp.dma_start(x[0:ROWS[i], i, :], src).then_inc(sg[f"x{i}"], 16)
                    if i == 0:
                        sp.dma_start(cf[:, :], a["const_f"]).then_inc(sg["const"], 16)
                        sp.dma_start(gain[:, :], a["norm_attn"][0:1, :].partition_broadcast(P).rearrange(
                            "p o d -> p (o d)")).then_inc(sg["gain_attn"], 16)
            elif kind == "store":
                store(sp, *key)
            else:
                sync_more(sp, kind, key)
        for name, total in final_waits:
            sp.wait_ge(sg[name], total)

    @block.gpsimd
    def _(pool):
        gps_begin(pool)
        for kind, key in PLAN:
            if kind == "rope":
                n, = key
                cc, i = proj[n]
                r = ROWS[i]
                sg.wait(pool, "m_act", ("proj", n))
                if ri[n] >= 2:
                    sg.wait(pool, "rotated", ropes[ri[n] - 2])
                src, dst = heads(raw, rq[n] % 4, r, cc), heads(swp, ri[n] % 2, r, cc)
                s, h = src.shape[1:3]
                if n == 0:
                    pool.wait_ge(sg["const"], 16)
                for to, frm in ((0, 32), (32, 0)):
                    sin = rope[0:r, i, HD + to:HD + to + 32].unsqueeze(1).unsqueeze(1).to_broadcast([r, s, h, 32])
                    ins = nc.gpsimd.tensor_tensor(dst[:, :, :, to:to + 32], src[:, :, :, frm:frm + 32], sin, ALU.mult)
                if cc == KV4:
                    ins = nc.gpsimd.tensor_copy(vsel[0:r, i, :], raw[0:r, rq[n] % 4, 384:512])
                if cc == KV2:
                    nc.gpsimd.tensor_copy(vwin[0:r, i, :], raw[0:r, rq[n] % 4, 128:256])
                    ins = nc.gpsimd.tensor_copy(gates[0:r, i, :], raw[0:r, rq[n] % 4, 256:280])
                ins.then_inc(sg["swapped"], 1)
            else:
                gps_more(pool, kind, key)

    @block.scalar
    def _(act):
        chain = [0]

        def link(ins):
            chain[0] += 1
            ins.then_inc(sg["act_chain"], 1)
            act.wait_ge(sg["act_chain"], chain[0])

        def inverse_rms(dst, width, name, key):
            sg.wait(act, "ssq", key)
            rows = dst.shape[0]
            link(nc.scalar.activation(dst, dst, ACT.Ln, bias=c["eps"][0:rows], scale=1.0 / width))
            nc.scalar.activation(dst, dst, ACT.Exp, scale=-0.5).then_inc(sg[name], 1)

        def copy_out(key):
            _, moves = transposes(key)
            sg.wait(act, "t_full", key)
            before_copy(act, key)
            for dst, src, scale in moves:
                ins = nc.scalar.activation(dst, src, ACT.Copy, scale=scale)
            ins.then_inc(sg["t_act"], 1)

        act.preload_act_table_set("natural_log_exp_and_others")
        act.wait_ge(sg["const"], 16)
        for kind, key in PLAN:
            if kind == "norm":
                i, = key
                inverse_rms(small[0:ROWS[i], i:i + 1], D, "rstd", ("attn", i))
            elif kind == "T":
                if freed_by("t", key) == "act":
                    copy_out(key)
            elif kind == "proj":
                n, half = key
                if not half:
                    continue
                cc, i = proj[n]
                r, w = ROWS[i], min(CHUNK, COLS - cc * CHUNK)
                sg.wait(act, "m_full", ("proj", n))
                if cc == SBV:
                    if i == 0:
                        act.wait_ge(sg["y_zero"], 16 * EXTRA)
                    dst = vsb[0:r, i, :]
                else:
                    dst = raw[0:r, rq[n] % 4, 0:w]
                    if rq[n] >= 4:
                        before = raws[rq[n] - 4]
                        pc = proj[before][0]
                        if pc in (SBQ, SBK):
                            sg.wait(act, "t_full", ("pT", before))
                        if pc in (SBK, KV4, KV2):
                            sg.wait(act, f"st_raw{rq[n] % 4}", before)
                        if pc in (NQ, KV4, KV2):
                            sg.wait(act, "rotated", before)
                nc.scalar.copy(dst, at("m", ("proj", n))[0:r, 0:w]).then_inc(sg["m_act"], 1)
            else:
                act_more(act, link, inverse_rms, kind, key)

    @block.vector
    def _(dve):
        chain = [0]

        def link(ins):
            chain[0] += 1
            ins.then_inc(sg["dve_chain"], 1)
            dve.wait_ge(sg["dve_chain"], chain[0])

        dve_begin(dve, link)
        for kind, key in PLAN:
            if kind == "norm":
                i, = key
                r = ROWS[i]
                dve.wait_ge(sg[f"x{i}"], 16)
                if i >= 2:
                    sg.wait(dve, "t_full", ("hT", i - 2, 1))
                h = hn[0:r, i % 2, :]
                nc.vector.tensor_tensor_reduce(h, x[0:r, i, :], x[0:r, i, :], 1.0, 0.0, ALU.mult, ALU.add,
                                               small[0:r, i:i + 1]).then_inc(sg["ssq"], 1)
                if i == 0:
                    dve.wait_ge(sg["gain_attn"], 16)
                sg.wait(dve, "rstd", ("attn", i))
                sg.wait(dve, "ssq", ("attn", i))
                nc.vector.scalar_tensor_tensor(h, x[0:r, i, :], small[0:r, i:i + 1], gain[0:r, :],
                                               ALU.mult, ALU.mult).then_inc(sg["h"], 1)
            elif kind == "T":
                if freed_by("t", key) == "dve":
                    _, moves = transposes(key)
                    sg.wait(dve, "t_full", key)
                    before_copy(dve, key)
                    for dst, src, scale in moves:
                        if scale == 1.0:
                            ins = nc.vector.tensor_copy(dst, src)
                        else:
                            ins = nc.vector.tensor_scalar(dst, src, scale, None, ALU.mult)
                    ins.then_inc(sg["t_dve"], 1)
            elif kind == "rope":
                n, = key
                cc, i = proj[n]
                r = ROWS[i]
                sg.wait(dve, "m_act", ("proj", n))
                if ri[n] >= 2:
                    before = ropes[ri[n] - 2]
                    sg.wait(dve, "t_full", ("pT", before))
                    if proj[before][0] in (KV4, KV2):
                        sg.wait(dve, f"st_rot{ri[n] % 2}", before)
                src, dst, sw = heads(raw, rq[n] % 4, r, cc), heads(rot, ri[n] % 2, r, cc), heads(swp, ri[n] % 2, r, cc)
                s, h = src.shape[1:3]
                cos = rope[0:r, i, 0:HD].unsqueeze(1).unsqueeze(1).to_broadcast([r, s, h, HD])
                if n == 0:
                    dve.wait_ge(sg["const"], 16)
                link(nc.vector.tensor_tensor(dst, src, cos, ALU.mult))
                sg.wait(dve, "swapped", n)
                nc.vector.tensor_tensor(dst, dst, sw, ALU.add).then_inc(sg["rotated"], 1)
            else:
                dve_more(dve, link, kind, key)

    @block.tensor
    def _(pe):
        pe.wait_ge(sg["const"], 16)
        for kind, key in PLAN:
            if kind == "T":
                if key[0] == "hT":
                    sg.wait(pe, "h", key[1])
                elif key[0] == "pT":
                    sg.wait(pe, "rotated" if proj[key[1]][0] >= NQ else "m_act",
                            key[1] if proj[key[1]][0] >= NQ else ("proj", key[1]))
                else:
                    before_transpose(pe, key)
                acquire(pe, "t", key)
                moves, _ = transposes(key)
                for dst, src in moves:
                    ins = nc.tensor.transpose(dst, src, ident[0:src.shape[0], 0:src.shape[0]])
                ins.then_inc(sg["t_full"], 1)
            elif kind == "proj":
                n, half = key
                cc, i = proj[n]
                pos = n // TILES
                r, w = ROWS[i], min(CHUNK, COLS - cc * CHUNK)
                if not half:
                    if i == 0:
                        sg.wait(pe, f"w{pos % 2}", pos)
                    if pos == 0:
                        wait_transposed(pe, ("hT", i, 0))
                        wait_transposed(pe, ("hT", i, 1))
                    acquire(pe, "m", ("proj", n))
                for k in range(4 * half, 4 * half + 4):
                    ins = nc.tensor.matmul(at("m", ("proj", n))[0:r, 0:w], hT[:, k, i * P:i * P + r],
                                           win[:, pos % 2, k, 0:w], start=(k == 0), stop=(k == KD - 1))
                if half:
                    ins.then_inc(sg["m_full"], 1)
            else:
                pe_more(pe, kind, key)


OUTS = [("y_p", (1, SEQ, D)), ("y_s", (NB, 1, D)), ("sb_k_p", (1, 1, SEQ, HEADS, HD)), ("sb_v_p", (1, 1, SEQ, HEADS, HD)),
        ("cmp_k_p", (1, 1, SEQ, GROUPS, HD)), ("cmp_v_p", (1, 1, SEQ, GROUPS, HD)),
        ("sel_k_p", (1, 1, SEQ, GROUPS, HD)), ("sel_v_p", (1, 1, SEQ, GROUPS, HD)),
        ("win_k_p", (1, 1, SEQ, GROUPS, HD)), ("win_v_p", (1, 1, SEQ, GROUPS, HD)),
        ("sb_k_s", (1, NB, 1, HEADS, HD)), ("sb_v_s", (1, NB, 1, HEADS, HD)),
        ("cmp_k_s", (1, NB, 1, GROUPS, HD)), ("cmp_v_s", (1, NB, 1, GROUPS, HD)),
        ("sel_k_s", (1, NB, 1, GROUPS, HD)), ("sel_v_s", (1, NB, 1, GROUPS, HD)),
        ("win_k_s", (1, NB, PAST, GROUPS, HD)), ("win_v_s", (1, NB, PAST, GROUPS, HD))]


def kernel(**inputs):
    import concourse.bacc as bacc
    from concourse.bass_utils import run_bass_kernel_spmd

    nc = bacc.Bacc("TRN2", target_bir_lowering=False, num_devices=1)
    parts, bparts = host_constants()
    constants = {"const_f": np.concatenate(list(parts.values()), 1).astype(np.float32),
                 "const_b": np.concatenate(list(bparts.values()), 1).astype(mybir.dt.np(BF16))}
    arrays, a, out = {}, {}, {}
    for name, v in list(inputs.items()) + list(constants.items()):
        v = np.ascontiguousarray(v)
        arrays[name] = v
        a[name] = nc.dram_tensor(name, v.shape, mybir.dt.from_np(v.dtype), kind="ExternalInput").ap()
    for name, shape in OUTS:
        out[name] = nc.dram_tensor("out_" + name, shape, F32, kind="ExternalOutput").ap()
    build(nc, a, out)
    r = run_bass_kernel_spmd(nc, [arrays], core_ids=[0])
    return tuple(r.results[0]["out_" + name] for name, _ in OUTS)
```
